# Optimizing a Trainium2 kernel written in Bass

```python
import jax, jax.numpy as jnp
from jax import lax
import numpy as np

D_MODEL = 2048
BATCH = 1
SEQ = 256
DEPTH = 1

GLA_HEADS = 4
GLA_DK = (D_MODEL // 2) // GLA_HEADS
GLA_DV = D_MODEL // GLA_HEADS
GLA_GATE_RANK = 16
GLA_GATE_NORMALIZER = 16.0
GLA_CHUNK = 64
MLA_HEADS = 16
MLA_Q_RANK = D_MODEL // 4
MLA_KV_RANK = 512
MLA_NOPE = 128
MLA_ROPE = 64
MLA_V = 128
ROPE_THETA = 10000.0
Q_BLOCK = 128
FFN_HIDDEN = ((8 * D_MODEL // 3 + 255) // 256) * 256
NORM_EPS = 1e-6
N_MOD = 6

IN_WIDTHS = (GLA_HEADS * GLA_DK, GLA_HEADS * GLA_DK, GLA_HEADS * GLA_DV, GLA_HEADS * GLA_DV,
             GLA_GATE_RANK, MLA_Q_RANK, MLA_KV_RANK, MLA_ROPE, D_MODEL, D_MODEL)
IN_TOTAL = sum(IN_WIDTHS)


def rmsnorm(x, g):
    xf = x.astype(jnp.float32)
    y = xf * lax.rsqrt(jnp.mean(xf * xf, axis=-1, keepdims=True) + NORM_EPS)
    return (y * g.astype(jnp.float32)).astype(x.dtype)

def rope(t, cos, sin):
    t1, t2 = jnp.split(t, 2, axis=-1)
    return jnp.concatenate([t1 * cos - t2 * sin, t2 * cos + t1 * sin], axis=-1)

def gla_chunked(q, k, v, log_a):
    B, H, S, dk = q.shape
    dv = v.shape[-1]
    C = GLA_CHUNK
    N = S // C

    def to_chunks(t):
        return t.astype(jnp.float32).reshape(B, H, N, C, t.shape[-1]).transpose(2, 0, 1, 3, 4)

    qc, kc, vc = to_chunks(q), to_chunks(k), to_chunks(v)
    bc = jnp.cumsum(to_chunks(log_a), axis=3)
    causal = jnp.tril(jnp.ones((C, C), dtype=bool))

    def step(state, inp):
        q_i, k_i, v_i, b_i = inp
        o_inter = jnp.einsum('bhid,bhdv->bhiv', q_i * jnp.exp(b_i), state)
        diff = b_i[:, :, :, None, :] - b_i[:, :, None, :, :]
        w = jnp.exp(jnp.where(causal[:, :, None], diff, -jnp.inf))
        att = jnp.einsum('bhid,bhjd,bhijd->bhij', q_i, k_i, w)
        o_intra = jnp.einsum('bhij,bhjv->bhiv', att, v_i)
        b_last = b_i[:, :, -1, :]
        k_dec = k_i * jnp.exp(b_last[:, :, None, :] - b_i)
        state = jnp.exp(b_last)[..., None] * state + jnp.einsum('bhjd,bhjv->bhdv', k_dec, v_i)
        return state, o_inter + o_intra

    state0 = jnp.zeros((B, H, dk, dv), jnp.float32)
    _, o = lax.scan(step, state0, (qc, kc, vc, bc))
    return o.transpose(1, 2, 0, 3, 4).reshape(B, H, S, dv).astype(v.dtype)

def mla_attention(q_nope, q_rope, k_nope, k_rope, v):
    B, S, H, dn = q_nope.shape
    R = q_rope.shape[-1]
    dv = v.shape[-1]
    NB = S // Q_BLOCK
    scale = (dn + R) ** -0.5
    qn = q_nope.reshape(B, NB, Q_BLOCK, H, dn).transpose(1, 0, 3, 2, 4)
    qr = q_rope.reshape(B, NB, Q_BLOCK, H, R).transpose(1, 0, 3, 2, 4)
    kn = k_nope.transpose(0, 2, 1, 3)
    vv = v.transpose(0, 2, 1, 3)
    key_pos = jnp.arange(S)

    def block(args):
        qn_b, qr_b, i = args
        s = (jnp.einsum('bhqd,bhkd->bhqk', qn_b, kn)
             + jnp.einsum('bhqr,bkr->bhqk', qr_b, k_rope)).astype(jnp.float32) * scale
        q_pos = i * Q_BLOCK + jnp.arange(Q_BLOCK)
        mask = key_pos[None, :] <= q_pos[:, None]
        p = jax.nn.softmax(jnp.where(mask, s, -jnp.inf), axis=-1)
        return jnp.einsum('bhqk,bhkd->bhqd', p.astype(vv.dtype), vv)

    o = lax.map(block, (qn, qr, jnp.arange(NB)))
    return o.transpose(1, 0, 3, 2, 4).reshape(B, S, H, dv)

def token_mix(h, cos, sin, w_in, gla_gk_w, gla_gk_b, gla_onorm_g, gla_wo,
              mla_q_norm_g, mla_wuq, mla_kv_norm_g, mla_wukv, mla_wo, w_out):
    B, S, _ = h.shape
    idx = [sum(IN_WIDTHS[:i + 1]) for i in range(len(IN_WIDTHS) - 1)]
    (p_q, p_k, p_v, p_g, p_gk, p_cq, p_ckv, p_kr, p_ga, p_gb) = jnp.split(h @ w_in, idx, axis=-1)

    def heads(t, d):
        return t.reshape(B, S, GLA_HEADS, d).transpose(0, 2, 1, 3)
    q = heads(p_q, GLA_DK) * (GLA_DK ** -0.5)
    k = heads(p_k, GLA_DK)
    v = heads(p_v, GLA_DV)
    log_a = jax.nn.log_sigmoid((p_gk @ gla_gk_w + gla_gk_b).astype(jnp.float32)) / GLA_GATE_NORMALIZER
    o = gla_chunked(q, k, v, heads(log_a, GLA_DK)).transpose(0, 2, 1, 3)
    o = rmsnorm(o, gla_onorm_g) * jax.nn.silu(p_g.reshape(B, S, GLA_HEADS, GLA_DV))
    y_gla = o.reshape(B, S, GLA_HEADS * GLA_DV) @ gla_wo

    q_lat = (rmsnorm(p_cq, mla_q_norm_g) @ mla_wuq).reshape(B, S, MLA_HEADS, MLA_NOPE + MLA_ROPE)
    q_nope, q_rope = q_lat[..., :MLA_NOPE], q_lat[..., MLA_NOPE:]
    q_rope = rope(q_rope, cos[:, :, None, :], sin[:, :, None, :])
    kv = (rmsnorm(p_ckv, mla_kv_norm_g) @ mla_wukv).reshape(B, S, MLA_HEADS, MLA_NOPE + MLA_V)
    k_nope, v_m = kv[..., :MLA_NOPE], kv[..., MLA_NOPE:]
    k_rope = rope(p_kr, cos, sin)
    o_m = mla_attention(q_nope, q_rope, k_nope, k_rope, v_m)
    y_mla = o_m.reshape(B, S, MLA_HEADS * MLA_V) @ mla_wo

    merged = jax.nn.sigmoid(p_ga) * y_gla + jax.nn.sigmoid(p_gb) * y_mla
    return merged @ w_out

def swiglu(h, w_in, w_down):
    g, u = jnp.split(h @ w_in, 2, axis=-1)
    return (jax.nn.silu(g) * u) @ w_down

def first_inputs(seed: int = 0) -> dict:
    key = jax.random.key(seed)
    ks = jax.random.split(key, 24)
    L, D = DEPTH, D_MODEL

    def nrm(k, shape, scale):
        return jax.random.normal(k, shape, jnp.float32) * scale

    def gain(k, n):
        return 1.0 + 0.02 * jax.random.normal(k, (L, n), jnp.float32)

    x = jax.random.normal(ks[0], (BATCH, SEQ, D), jnp.float32)
    c = jax.random.normal(ks[1], (BATCH, D), jnp.float32)
    offsets = jax.random.randint(ks[2], (BATCH, 1), 0, 1024, dtype=jnp.int32)
    positions = offsets + jnp.arange(SEQ, dtype=jnp.int32)[None, :]
    return {
        "x": x,
        "c": c,
        "positions": positions,
        "ada_w": nrm(ks[3], (L, D, N_MOD * D), 0.5 * D ** -0.5),
        "ada_b": nrm(ks[4], (L, N_MOD * D), 0.02),
        "norm_mix_g": gain(ks[5], D),
        "w_in": nrm(ks[6], (L, D, IN_TOTAL), D ** -0.5),
        "gla_gk_w": nrm(ks[7], (L, GLA_GATE_RANK, GLA_HEADS * GLA_DK), GLA_GATE_RANK ** -0.5),
        "gla_gk_b": nrm(ks[8], (L, GLA_HEADS * GLA_DK), 0.5),
        "gla_onorm_g": gain(ks[9], GLA_DV),
        "gla_wo": nrm(ks[10], (L, GLA_HEADS * GLA_DV, D), (GLA_HEADS * GLA_DV) ** -0.5),
        "mla_q_norm_g": gain(ks[11], MLA_Q_RANK),
        "mla_wuq": nrm(ks[12], (L, MLA_Q_RANK, MLA_HEADS * (MLA_NOPE + MLA_ROPE)), MLA_Q_RANK ** -0.5),
        "mla_kv_norm_g": gain(ks[13], MLA_KV_RANK),
        "mla_wukv": nrm(ks[14], (L, MLA_KV_RANK, MLA_HEADS * (MLA_NOPE + MLA_V)), MLA_KV_RANK ** -0.5),
        "mla_wo": nrm(ks[15], (L, MLA_HEADS * MLA_V, D), (MLA_HEADS * MLA_V) ** -0.5),
        "w_out": nrm(ks[16], (L, D, D), D ** -0.5),
        "norm_ffn_g": gain(ks[17], D),
        "ffn_w_in": nrm(ks[18], (L, D, 2 * FFN_HIDDEN), D ** -0.5),
        "ffn_w_down": nrm(ks[19], (L, FFN_HIDDEN, D), FFN_HIDDEN ** -0.5),
        "final_norm_g": 1.0 + 0.02 * jax.random.normal(ks[20], (D,), jnp.float32),
    }

def first_block(x, c, positions, ada_w, ada_b, norm_mix_g, w_in, gla_gk_w, gla_gk_b, gla_onorm_g,
              gla_wo, mla_q_norm_g, mla_wuq, mla_kv_norm_g, mla_wukv, mla_wo, w_out,
              norm_ffn_g, ffn_w_in, ffn_w_down, final_norm_g):
    B, S, D = x.shape
    inv_freq = ROPE_THETA ** (-jnp.arange(0, MLA_ROPE, 2, dtype=jnp.float32) / MLA_ROPE)
    ang = positions.astype(jnp.float32)[..., None] * inv_freq
    cos = jnp.cos(ang).astype(x.dtype)
    sin = jnp.sin(ang).astype(x.dtype)
    c_act = jax.nn.silu(c)
    for l in range(DEPTH):
        mod = (c_act @ ada_w[l] + ada_b[l]).reshape(B, N_MOD, D)[:, :, None, :]
        shift_m, scale_m, gate_m, shift_f, scale_f, gate_f = [mod[:, i] for i in range(N_MOD)]
        h = rmsnorm(x, norm_mix_g[l]) * (1.0 + scale_m) + shift_m
        x = x + gate_m * token_mix(h, cos, sin, w_in[l], gla_gk_w[l], gla_gk_b[l], gla_onorm_g[l],
                                   gla_wo[l], mla_q_norm_g[l], mla_wuq[l], mla_kv_norm_g[l],
                                   mla_wukv[l], mla_wo[l], w_out[l])
        h = rmsnorm(x, norm_ffn_g[l]) * (1.0 + scale_f) + shift_f
        x = x + gate_f * swiglu(h, ffn_w_in[l], ffn_w_down[l])
    return rmsnorm(x, final_norm_g)


DEPTH_2 = 2

MEM_LEN = 256
HEAD_DIM = 128
MIX_W = D_MODEL
MEM_HEADS = 4
MEM_W = MEM_HEADS * HEAD_DIM
POOL_W = MIX_W - MEM_W
POOL_WINDOWS = (2, 4, 8, 16)
POOL_GROUPS = len(POOL_WINDOWS)
POOL_GC = POOL_W // POOL_GROUPS
NSA_W = MIX_W - MEM_W
NSA_HEADS = NSA_W // HEAD_DIM
NSA_KV_HEADS = 4
NSA_GROUP = NSA_HEADS // NSA_KV_HEADS
NSA_KV_W = NSA_KV_HEADS * HEAD_DIM
CMP_LEN = 32
CMP_STRIDE = 16
CMP_HID = 256
SEL_LEN = 64
SEL_TOPK = 16
WINDOW = 512
Q_CHUNK = 32
ROT_DIM = HEAD_DIM // 4
ROPE_THETA_2 = 500000.0
FORCE_SCORE = 1e4
NEG_INF = -1e30


def rmsnorm_2(x, g):
    xf = x.astype(jnp.float32)
    y = xf * lax.rsqrt(jnp.mean(xf * xf, axis=-1, keepdims=True) + NORM_EPS)
    return (y * g.astype(jnp.float32)).astype(x.dtype)

def rope_2(x, pos):
    half = ROT_DIM // 2
    inv = ROPE_THETA_2 ** (-jnp.arange(half, dtype=jnp.float32) * 2.0 / ROT_DIM)
    ang = pos.astype(jnp.float32)[..., None] * inv
    cos = jnp.cos(ang)[:, :, None, :]
    sin = jnp.sin(ang)[:, :, None, :]
    xr = x[..., :ROT_DIM].astype(jnp.float32)
    x1, x2 = xr[..., :half], xr[..., half:]
    rot = jnp.concatenate([x1 * cos - x2 * sin, x2 * cos + x1 * sin], axis=-1)
    return jnp.concatenate([rot.astype(x.dtype), x[..., ROT_DIM:]], axis=-1)

def masked_softmax(s, mask):
    s = jnp.where(mask, s.astype(jnp.float32), NEG_INF)
    p = jax.nn.softmax(s, axis=-1)
    return jnp.where(mask, p, 0.0)

def memory_attention(q, mem, mem_g, w_mem_kv):
    b, m, _ = mem.shape
    mn = rmsnorm_2(mem, mem_g)
    kv = (mn @ w_mem_kv).reshape(b, m, 2, MEM_HEADS, HEAD_DIM)
    k, v = kv[:, :, 0], kv[:, :, 1]
    s = jnp.einsum('bshd,bmhd->bhsm', q, k).astype(jnp.float32)
    p = jax.nn.softmax(s, axis=-1).astype(v.dtype)
    o = jnp.einsum('bhsm,bmhd->bshd', p, v)
    return o.reshape(q.shape[0], q.shape[1], MEM_W)

def multiscale_pool(u, w_pool, scale):
    b, s, _ = u.shape
    ug = u.reshape(b, s, POOL_GROUPS, POOL_GC)
    t1 = jnp.arange(1, s + 1, dtype=jnp.float32)[None, :, None]
    outs = []
    for gi, win in enumerate(POOL_WINDOWS):
        v = ug[:, :, gi].astype(jnp.float32)
        c = jnp.cumsum(v, axis=1)
        c_lag = jnp.pad(c, ((0, 0), (win, 0), (0, 0)))[:, :s]
        outs.append((c - c_lag) / jnp.minimum(t1, float(win)) - v)
    pooled = jnp.stack(outs, axis=2).astype(u.dtype)
    mixed = jnp.einsum('bsgc,gcd->bsgd', pooled, w_pool).reshape(b, s, POOL_W)
    return mixed * scale

def nsa_shared_kv(h, kv_norm_g, w_kv, cmp_pe, cmp_w1, cmp_w2, positions):
    b, s, _ = h.shape
    hn = rmsnorm_2(h, kv_norm_g)
    kv = (hn @ w_kv).reshape(b, s, 6, NSA_KV_HEADS, HEAD_DIM)
    k_c, v_c, k_s, v_s, k_w, v_w = [kv[:, :, i] for i in range(6)]
    k_s = rope_2(k_s, positions)
    k_w = rope_2(k_w, positions)
    n_cmp = (s - CMP_LEN) // CMP_STRIDE + 1
    blk = jnp.arange(n_cmp)[:, None] * CMP_STRIDE + jnp.arange(CMP_LEN)[None, :]

    def compress(z, pe, w1, w2):
        zb = z[:, blk] + pe[None, None, :, None, :]
        zb = zb.transpose(0, 1, 3, 2, 4).reshape(b, n_cmp, NSA_KV_HEADS, CMP_LEN * HEAD_DIM)
        return jax.nn.silu(zb @ w1) @ w2

    k_cmp = compress(k_c, cmp_pe[0], cmp_w1[0], cmp_w2[0])
    v_cmp = compress(v_c, cmp_pe[1], cmp_w1[1], cmp_w2[1])
    k_cmp = rope_2(k_cmp, positions[:, blk[:, -1]])
    n_sel = s // SEL_LEN
    k_blk = k_s.reshape(b, n_sel, SEL_LEN, NSA_KV_HEADS, HEAD_DIM).transpose(0, 3, 1, 2, 4)
    v_blk = v_s.reshape(b, n_sel, SEL_LEN, NSA_KV_HEADS, HEAD_DIM).transpose(0, 3, 1, 2, 4)
    pad = ((0, 0), (WINDOW, 0), (0, 0), (0, 0))
    return (k_cmp, v_cmp, k_blk, v_blk, jnp.pad(k_w, pad), jnp.pad(v_w, pad))

def nsa_attention(q, gates, k_cmp, v_cmp, k_blk, v_blk, k_win, v_win):
    b, s, _, _ = q.shape
    n_cmp = k_cmp.shape[1]
    n_sel = k_blk.shape[2]
    n_top = min(SEL_TOPK, n_sel)
    G, R, L = NSA_KV_HEADS, NSA_GROUP, SEL_LEN
    cmp_start = jnp.arange(n_cmp) * CMP_STRIDE
    cmp_end = cmp_start + CMP_LEN - 1
    sel_start = jnp.arange(n_sel) * SEL_LEN
    ov = (jnp.minimum(cmp_end[:, None], sel_start[None, :] + L - 1)
          - jnp.maximum(cmp_start[:, None], sel_start[None, :]) + 1)
    overlap = jnp.maximum(ov, 0).astype(jnp.float32) / CMP_LEN
    bi = jnp.arange(b)[:, None, None, None]
    gi = jnp.arange(G)[None, :, None, None]
    jsel = jnp.arange(n_sel)

    def chunk(c):
        t0 = c * Q_CHUNK
        t = t0 + jnp.arange(Q_CHUNK)
        qc = lax.dynamic_slice_in_dim(q, t0, Q_CHUNK, axis=1).reshape(b, Q_CHUNK, G, R, HEAD_DIM)
        gc = lax.dynamic_slice_in_dim(gates, t0, Q_CHUNK, axis=1).reshape(b, Q_CHUNK, G, R, 3)
        sc = jnp.einsum('bqgrd,bngd->bgrqn', qc, k_cmp)
        p_cmp = masked_softmax(sc, cmp_end[None, :] <= t[:, None])
        o_cmp = jnp.einsum('bgrqn,bngd->bqgrd', p_cmp.astype(v_cmp.dtype), v_cmp)
        imp = jnp.einsum('bgrqn,nj->bgqj', p_cmp, overlap)
        cur = t // L
        forced = (jsel[None, :] == 0) | (jsel[None, :] == cur[:, None]) | (jsel[None, :] == cur[:, None] - 1)
        ok = sel_start[None, :] <= t[:, None]
        score = jnp.where(ok, jnp.where(forced, FORCE_SCORE, imp), NEG_INF)
        _, idx = lax.top_k(score, n_top)
        k_sel = k_blk[bi, gi, idx].reshape(b, G, Q_CHUNK, n_top * L, HEAD_DIM)
        v_sel = v_blk[bi, gi, idx].reshape(b, G, Q_CHUNK, n_top * L, HEAD_DIM)
        key_pos = (idx[..., None] * L + jnp.arange(L)).reshape(b, G, 1, Q_CHUNK, n_top * L)
        ss = jnp.einsum('bqgrd,bgqmd->bgrqm', qc, k_sel)
        p_sel = masked_softmax(ss, key_pos <= t[None, None, None, :, None])
        o_sel = jnp.einsum('bgrqm,bgqmd->bqgrd', p_sel.astype(v_sel.dtype), v_sel)
        kw = lax.dynamic_slice_in_dim(k_win, t0, WINDOW + Q_CHUNK, axis=1)
        vw = lax.dynamic_slice_in_dim(v_win, t0, WINDOW + Q_CHUNK, axis=1)
        spos = t0 - WINDOW + jnp.arange(WINDOW + Q_CHUNK)
        dist = t[:, None] - spos[None, :]
        win_ok = (dist >= 0) & (dist < WINDOW) & (spos[None, :] >= 0)
        sw = jnp.einsum('bqgrd,bsgd->bgrqs', qc, kw)
        p_w = masked_softmax(sw, win_ok)
        o_win = jnp.einsum('bgrqs,bsgd->bqgrd', p_w.astype(vw.dtype), vw)
        return gc[..., 0:1] * o_cmp + gc[..., 1:2] * o_sel + gc[..., 2:3] * o_win

    out = lax.map(chunk, jnp.arange(s // Q_CHUNK))
    return jnp.moveaxis(out, 0, 1).reshape(b, s, NSA_W)

def pool_layer(x, mem, norm_g, w_in, w_pool, pool_scale, mem_g, w_mem_kv, w_out):
    b, s, _ = x.shape
    h = rmsnorm_2(x, norm_g)
    proj = h @ w_in
    u, zu, qm, zm = jnp.split(proj, [POOL_W, 2 * POOL_W, 2 * POOL_W + MEM_W], axis=-1)
    y_pool = multiscale_pool(u, w_pool, pool_scale) * jax.nn.silu(zu)
    qm = qm.reshape(b, s, MEM_HEADS, HEAD_DIM) * (HEAD_DIM ** -0.5)
    y_mem = memory_attention(qm, mem, mem_g, w_mem_kv) * jax.nn.silu(zm)
    return x + jnp.concatenate([y_pool, y_mem], axis=-1) @ w_out

def nsa_layer(x, mem, positions, norm_g, w_in, mem_g, w_mem_kv, w_out, shared):
    b, s, _ = x.shape
    h = rmsnorm_2(x, norm_g)
    proj = h @ w_in
    o1 = NSA_W
    o2 = o1 + 3 * NSA_HEADS
    o3 = o2 + NSA_W
    o4 = o3 + MEM_W
    q, gl, zq, qm, zm = jnp.split(proj, [o1, o2, o3, o4], axis=-1)
    q = rope_2(q.reshape(b, s, NSA_HEADS, HEAD_DIM), positions) * (HEAD_DIM ** -0.5)
    gates = jax.nn.sigmoid(gl.reshape(b, s, NSA_HEADS, 3))
    y_nsa = nsa_attention(q, gates, *shared) * jax.nn.silu(zq)
    qm = qm.reshape(b, s, MEM_HEADS, HEAD_DIM) * (HEAD_DIM ** -0.5)
    y_mem = memory_attention(qm, mem, mem_g, w_mem_kv) * jax.nn.silu(zm)
    return x + jnp.concatenate([y_nsa, y_mem], axis=-1) @ w_out

def second_inputs(seed: int = 0) -> dict:
    key = jax.random.key(seed)
    ks = jax.random.split(key, 20)
    n_a = DEPTH_2 // 2
    n_b = DEPTH_2 - n_a
    f32 = jnp.float32

    def w(k, shape, fan_in):
        return jax.random.normal(k, shape, f32) * (fan_in ** -0.5)

    def gain(k, shape):
        return 1.0 + 0.05 * jax.random.normal(k, shape, f32)

    x = jax.random.normal(ks[0], (BATCH, SEQ, D_MODEL), f32)
    mem = jax.random.normal(ks[1], (BATCH, MEM_LEN, D_MODEL), f32)
    offs = jax.random.randint(ks[2], (BATCH, 1), 0, 1024, dtype=jnp.int32)
    positions = (offs + jnp.arange(SEQ, dtype=jnp.int32)[None, :]).astype(jnp.int32)
    b_in_w = 2 * NSA_W + 3 * NSA_HEADS + 2 * MEM_W
    return {
        "x": x,
        "mem": mem,
        "positions": positions,
        "norm_g": gain(ks[3], (DEPTH_2, D_MODEL)),
        "mem_norm_g": gain(ks[4], (DEPTH_2, D_MODEL)),
        "w_mem_kv": w(ks[5], (DEPTH_2, D_MODEL, 2 * MEM_W), D_MODEL),
        "w_out": w(ks[6], (DEPTH_2, MIX_W, D_MODEL), MIX_W),
        "a_w_in": w(ks[7], (n_a, D_MODEL, 2 * POOL_W + 2 * MEM_W), D_MODEL),
        "a_w_pool": w(ks[8], (n_a, POOL_GROUPS, POOL_GC, POOL_GC), POOL_GC),
        "a_pool_scale": gain(ks[9], (n_a, POOL_W)),
        "b_w_in": w(ks[10], (n_b, D_MODEL, b_in_w), D_MODEL),
        "kv_norm_g": gain(ks[11], (D_MODEL,)),
        "w_kv": w(ks[12], (D_MODEL, 6 * NSA_KV_W), D_MODEL),
        "cmp_pe": 0.1 * jax.random.normal(ks[13], (2, CMP_LEN, HEAD_DIM), f32),
        "cmp_w1": w(ks[14], (2, CMP_LEN * HEAD_DIM, CMP_HID), CMP_LEN * HEAD_DIM),
        "cmp_w2": w(ks[15], (2, CMP_HID, HEAD_DIM), CMP_HID),
        "final_g": gain(ks[16], (D_MODEL,)),
    }

def second_block(x, mem, positions, norm_g, mem_norm_g, w_mem_kv, w_out, a_w_in, a_w_pool,
              a_pool_scale, b_w_in, kv_norm_g, w_kv, cmp_pe, cmp_w1, cmp_w2, final_g):
    n_a = DEPTH_2 // 2
    h = x
    shared = None
    for layer in range(DEPTH_2):
        if layer < n_a:
            h = pool_layer(h, mem, norm_g[layer], a_w_in[layer], a_w_pool[layer],
                           a_pool_scale[layer], mem_norm_g[layer], w_mem_kv[layer], w_out[layer])
        else:
            if layer == n_a:
                shared = nsa_shared_kv(h, kv_norm_g, w_kv, cmp_pe, cmp_w1, cmp_w2, positions)
            h = nsa_layer(h, mem, positions, norm_g[layer], b_w_in[layer - n_a],
                          mem_norm_g[layer], w_mem_kv[layer], w_out[layer], shared)
    return rmsnorm_2(h, final_g)


def setup_inputs(seed=0):
    out = dict(first_inputs(seed))
    for name, value in second_inputs(seed + 1).items():
        if name != "x":
            out[name + "_2"] = value
    return out


def reference(
    x, c, positions, ada_w, ada_b, norm_mix_g, w_in, gla_gk_w, gla_gk_b, gla_onorm_g, gla_wo,
    mla_q_norm_g, mla_wuq, mla_kv_norm_g, mla_wukv, mla_wo, w_out, norm_ffn_g, ffn_w_in,
    ffn_w_down, final_norm_g, mem_2, positions_2, norm_g_2, mem_norm_g_2, w_mem_kv_2, w_out_2,
    a_w_in_2, a_w_pool_2, a_pool_scale_2, b_w_in_2, kv_norm_g_2, w_kv_2, cmp_pe_2, cmp_w1_2,
    cmp_w2_2, final_g_2,
):
    x = first_block(
        x, c, positions, ada_w, ada_b, norm_mix_g, w_in, gla_gk_w, gla_gk_b, gla_onorm_g,
        gla_wo, mla_q_norm_g, mla_wuq, mla_kv_norm_g, mla_wukv, mla_wo, w_out, norm_ffn_g,
        ffn_w_in, ffn_w_down, final_norm_g,
    )
    return second_block(
        x, mem_2, positions_2, norm_g_2, mem_norm_g_2, w_mem_kv_2, w_out_2, a_w_in_2,
        a_w_pool_2, a_pool_scale_2, b_w_in_2, kv_norm_g_2, w_kv_2, cmp_pe_2, cmp_w1_2, cmp_w2_2,
        final_g_2,
    )


_drawn_inputs = setup_inputs


def setup_inputs(seed=0):
    import zlib

    import numpy as np

    out = dict(_drawn_inputs(seed))
    spreads = {}
    factors = {'norm_mix_g': 8.0,
     'gla_onorm_g': 8.0,
     'mla_q_norm_g': 8.0,
     'mla_kv_norm_g': 8.0,
     'norm_ffn_g': 8.0,
     'mem_norm_g_2': 8.0,
     'a_pool_scale_2': 2.737,
     'kv_norm_g_2': 8.0,
     'cmp_pe_2': 4.339}
    for name, (base, spread) in spreads.items():
        noise = np.random.default_rng([zlib.crc32(name.encode()), seed]).standard_normal(out[name].shape)
        drawn = base * np.exp(spread * noise) if base else spread * noise
        out[name] = __import__('jax').numpy.asarray(drawn.astype(out[name].dtype))
    for name, factor in factors.items():
        out[name] = (out[name] * factor).astype(out[name].dtype)
    return out
```

```python
import math
from contextlib import ExitStack

import numpy as np

import concourse.bass as bass
from concourse import mybir

F32 = mybir.dt.float32
F32R = mybir.dt.float32r
I32 = mybir.dt.int32
ALU = mybir.AluOpType
ACT = mybir.ActivationFunctionType
AX = mybir.AxisListType

P = 128
S = 256
TT = S // P
D = 2048
DC = D // P
NT = 512
BLK = NT // P
EPS = 1e-6

GLA_H, GLA_DK, GLA_DV, RANK = 4, 256, 512, 16
LEVELS = 7
MLA_H, NOPE, ROPE, QR, KVR = 16, 128, 64, 512, 512
HALF_H = MLA_H // 2
FFN = 5632
FFN_PARTS = (6, 5)
MEM_H, HD = 4, 128
POOL_W, POOL_G, POOL_GC = 1536, 4, 384
NSA_H, NSA_G = 12, 4
CMP_LEN, CMP_STRIDE, CMP_HID = 32, 16, 256
NCMP = (S - CMP_LEN) // CMP_STRIDE + 1
NEG = -1e30

W_Q, W_K, W_V, W_G = 0, 1024, 2048, 4096
W_GK = 6144
W_CQ = W_GK + RANK
W_CKV = W_CQ + QR
W_KR = W_CKV + KVR
W_GA = W_KR + ROPE
W_GB = W_GA + D
B_Q, B_GL = 0, NSA_H * HD
B_ZQ = B_GL + 3 * NSA_H
B_QM = B_ZQ + NSA_H * HD
B_ZM = B_QM + MEM_H * HD

CONST = {}
_at = 0
for _n, _w in (("ident", P), ("ones", P), ("rot_mla", P), ("rot_nsa", P), ("causal", 2 * P),
               ("cmp_add", 2 * NCMP), ("cmp_mul", 2 * NCMP), ("freq_mla", 1), ("freq_nsa", 1),
               ("pool_head", POOL_G * 16)):
    CONST[_n] = (_at, _w)
    _at += _w
CONST_W = _at
GLA_SLOTS = LEVELS + 1
GLA_CONST_W = 3 * GLA_SLOTS * P

VECTORS = {}
_at = 0
for _n, _w in (("norm_mix_g", DC), ("ada_b", 6 * DC), ("gla_onorm_g", GLA_DV // P), ("mla_q_norm_g", QR // P),
               ("mla_kv_norm_g", KVR // P), ("norm_ffn_g", DC), ("final_norm_g", DC), ("norm_g_2", 2 * DC),
               ("mem_norm_g_2", 2 * DC), ("a_pool_scale_2", POOL_W // P), ("kv_norm_g_2", DC),
               ("final_g_2", DC), ("c", DC), ("cmp_pe_2", 2 * CMP_LEN)):
    VECTORS[_n] = (_at, _w)
    _at += _w
VEC_W = _at


def constants():
    t = np.arange(P)
    c = np.zeros((P, CONST_W), np.float32)

    def put(name, a):
        at, w = CONST[name]
        c[:, at:at + w] = a

    put("ident", np.eye(P))
    put("ones", 1.0)
    rot = np.zeros((P, P))
    for m in range(P):
        rot[(m + 32, m) if m % 64 < 32 else (m - 32, m)] = -1.0 if m % 64 < 32 else 1.0
    put("rot_mla", rot)
    rot = np.zeros((P, P))
    for m in range(32):
        rot[(m + 16, m) if m < 16 else (m - 16, m)] = -1.0 if m < 16 else 1.0
    put("rot_nsa", rot)
    put("causal", np.concatenate([np.zeros((P, P)), np.where(t[None, :] <= t[:, None], 0.0, NEG)], 1))
    ends = np.arange(NCMP) * CMP_STRIDE + CMP_LEN - 1
    seen = np.concatenate([ends[None, :] <= (t[:, None] + tt * P) for tt in range(TT)], 1)
    put("cmp_add", np.where(seen, 0.0, NEG))
    put("cmp_mul", seen)
    put("freq_mla", (10000.0 ** (-(t % 32) * 2.0 / ROPE))[:, None])
    put("freq_nsa", np.where(t < 32, 500000.0 ** (-(t % 16) * 2.0 / 32), 0.0)[:, None])
    head = [2.0 ** (g + 1) / np.minimum(np.arange(16) + 1, 2.0 ** (g + 1)) for g in range(POOL_G)]
    put("pool_head", np.concatenate(head)[None, :])

    g = np.zeros((P, 3, GLA_SLOTS, P), np.float32)
    s, i = np.meshgrid(t, t, indexing="ij")
    for l in range(LEVELS):
        m = 2 ** l
        mid = i // (2 * m) * (2 * m) + m
        right = i % (2 * m) >= m
        g[:, 0, l] = g[:, 1, l] = np.where(right, (s >= mid) & (s <= i), (s > i) & (s < mid)) / 16.0
        g[:, 2, l] = (s // (2 * m) == i // (2 * m)) & (s % (2 * m) < m) & right
    g[:, 0, LEVELS] = (s > i) / 16.0
    g[:, 1, LEVELS] = (s <= i) / 16.0
    g[:, 2, LEVELS] = s == i
    return c, g.reshape(P, GLA_CONST_W)


class Product:

    def __init__(self, name, tiles, kp, kc=4, width=NT, split=True, mode="T", dmas=1):
        self.name, self.tiles, self.kp, self.kc, self.width = name, tiles, kp, kc, width
        self.split, self.mode, self.dmas = split, mode, dmas
        for b in (2, 4):
            if (b * kp) % 4 == 0 and tiles % b == 0:
                break
        self.body, self.turns = (b, tiles // b) if tiles % b == 0 and (b * kp) % 4 == 0 else (tiles, 1)


PRODUCTS = [Product("mem_k0", 1, 4), Product("mem_v0", 1, 4, mode="N"),
            Product("mem_k1", 1, 4), Product("mem_v1", 1, 4, mode="N"),
            Product("ada", 24, 4, split=False),
            Product("gla_q", 2, 4), Product("gla_k", 2, 4), Product("gla_v", 4, 4, mode="N"),
            Product("gla_gk", 1, 1, kc=16, width=RANK, split=False),
            Product("gla_g", 4, 4), Product("gate_a", 4, 4), Product("gla_wo", 4, 4),
            Product("mla_cq", 1, 4), Product("mla_ckv", 1, 4),
            Product("mla_kr", 1, 1, kc=16, width=P, split=False, dmas=2),
            Product("gate_b", 4, 4)]
for _h in range(2):
    PRODUCTS += [Product(f"mla_qn{_h}", 2, 1, dmas=4), Product(f"mla_qr{_h}", 1, 1, dmas=4),
                 Product(f"mla_k{_h}", 2, 1, dmas=4), Product(f"mla_v{_h}", 2, 1, mode="N", dmas=4)]
PRODUCTS += [Product("mla_wo", 4, 4), Product("w_out", 4, 4)]
for _h, _n in enumerate(FFN_PARTS):
    PRODUCTS += [Product(f"ffn_in{_h}", 2 * _n, 4), Product(f"ffn_down{_h}", 4, _n)]
PRODUCTS += [Product("pool_u", 3, 4), Product("pool_zu", 3, 4), Product("pool_qm", 1, 4), Product("pool_zm", 1, 4),
             Product("pool_w", 4, 1, kc=3, width=POOL_GC), Product("pool_out", 4, 4),
             Product("nsa_kc", 1, 4), Product("nsa_vc", 1, 4),
             Product("nsa_ks", 1, 4), Product("nsa_vs", 1, 4, mode="N"),
             Product("nsa_kw", 1, 4), Product("nsa_vw", 1, 4, mode="N"),
             Product("cmp_k1", 1, 4, kc=8, width=CMP_HID, split=False),
             Product("cmp_k2", 1, 1, kc=2, width=HD, split=False),
             Product("cmp_v1", 1, 4, kc=8, width=CMP_HID, split=False),
             Product("cmp_v2", 1, 1, kc=2, width=HD, split=False, mode="C"),
             Product("nsa_q", 3, 4), Product("nsa_gl", 1, 1, kc=16, width=3 * NSA_H, split=False, mode="N"),
             Product("nsa_zq", 3, 4), Product("nsa_qm", 1, 4), Product("nsa_zm", 1, 4),
             Product("nsa_out", 4, 4)]
G = {}
LANDED = []
_in_slot = [0] * 4
_p = _s = _t = 0
for _i, _g in enumerate(PRODUCTS):
    _g.p0, _g.s0, _g.t0 = _p, _s, _t
    for _ in range(_g.tiles * _g.kp):
        _in_slot[len(LANDED) % 4] += 16 * _g.dmas
        LANDED.append(_in_slot[len(LANDED) % 4])
    _p += _g.tiles * _g.kp
    _s += _g.tiles * _g.kp * _g.split
    _t += _g.tiles
    _g.p1, _g.t1 = _p, _t
    _next = PRODUCTS[_i + 1] if _i + 1 < len(PRODUCTS) else None
    _g.ahead = bool(_g.split and _next and _next.split and (_g.turns == 1 or _next.dmas == 1))
    _g.first_ahead = _i > 0 and PRODUCTS[_i - 1].ahead
    G[_g.name] = _g


class Norm:

    def __init__(self, name, n, split=True):
        self.name, self.n, self.split = name, n, split


NORMS = [Norm("mem0", DC), Norm("mem1", DC), Norm("mix", DC)]
NORMS += [Norm(f"gla{h}", GLA_DV // P, split=False) for h in range(GLA_H)]
NORMS += [Norm("cq", QR // P), Norm("ckv", KVR // P), Norm("ffn", DC), Norm("final1", DC, split=False),
          Norm("pool", DC), Norm("kv", DC), Norm("nsa", DC), Norm("final2", DC, split=False)]
N = {}
_a = _c = 0
for _i, _g in enumerate(NORMS):
    _g.k, _g.a0, _g.c0 = _i, _a, _c
    _a += _g.n // 2
    _c += _g.n * _g.split
    N[_g.name] = _g

ROPES = [("mla_kr", 1), ("mla_q0", BLK), ("mla_q1", BLK), ("nsa_ks", BLK), ("nsa_kw", BLK), ("cmp_k", 1), ("nsa_q", NSA_H)]
ROPE0 = {}
_a = 0
for _n, _w in ROPES:
    ROPE0[_n] = _a
    _a += _w


PLAIN_BEFORE = {}
_a = 0
for _g in NORMS:
    PLAIN_BEFORE[_g.name] = _a
    _a += 0 if _g.split else _g.n

STEPS = {"gla_g": 2, "mla_wo": 3, "w_out": 1, "ffn_in0": 2, "ffn_down0": 1, "ffn_in1": 2, "ffn_down1": 1, "pool_w": 3}
STEP0 = {}
_a = 0
for _g in PRODUCTS:
    if _g.name in STEPS:
        STEP0[_g.name] = _a
        _a += STEPS[_g.name] * (_g.tiles // 2 if _g.name.startswith("ffn_in") else _g.tiles)

N_VEC_DMA = sum((a + w - 1) // P - a // P + 1 for a, w in VECTORS.values())
TURNS_BEFORE_OUT = 4


class Steps:

    def __init__(self, eng, sem):
        self.eng, self.sem, self.n = eng, sem, 0

    def wait(self, ins):
        self.n += 1
        ins.then_inc(self.sem, 1)
        self.eng.wait_ge(self.sem, self.n)


def program(nc, A, out):
    with ExitStack() as ctx:
        def sem(name):
            return ctx.enter_context(nc.semaphore(name))

        base = (nc.sbuf_base + 63) // 64 * 64
        arena = ctx.enter_context(nc.sbuf_tensor("arena", [P, (nc.sbuf_usable_end - base - 64) // 4], F32))
        KB = 1024
        RAW, WHI, WLO, XB, HB, OB, BIG, SMALL = (k * KB for k in (0, 32, 48, 64, 80, 112, 144, 192))

        def at(name, off, shape, dt=F32):
            return nc.alloc_sbuf_tensor_at(name, shape, dt, offset=base + off)

        w_raw = [at(f"w_raw{i}", RAW + 8 * KB * i, [P, 2048]) for i in range(4)]
        w_hi = [at(f"w_hi{i}", WHI + 8 * KB * i, [P, 2048], F32R) for i in range(2)]
        w_lo = [at(f"w_lo{i}", WLO + 8 * KB * i, [P, 2048], F32R) for i in range(2)]
        x = at("x", XB, [P, DC, S])
        h_hi = at("h_hi", HB, [P, DC, S], F32R)
        h_lo = at("h_lo", HB + 16 * KB, [P, DC, S], F32R)
        o_hi = at("o_hi", OB, [P, DC, S], F32R)
        o_lo = at("o_lo", OB + 16 * KB, [P, DC, S], F32R)
        x_rows = at("x_rows", OB, [P, TT, D])
        mem_rows = at("mem_rows", OB + 16 * KB, [P, TT, D])
        mem_t = at("mem_t", BIG, [P, DC, S])
        mem_k_out = at("mem_k_out", BIG + 16 * KB, [P, 2, BLK, S])
        mem_v_out = at("mem_v_out", BIG + 24 * KB, [P, 2, TT, NT])
        vec_rows = at("vec_rows", BIG + 32 * KB, [P, 3, P])
        nscratch_b = at("nscratch_b", BIG + 40 * KB, [P, 2, 2 * S])
        ntmp_b = at("ntmp_b", BIG + 44 * KB, [P, 2, S])
        qk = at("qk", BIG, [P, GLA_H, 4, S])
        gla_v = at("gla_v", BIG + 16 * KB, [P, TT, D])
        log_a = at("log_a", BIG + 32 * KB, [P, TT, GLA_H * GLA_DK])
        gla_const = at("gla_const", OB, [P, 3, GLA_SLOTS, P])
        q_lev = at("q_lev", OB + 12 * KB, [P, 2, GLA_SLOTS, P])
        k_lev = at("k_lev", OB + 20 * KB, [P, 2, GLA_SLOTS, P])
        gk_w = at("gk_w", OB + 12 * KB, [RANK, GLA_H * GLA_DK])
        gk_b = at("gk_b", OB + 20 * KB, [1, GLA_H * GLA_DK])
        decay = [at("decay0", OB + 28 * KB, [P, GLA_SLOTS, P]), at("decay1", BIG + 40 * KB, [P, GLA_SLOTS, P])]
        gla_att = at("gla_att", BIG + 44 * KB, [P, 3, P])
        k_across = at("k_across", BIG + 44 * KB + 1536, [P, 2, P])
        gk_t = at("gk_t", BIG + 46 * KB + 512, [P, S])
        gla_sq = at("gla_sq", OB + 12 * KB, [P, 2, 2 * S])
        gla_tmp = at("gla_tmp", BIG + 40 * KB, [P, 2, BLK * S])
        merged = at("merged", BIG + 16 * KB, [P, DC, S])
        gate_b = at("gate_b", BIG, [P, DC, S])
        cq = at("cq", OB, [P, BLK, S])
        ckv = at("ckv", OB + 4 * KB, [P, BLK, S])
        cq_hi = at("cq_hi", BIG + 32 * KB, [P, BLK, S], F32R)
        cq_lo = at("cq_lo", BIG + 36 * KB, [P, BLK, S], F32R)
        ckv_hi = at("ckv_hi", BIG + 40 * KB, [P, BLK, S], F32R)
        ckv_lo = at("ckv_lo", BIG + 44 * KB, [P, BLK, S], F32R)
        mla_q = at("mla_q", HB, [P, HALF_H, S])
        mla_k = at("mla_k", HB + 8 * KB, [P, HALF_H, S])
        mla_qr = at("mla_qr", HB + 16 * KB, [P, BLK, S])
        mla_v = at("mla_v", HB + 20 * KB, [P, TT, HALF_H * P])
        mla_tmp = at("mla_tmp", BIG + 32 * KB, [P, BLK * S])
        nscratch_o = at("nscratch_o", OB + 8 * KB, [P, 2, 2 * S])
        ntmp_o = at("ntmp_o", OB + 12 * KB, [P, 2, S])
        o_tmp = at("o_tmp", OB, [P, 2, BLK * S])
        h_tmp = at("h_tmp", HB, [P, BLK * S])
        sw_hi = at("sw_hi", BIG, [P, 24, S], F32R)
        sw_lo = at("sw_lo", BIG + 24 * KB, [P, 24, S], F32R)
        u_t = at("u_t", BIG, [P, 12, S])
        pool_hi = at("pool_hi", BIG + 12 * KB, [P, 12, S], F32R)
        pool_lo = at("pool_lo", BIG + 24 * KB, [P, 12, S], F32R)
        silu_z = at("silu_z", BIG + 36 * KB, [P, 12, S])
        run_a = at("run_a", OB, [P, 12, S])
        run_b = at("run_b", OB + 12 * KB, [P, 12, S])
        mem_q = at("mem_q", BIG, [P, MEM_H, S])
        mem_z = at("mem_z", BIG + 4 * KB, [P, MEM_H, S])
        pool_tmp = at("pool_tmp", BIG + 8 * KB, [P, 3 * S])
        mem_k = at("mem_k", HB + 8 * KB, [P, MEM_H, S])
        mem_v = at("mem_v", HB + 12 * KB, [P, TT, NT])
        kc = at("kc", BIG, [P, NSA_G, S])
        vc = at("vc", BIG + 4 * KB, [P, NSA_G, S])
        ks = at("ks", BIG + 8 * KB, [P, NSA_G, S])
        vs = at("vs", BIG + 12 * KB, [P, TT, NT])
        kw = at("kw", BIG + 16 * KB, [P, NSA_G, S])
        vw = at("vw", BIG + 20 * KB, [P, TT, NT])
        nsa_q = at("nsa_q", BIG + 24 * KB, [P, NSA_H, S])
        z_pe = at("z_pe", OB, [P, CMP_LEN, NSA_G * NCMP])
        hidden = at("hidden", OB + 8 * KB, [P, 2, NSA_G * NCMP])
        k_cmp = at("k_cmp", OB + 16 * KB + 13 * KB, [P, NSA_G * NCMP])
        v_cmp = at("v_cmp", OB + 16 * KB + 14 * KB, [NCMP, NSA_G * HD])
        out_rows = at("out_rows", BIG, [P, TT, D])
        small = [SMALL]

        def keep(name, shape, dt=F32):
            off = small[0]
            small[0] += (4 * int(np.prod(shape[1:])) + 31) // 32 * 32
            assert base + small[0] <= nc.sbuf_usable_end, small[0]
            return at(name, off, shape, dt)

        const = keep("const", [P, CONST_W])
        cols = keep("cols", [P, VEC_W])
        mod = keep("mod", [P, 6 * DC])
        gain_eff = keep("gain_eff", [P, 2, DC])
        c_act = keep("c_act", [P, DC])
        rope_cos = keep("rope_cos", [P, S])
        rope_sin = keep("rope_sin", [P, S])
        rstd = keep("rstd", [P, S])
        var = keep("var", [P, S])
        probs = keep("probs", [P, 3, S])
        probs_t = keep("probs_t", [P, 2, TT, P])
        stats = keep("stats", [P, 16])
        gates = keep("gates", [P, TT, 3 * NSA_H])
        k_rope = keep("k_rope", [P, S])
        assert small[0] <= (nc.sbuf_usable_end - base), small

        tile_ps = [ctx.enter_context(nc.psum_tensor(f"tile_ps{i}", [P, 1024], F32)) for i in range(2)]
        misc_ps = [ctx.enter_context(nc.psum_tensor(f"misc_ps{i}", [P, 1024], F32)) for i in range(2)]
        bank = [misc_ps[i // 2][:, (i % 2) * 512:(i % 2 + 1) * 512] for i in range(4)]

        def cst(name):
            a, w = CONST[name]
            return const[:, a:a + w]

        def vec(name, i=0, n=1):
            a, _ = VECTORS[name]
            return cols[:, a + i:a + i + n]

        ident, ones = cst("ident"), cst("ones")
        half_pi = stats[:, 15:16]
        h_hi32, h_lo32 = h_hi[:].bitcast(F32), h_lo[:].bitcast(F32)

        b_scr, o_scr = (nscratch_b, ntmp_b), (nscratch_o, ntmp_o)
        H_OUT = (h_hi, h_lo)
        SCRATCH, SOURCE, DEST, GAIN = {}, {}, {}, {}
        SHIFT = {"mix": mod[:, 0:DC], "ffn": mod[:, 3 * DC:4 * DC]}
        for name_, scr, src_, dst_, gain_ in (
                ("mem0", b_scr, mem_t[:], H_OUT, vec("mem_norm_g_2", 0, DC)),
                ("mem1", b_scr, mem_t[:], H_OUT, vec("mem_norm_g_2", DC, DC)),
                ("mix", o_scr, x[:], H_OUT, gain_eff[:, 0, :]),
                *((f"gla{h}", (gla_sq, None), qk[:, h], (qk[:, h],), vec("gla_onorm_g", 0, 4)) for h in range(GLA_H)),
                ("cq", o_scr, cq[:], (cq_hi, cq_lo), vec("mla_q_norm_g", 0, 4)),
                ("ckv", o_scr, ckv[:], (ckv_hi, ckv_lo), vec("mla_kv_norm_g", 0, 4)),
                ("ffn", o_scr, x[:], H_OUT, gain_eff[:, 1, :]),
                ("final1", o_scr, x[:], (x,), vec("final_norm_g", 0, DC)),
                ("pool", o_scr, x[:], H_OUT, vec("norm_g_2", 0, DC)),
                ("kv", o_scr, x[:], H_OUT, vec("kv_norm_g_2", 0, DC)),
                ("nsa", o_scr, x[:], H_OUT, vec("norm_g_2", DC, DC)),
                ("final2", o_scr, x[:], (x,), vec("final_g_2", 0, DC))):
            SCRATCH[name_], DEST[name_], GAIN[name_] = scr, dst_, gain_
            SOURCE[name_] = lambda c, t=src_: t[:, c, :]
        mem_store = [nc.dram_tensor(f"mem_store{i}", (P, 2, 1024), F32, kind="Internal").ap() for i in range(2)]

        landed = [sem(f"landed{i}") for i in range(4)]
        cut_hi = sem("cut_hi")
        cut_lo = sem("cut_lo")
        piece_done = sem("piece_done")
        taken = [sem(f"taken{i}") for i in range(2)]
        silu_ready = sem("silu_ready")
        tile_step = sem("tile_step")
        act_step, dve_step = sem("act_step"), sem("dve_step")
        ld_const, ld_vec, ld_x, ld_mem = sem("ld_const"), sem("ld_vec"), sem("ld_x"), sem("ld_mem")
        ld_pos, ld_gla, ld_gk = sem("ld_pos"), sem("ld_gla"), sem("ld_gk")
        ld_mkv, st_mkv, st_out = sem("ld_mkv"), sem("st_mkv"), sem("st_out")
        vec_turned, vec_ready, c_ready = sem("vec_turned"), sem("vec_ready"), sem("c_ready")
        turned = sem("turned")
        turn_out = [sem(f"turn_out{i}") for i in range(2)]
        nm_sq, nm_acc, nm_var, nm_std = sem("nm_sq"), sem("nm_acc"), sem("nm_var"), sem("nm_std")
        nm_t, nm_hi, nm_lo, nm_plain = sem("nm_t"), sem("nm_hi"), sem("nm_lo"), sem("nm_plain")
        tab_arg, tab_ready = sem("tab_arg"), sem("tab_ready")
        rp_rot, rp_done = sem("rp_rot"), sem("rp_done")
        z_ready, z_abs, la_ready = sem("z_ready"), sem("z_abs"), sem("la_ready")
        gl_e, gl_ex, gl_qk, gl_att = sem("gl_e"), sem("gl_ex"), sem("gl_qk"), sem("gl_att")
        gl_red, gl_o, gl_out = sem("gl_red"), sem("gl_o"), sem("gl_out")
        at_s, at_masked, at_max, at_exp = sem("at_s"), sem("at_masked"), sem("at_max"), sem("at_exp")
        at_p, at_t, at_pt, at_o, at_fin = (sem(f"at_{n}") for n in ("p", "t", "pt", "o", "fin"))
        pl_t, pl_hi, pl_lo = sem("pl_t"), sem("pl_hi"), sem("pl_lo")
        zp_ready = sem("zp_ready")

        def rows(w, chunks=None):
            return w.rearrange("(c p) n -> p c n", p=P)

        w_in = rows(A["w_in"][0])
        ada_w, w_out = rows(A["ada_w"][0]), rows(A["w_out"][0])
        gla_wo, mla_wo = rows(A["gla_wo"][0]), rows(A["mla_wo"][0])
        wuq = A["mla_wuq"][0].rearrange("(c p) (h e) -> p c h e", p=P, e=NOPE + ROPE)
        wukv = A["mla_wukv"][0].rearrange("(c p) (h e) -> p c h e", p=P, e=2 * P)
        ffn_in, ffn_down = rows(A["ffn_w_in"][0]), rows(A["ffn_w_down"][0])
        mem_kv = [rows(A["w_mem_kv_2"][i]) for i in range(2)]
        out_2 = [rows(A["w_out_2"][i]) for i in range(2)]
        a_in, b_in, w_kv = rows(A["a_w_in_2"][0]), rows(A["b_w_in_2"][0]), rows(A["w_kv_2"])

        def plain(w, col):
            return lambda i, tb, g, q: (w[:, g.kc * q:g.kc * (q + 1), bass.ds(i * (g.body * NT) + col + tb * NT, NT)]
                                        if g.turns > 1 else w[:, g.kc * q:g.kc * (q + 1), col + tb * NT:col + tb * NT + NT])

        def ffn_cols(part):
            first = sum(FFN_PARTS[:part]) * NT
            return lambda i, tb, g, q: ffn_in[:, 4 * q:4 * q + 4,
                                              bass.ds(i * (g.body // 2 * NT) + first + tb // 2 * NT + tb % 2 * FFN, NT)]

        def ffn_rows(part):
            c0 = sum(FFN_PARTS[:part]) * BLK

            def src(i, tb, g, q):
                cs = slice(c0 + 4 * q, c0 + 4 * q + 4)
                if g.turns > 1:
                    return ffn_down[:, cs, bass.ds(i * (g.body * NT) + tb * NT, NT)]
                return ffn_down[:, cs, tb * NT:tb * NT + NT]
            return src

        SRC = {"mem_k0": plain(mem_kv[0], 0), "mem_v0": plain(mem_kv[0], NT),
               "mem_k1": plain(mem_kv[1], 0), "mem_v1": plain(mem_kv[1], NT),
               "ada": plain(ada_w, 0), "gla_q": plain(w_in, W_Q), "gla_k": plain(w_in, W_K),
               "gla_v": plain(w_in, W_V), "gla_g": plain(w_in, W_G), "gate_a": plain(w_in, W_GA),
               "gla_gk": lambda i, tb, g, q: w_in[:, :, W_GK:W_GK + RANK],
               "gla_wo": plain(gla_wo, 0), "mla_cq": plain(w_in, W_CQ), "mla_ckv": plain(w_in, W_CKV),
               "mla_kr": lambda i, tb, g, q: w_in[:, :, W_KR:W_KR + ROPE],
               "gate_b": plain(w_in, W_GB), "mla_wo": plain(mla_wo, 0), "w_out": plain(w_out, 0),
               "pool_u": plain(a_in, 0), "pool_zu": plain(a_in, POOL_W), "pool_qm": plain(a_in, 2 * POOL_W),
               "pool_zm": plain(a_in, 2 * POOL_W + MEM_H * HD),
               "pool_w": lambda i, tb, g, q: rows(A["a_w_pool_2"][0, tb]),
               "pool_out": plain(out_2[0], 0), "nsa_out": plain(out_2[1], 0),
               "cmp_k1": lambda i, tb, g, q: rows(A["cmp_w1_2"][0])[:, 8 * q:8 * q + 8],
               "cmp_v1": lambda i, tb, g, q: rows(A["cmp_w1_2"][1])[:, 8 * q:8 * q + 8],
               "cmp_k2": lambda i, tb, g, q: rows(A["cmp_w2_2"][0]),
               "cmp_v2": lambda i, tb, g, q: rows(A["cmp_w2_2"][1]),
               "nsa_q": plain(b_in, B_Q), "nsa_zq": plain(b_in, B_ZQ), "nsa_qm": plain(b_in, B_QM),
               "nsa_zm": plain(b_in, B_ZM), "nsa_gl": lambda i, tb, g, q: b_in[:, :, B_GL:B_GL + 3 * NSA_H]}
        for n_, name in enumerate(("nsa_kc", "nsa_vc", "nsa_ks", "nsa_vs", "nsa_kw", "nsa_vw")):
            SRC[name] = plain(w_kv, n_ * NT)
        for hf in range(2):
            h0 = hf * HALF_H
            SRC[f"mla_qn{hf}"] = lambda i, tb, g, q, h0=h0: wuq[:, :, h0 + 4 * tb:h0 + 4 * tb + 4, 0:NOPE]
            SRC[f"mla_qr{hf}"] = lambda i, tb, g, q, h0=h0: wuq[:, :, h0:h0 + 8, NOPE:NOPE + ROPE]
            SRC[f"mla_k{hf}"] = lambda i, tb, g, q, h0=h0: wukv[:, :, h0 + 4 * tb:h0 + 4 * tb + 4, 0:P]
            SRC[f"mla_v{hf}"] = lambda i, tb, g, q, h0=h0: wukv[:, :, h0 + 4 * tb:h0 + 4 * tb + 4, P:2 * P]
            SRC[f"ffn_in{hf}"] = ffn_cols(hf)
            SRC[f"ffn_down{hf}"] = ffn_rows(hf)

        def turns(eng, g, peel_last=False):
            if g.turns == 1:
                yield 0, True
                return
            n = g.turns - 1 if peel_last else g.turns
            with eng.Fori(0, n) as i:
                yield i, not peel_last
            if peel_last:
                yield g.turns - 1, True

        def per(i, n):
            return 0 if isinstance(i, int) and i == 0 else i * n

        def all_taken(eng, g):
            for b in range(2):
                n = (g.t1 - b + 1) // 2
                if n:
                    eng.wait_ge(taken[b], n)

        def tile_is_done(eng, g, i, tb):
            eng.wait_ge(piece_done, g.p0 + (tb + 1) * g.kp + per(i, g.body * g.kp))

        def last_taken(eng, g, i, tb):
            t = g.t0 + tb - 1
            eng.wait_ge(taken[t % 2], t // 2 + 1 + per(i, g.body // 2))

        def psum_tile(g, tb):
            return tile_ps[(g.t0 + tb) % 2], taken[(g.t0 + tb) % 2]

        def mla_units(hf):
            units = []
            for h in range(HALF_H):
                r = slice(64 * (h % 2), 64 * (h % 2) + 64)
                for tt in range(TT):
                    q = slice(tt * P, tt * P + P)
                    nk = (tt + 1) * P
                    units.append(dict(
                        scores=[(mla_q[:, h, q], mla_k[:, h, 0:nk]), (mla_qr[r, h // 2, q], k_rope[r, 0:nk])],
                        nk=nk, scale=(NOPE + ROPE) ** -0.5, add=cst("causal")[:, 2 * P - nk:2 * P], gate=None,
                        mul=None, v=[mla_v[:, j, h * P:(h + 1) * P] for j in range(tt + 1)], first=True, last=True,
                        chunk=hf * HALF_H + h, q=q, z=None))
            return units

        def mem_units():
            return [dict(scores=[(mem_q[:, h, tt * P:tt * P + P], mem_k[:, h, :])], nk=S, scale=HD ** -0.5, add=None,
                         gate=None, mul=None, v=[mem_v[:, j, h * P:(h + 1) * P] for j in range(TT)], first=True,
                         last=True, chunk=12 + h, q=slice(tt * P, tt * P + P), z=mem_z[:, h, tt * P:tt * P + P])
                    for h in range(MEM_H) for tt in range(TT)]

        def nsa_units():
            units = []
            for h in range(NSA_H):
                g = h // (NSA_H // NSA_G)
                gv = slice(g * HD, (g + 1) * HD)
                for tt in range(TT):
                    q = slice(tt * P, tt * P + P)
                    nk = (tt + 1) * P
                    common = dict(scale=HD ** -0.5, chunk=h, q=q, z=silu_z[:, h, q])
                    units.append(dict(common, scores=[(nsa_q[:, h, q], k_cmp[:, g * NCMP:(g + 1) * NCMP])], nk=NCMP,
                                      add=cst("cmp_add")[:, tt * NCMP:(tt + 1) * NCMP],
                                      mul=cst("cmp_mul")[:, tt * NCMP:(tt + 1) * NCMP],
                                      gate=gates[:, tt, 3 * h:3 * h + 1], v=[v_cmp[:, gv]], first=True, last=False))
                    for b, (k, v) in enumerate(((ks, vs), (kw, vw))):
                        units.append(dict(common, scores=[(nsa_q[:, h, q], k[:, g, 0:nk])], nk=nk,
                                          add=cst("causal")[:, 2 * P - nk:2 * P], mul=None,
                                          gate=gates[:, tt, 3 * h + 1 + b:3 * h + 2 + b],
                                          v=[v[:, j, gv] for j in range(tt + 1)], first=False, last=b == 1))
            return units

        UNITS = {"mla0": mla_units(0), "mla1": mla_units(1), "mem_a": mem_units(), "nsa": nsa_units(),
                 "mem_b": mem_units()}
        U0, FIN0 = {}, {}
        n_u = n_f = 0
        for name, us in UNITS.items():
            U0[name], FIN0[name] = n_u, n_f
            n_u += len(us)
            n_f += sum(u["last"] for u in us)
            UNITS[name] = us

        block = ctx.enter_context(nc.Block())

        @block.sync
        def _(sp):
            x_in, mem_in = A["x"][0], A["mem_2"][0]
            sp.dma_start(const[:], A["const"]).then_inc(ld_const, 16)
            n_vec = 0
            for name, (at0, w) in VECTORS.items():
                v = A[name]
                v = v.rearrange(" ".join(f"a{k}" for k in range(len(v.shape))) + " -> (" +
                                " ".join(f"a{k}" for k in range(len(v.shape))) + ")") if len(v.shape) > 1 else v
                v = v.rearrange("(r p) -> r p", p=P)
                done = 0
                while done < w:
                    r, t = (at0 + done) % P, (at0 + done) // P
                    n = min(P - r, w - done)
                    sp.dma_start(vec_rows[r:r + n, t, :], v[done:done + n]).then_inc(ld_vec, 16)
                    n_vec += 1
                    done += n
            assert n_vec == N_VEC_DMA
            sp.dma_start(mem_rows[:], mem_in.rearrange("(t p) d -> p t d", p=P)).then_inc(ld_mem, 16)
            sp.dma_start(x_rows[:], x_in.rearrange("(t p) d -> p t d", p=P)).then_inc(ld_x, 16)

            def load(name):
                g = G[name]
                for i, _ in turns(sp, g):
                    for tb in range(g.body):
                        for q in range(g.kp):
                            p = g.p0 + tb * g.kp + q
                            if p >= 4:
                                sp.wait_ge(piece_done, p - 3 + per(i, g.body * g.kp))
                            src = SRC[name](i, tb, g, q)
                            dst = w_raw[p % 4][:, 0:g.kc * g.width].rearrange("p (c n) -> p c n", c=g.kc)
                            parts = [(dst, src)]
                            if len(src.shape) == 4:
                                dst = dst.rearrange("p c (h e) -> p c h e", h=src.shape[2])
                                parts = [(dst[:, c], src[:, c]) for c in range(g.kc)]
                            elif name == "mla_kr":
                                parts = [(dst[:, :, k * ROPE:(k + 1) * ROPE], src) for k in range(2)]
                            assert len(parts) == g.dmas
                            for d_, s_ in parts:
                                sp.dma_start(d_, s_).then_inc(landed[p % 4], 16)

            def mem_kv_load(i, name, after):
                sp.wait_ge(piece_done, G[after].p1)
                if i == 0:
                    sp.wait_ge(st_mkv, 64)
                sp.dma_start(mem_k[:].rearrange("p h n -> p (h n)"), mem_store[i][:, 0]).then_inc(ld_mkv, 16)
                sp.dma_start(mem_v[:].rearrange("p t n -> p (t n)"), mem_store[i][:, 1]).then_inc(ld_mkv, 16)

            for name in ("mem_k0", "mem_v0", "mem_k1", "mem_v1"):
                load(name)
            load("ada")
            all_taken(sp, G["mem_v1"])
            for i in range(2):
                sp.dma_start(mem_store[i][:, 0], mem_k_out[:, i].rearrange("p h n -> p (h n)")).then_inc(st_mkv, 16)
                sp.dma_start(mem_store[i][:, 1], mem_v_out[:, i].rearrange("p t n -> p (t n)")).then_inc(st_mkv, 16)
            load("gla_q")
            load("gla_k")
            load("gla_v")
            load("gla_gk")
            sp.wait_ge(nm_lo, N["mix"].c0 + DC)
            sp.dma_start(gla_const[:].rearrange("p a b c -> p (a b c)"), A["gla_const"]).then_inc(ld_gla, 16)
            sp.dma_start(gk_w[:], A["gla_gk_w"][0]).then_inc(ld_gk, 16)
            sp.dma_start(gk_b[:], A["gla_gk_b"]).then_inc(ld_gk, 16)
            for name in ("gla_g", "gate_a", "gla_wo", "mla_cq", "mla_ckv", "mla_kr", "gate_b"):
                load(name)
            for hf in range(2):
                for name in ("mla_qn", "mla_qr", "mla_k", "mla_v"):
                    load(f"{name}{hf}")
            for name in ("mla_wo", "w_out", "ffn_in0", "ffn_down0", "ffn_in1", "ffn_down1",
                         "pool_u", "pool_zu", "pool_qm", "pool_zm"):
                load(name)
            load("pool_w")
            mem_kv_load(0, "mem_a", "pool_zm")
            for name in ("pool_out", "nsa_kc", "nsa_vc", "nsa_ks", "nsa_vs", "nsa_kw", "nsa_vw",
                         "cmp_k1", "cmp_k2", "cmp_v1", "cmp_v2", "nsa_q", "nsa_gl", "nsa_zq", "nsa_qm", "nsa_zm"):
                load(name)
            mem_kv_load(1, "mem_b", "nsa_zm")
            load("nsa_out")
            for tt in range(TT):
                for b in range(2):
                    sp.wait_ge(turn_out[b], TURNS_BEFORE_OUT + tt + 1)
                sp.dma_start(out[0, tt * P:(tt + 1) * P, :], out_rows[:, tt]).then_inc(st_out, 16)
            sp.wait_ge(st_out, 32)
            sp.wait_ge(st_mkv, 64)

        @block.gpsimd
        def _(pool):
            for i, name in enumerate(("positions", "positions_2")):
                if i:
                    pool.wait_ge(at_t, U0["mem_a"] + len(UNITS["mem_a"]))
                pool.dma_start(probs[:, 2, :].bitcast(I32), A[name].broadcast_to([P, S])).then_inc(ld_pos, 16)

        @block.tensor
        def _(pe):
            def mm(o, l, r, start, stop):
                return nc.tensor.matmul(o, l, r, start=start, stop=stop, skip_group_check=True)

            def product(name, x_hi, x_lo=None, ready=()):
                g = G[name]
                for s_, v_ in ready:
                    pe.wait_ge(s_, v_)
                for i, _ in turns(pe, g):
                    for tb in range(g.body):
                        ps, tk = psum_tile(g, tb)
                        use = (g.t0 + tb) // 2
                        if use:
                            pe.wait_ge(tk, use + per(i, g.body // 2))
                        for q in range(g.kp):
                            p = g.p0 + tb * g.kp + q
                            if g.split:
                                s_ = g.s0 + tb * g.kp + q
                                pe.wait_ge(cut_lo, s_ + 1 + per(i, g.body * g.kp))
                                slots = [w_hi[s_ % 2], w_lo[s_ % 2]]
                                passes = [(0, x_hi), (1, x_hi), (0, x_lo)]
                            else:
                                pe.wait_ge(landed[p % 4], LANDED[p] + per(i, 16 * g.body * g.kp // 4))
                                slots, passes = [w_raw[p % 4]], [(0, x_hi)] + ([(0, x_lo)] if x_lo else [])
                            w = [t[:, 0:g.kc * g.width].rearrange("p (c n) -> p c n", c=g.kc) for t in slots]
                            for c in range(g.kc):
                                k = q * g.kc + c
                                begin, end = k == 0, k == g.kp * g.kc - 1
                                for a, (wi, xx) in enumerate(passes):
                                    first, final = begin and a == 0, end and a == len(passes) - 1
                                    xk = xx(tb, k)
                                    if g.mode == "T":
                                        n = xk.shape[-1]
                                        pad = 1 if n == 1 else S
                                        for b in range((g.width + P - 1) // P):
                                            m = min(P, g.width - b * P)
                                            last = mm(ps[0:m, b * pad:b * pad + n], w[wi][:, c, b * P:b * P + m], xk,
                                                      first and (b * pad) % 512 == 0, final)
                                    elif g.mode == "N":
                                        for tt in range(TT):
                                            last = mm(ps[:, tt * 512:tt * 512 + g.width],
                                                      xk[:, tt * P:(tt + 1) * P], w[wi][:, c, :], first, final)
                                    else:
                                        for gg in range(NSA_G):
                                            last = mm(ps[0:NCMP, gg * HD:(gg + 1) * HD],
                                                      xk[:, gg * NCMP:(gg + 1) * NCMP], w[wi][:, c, :],
                                                      first and gg == 0, final)
                            last.then_inc(piece_done, 1)

            def of(t, c0=0):
                return lambda tb, k: t[:, c0 + k, :]

            def norm(name):
                n = N[name]
                for j in range(n.n // 2):
                    pe.wait_ge(nm_sq, n.a0 + j + 1)
                    if j == 0 and n.k:
                        pe.wait_ge(nm_var, n.k)
                    for e in range(2):
                        last = mm(bank[0][:, 0:S], ones, SCRATCH[name][0][:, j % 2, e * S:(e + 1) * S],
                                  j == 0 and e == 0, j == n.n // 2 - 1 and e == 1)
                    last.then_inc(nm_acc, 1)

            def rotate(name, rot, chunks):
                for j, t in enumerate(chunks):
                    k = ROPE0[name] + j
                    if k >= 2:
                        pe.wait_ge(rp_done, k - 1)
                    mm(bank[1 + k % 2][:, 0:t.shape[-1]], rot, t, True, True).then_inc(rp_rot, 1)

            def attention(name):
                us, u0, f0 = UNITS[name], U0[name], FIN0[name]
                n, fins = len(us), f0
                for s_ in range(n + 3):
                    if s_ < n:
                        u = us[s_]
                        if u0 + s_ >= 2:
                            pe.wait_ge(at_masked, u0 + s_ - 1)
                        for e, (l, r) in enumerate(u["scores"]):
                            last = mm(bank[s_ % 2][:, 0:u["nk"]], l, r, e == 0, e == len(u["scores"]) - 1)
                        last.then_inc(at_s, 1)
                    if 0 <= s_ - 2 < n:
                        e, u = s_ - 2, us[s_ - 2]
                        pe.wait_ge(at_p, u0 + e + 1)
                        if u0 + e:
                            pe.wait_ge(at_pt, u0 + e)
                        for j in range(len(u["v"])):
                            k = min(P, u["nk"] - j * P)
                            last = nc.tensor.transpose(bank[2][0:k, j * P:(j + 1) * P],
                                                       probs[:, (u0 + e) % 3, j * P:j * P + k], ident)
                        last.then_inc(at_t, 1)
                    if 0 <= s_ - 3 < n:
                        e, u = s_ - 3, us[s_ - 3]
                        pe.wait_ge(at_pt, u0 + e + 1)
                        if u["first"] and fins:
                            pe.wait_ge(at_fin, fins)
                        for j, v in enumerate(u["v"]):
                            k = min(P, u["nk"] - j * P)
                            last = mm(bank[3][:, 0:P], v, probs_t[0:k, (u0 + e) % 2, j, :],
                                      u["first"] and j == 0, u["last"] and j == len(u["v"]) - 1)
                        fins += u["last"]
                        last.then_inc(at_o, 1)

            pe.wait_ge(ld_const, 16)
            pe.wait_ge(ld_vec, 16 * N_VEC_DMA)
            for t in range(3):
                n = min(P, VEC_W - t * P)
                last = nc.tensor.transpose(bank[0][:, t * P:t * P + n], vec_rows[0:n, t, :], ident[0:n, 0:n])
            last.then_inc(vec_turned, 1)
            for k in range(8):
                if k % 4 == 0:
                    pe.wait_ge(ld_x if k else ld_mem, 16)
                src = x_rows if k >= 4 else mem_rows
                if k >= 2:
                    pe.wait_ge(turn_out[k % 2], k // 2)
                for c in range(4):
                    for tt in range(TT):
                        last = nc.tensor.transpose(tile_ps[k % 2][:, c * S + tt * P:c * S + (tt + 1) * P],
                                                   src[:, tt, (k % 4 * 4 + c) * P:(k % 4 * 4 + c + 1) * P], ident)
                last.then_inc(turned, 1)
            pe.wait_ge(vec_ready, 1)
            for b in range(2):
                pe.wait_ge(turn_out[b], 4)
            norm("mem0")
            h = (of(h_hi), of(h_lo))
            o = (of(o_hi), of(o_lo))
            done = lambda n: [(nm_lo, N[n].c0 + N[n].n)]
            product("mem_k0", *h, ready=done("mem0"))
            product("mem_v0", *h)
            norm("mem1")
            product("mem_k1", *h, ready=done("mem1"))
            product("mem_v1", *h)
            product("ada", lambda tb, k: c_act[:, k:k + 1], ready=[(c_ready, 1)])
            norm("mix")
            product("gla_q", *h, ready=done("mix"))
            product("gla_k", *h)
            product("gla_v", *h)
            product("gla_gk", of(h_hi32), of(h_lo32))
            all_taken(pe, G["gla_gk"])
            pe.wait_ge(ld_gk, 32)
            for tt in range(TT):
                for e in range(2):
                    half = slice(e * 512, (e + 1) * 512)
                    mm(misc_ps[tt][:, half], gk_t[0:RANK, tt * P:(tt + 1) * P], gk_w[:, half], True, False)
                    last = mm(misc_ps[tt][:, half], ones[0:1, :], gk_b[:, half], False, True)
                last.then_inc(z_ready, 1)

            def decays(e):
                hd, tt, d = e // 4, e // 2 % 2, e % 2
                if e == 0:
                    pe.wait_ge(la_ready, 2)
                    pe.wait_ge(ld_gla, 16)
                if e >= 2:
                    pe.wait_ge(gl_ex, e - 1)
                for c in range(2):
                    last = mm(misc_ps[e % 2][:, c * 512:(c + 1) * 512],
                              log_a[:, tt, (2 * hd + d) * P:(2 * hd + d + 1) * P],
                              gla_const[:, tt, 4 * c:4 * c + 4, :], True, True)
                last.then_inc(gl_e, 1)

            def gla_scores(k):
                hd, tt = k // 2, k % 2
                pe.wait_ge(gl_qk, 2 * k + 2)
                if k:
                    pe.wait_ge(gl_red, k)
                for l in range(GLA_SLOTS):
                    for d in range(2):
                        if l < LEVELS:
                            kk, qq = k_lev[:, d, l, :], q_lev[:, d, l, :]
                        else:
                            kk, qq = (qk[:, hd, c + d, tt * P:(tt + 1) * P] for c in (2, 0))
                        last = mm(tile_ps[0][:, l * P:(l + 1) * P], kk, qq, l % 4 == 0 and d == 0, d == 1)
                if tt:
                    if hd:
                        pe.wait_ge(gl_out, hd)
                    for d in range(2):
                        last = mm(tile_ps[1][:, 0:P], k_across[:, d, :], q_lev[:, d, LEVELS, :], d == 0, d == 1)
                last.then_inc(gl_att, 1)

            def gla_output(hd):
                pe.wait_ge(gl_red, 2 * hd + 2)
                for c in range(BLK):
                    v = slice(hd * GLA_DV + c * P, hd * GLA_DV + (c + 1) * P)
                    mm(tile_ps[1][:, c * S:(c + 1) * S], gla_v[:, 0, v], gla_att[:, 0:2, :], c % 2 == 0, False)
                    last = mm(tile_ps[1][:, c * S + P:(c + 1) * S], gla_v[:, 1, v], gla_att[:, 2, :], False, True)
                last.then_inc(gl_o, 1)

            decays(0)
            decays(1)
            for k in range(2 * GLA_H):
                for e in (2 * k + 2, 2 * k + 3):
                    if e < 4 * GLA_H:
                        decays(e)
                gla_scores(k)
                if k % 2:
                    gla_output(k // 2)
            for hd in range(GLA_H):
                norm(f"gla{hd}")
            pe.wait_ge(gl_out, GLA_H)
            product("gla_g", *h)
            product("gate_a", *h)
            for b in range(2):
                pe.wait_ge(taken[b], (G["gla_g"].t1 - b + 1) // 2)
            product("gla_wo", *o)
            product("mla_cq", *h)
            product("mla_ckv", *h)
            product("mla_kr", of(h_hi32), of(h_lo32))
            product("gate_b", *h)
            norm("cq")
            norm("ckv")
            all_taken(pe, G["mla_kr"])
            rotate("mla_kr", cst("rot_mla"), [k_rope[:, :]])
            for hf in range(2):
                q_op, kv_op = (of(cq_hi), of(cq_lo)), (of(ckv_hi), of(ckv_lo))
                product(f"mla_qn{hf}", *q_op, ready=done("cq"))
                product(f"mla_qr{hf}", *q_op)
                all_taken(pe, G[f"mla_qr{hf}"])
                rotate(f"mla_q{hf}", cst("rot_mla"), [mla_qr[:, c, :] for c in range(BLK)])
                product(f"mla_k{hf}", *kv_op, ready=done("ckv"))
                product(f"mla_v{hf}", *kv_op)
                all_taken(pe, G[f"mla_v{hf}"])
                pe.wait_ge(rp_done, ROPE0[f"mla_q{hf}"] + BLK)
                attention(f"mla{hf}")
            fin = lambda a: [(at_fin, FIN0[a] + sum(u["last"] for u in UNITS[a]))]
            product("mla_wo", *o, ready=fin("mla1"))
            all_taken(pe, G["mla_wo"])
            product("w_out", *h)
            norm("ffn")
            product("ffn_in0", *h, ready=done("ffn"))
            all_taken(pe, G["ffn_in0"])
            product("ffn_down0", of(sw_hi), of(sw_lo))
            product("ffn_in1", *h)
            all_taken(pe, G["ffn_in1"])
            product("ffn_down1", of(sw_hi), of(sw_lo))
            norm("final1")
            norm("pool")
            product("pool_u", *h, ready=done("pool"))
            product("pool_zu", *h)
            product("pool_qm", *h)
            product("pool_zm", *h)
            pe.wait_ge(pl_lo, 1)
            product("pool_w", lambda tb, k: pool_hi[:, 3 * tb + k, :], lambda tb, k: pool_lo[:, 3 * tb + k, :])
            all_taken(pe, G["pool_zm"])
            pe.wait_ge(ld_mkv, 32)
            attention("mem_a")
            all_taken(pe, G["pool_w"])
            product("pool_out", *o, ready=fin("mem_a"))
            norm("kv")
            product("nsa_kc", *h, ready=done("kv"))
            for name in ("vc", "ks", "vs", "kw", "vw"):
                product(f"nsa_{name}", *h)
            for n_, kv in enumerate("kv"):
                product(f"cmp_{kv}1", of(z_pe), ready=[(zp_ready, n_ + 1)])
                all_taken(pe, G[f"cmp_{kv}1"])
                product(f"cmp_{kv}2", of(hidden))
            rotate("nsa_ks", cst("rot_nsa"), [ks[:, c, :] for c in range(NSA_G)])
            rotate("nsa_kw", cst("rot_nsa"), [kw[:, c, :] for c in range(NSA_G)])
            all_taken(pe, G["cmp_k2"])
            rotate("cmp_k", cst("rot_nsa"), [k_cmp[:, :]])
            norm("nsa")
            product("nsa_q", *h, ready=done("nsa"))
            product("nsa_gl", of(h_hi32), of(h_lo32))
            product("nsa_zq", *h)
            rotate("nsa_q", cst("rot_nsa"), [nsa_q[:, c, :] for c in range(NSA_H)])
            product("nsa_qm", *h)
            product("nsa_zm", *h)
            all_taken(pe, G["nsa_zm"])
            pe.wait_ge(rp_done, ROPE0["nsa_q"] + NSA_H)
            attention("nsa")
            pe.wait_ge(ld_mkv, 64)
            attention("mem_b")
            product("nsa_out", *o, ready=fin("mem_b"))
            norm("final2")
            pe.wait_ge(nm_plain, PLAIN_BEFORE["final2"] + DC)
            for k in range(4):
                pe.wait_ge(turn_out[k % 2], TURNS_BEFORE_OUT + k // 2)
                if k < 2:
                    all_taken(pe, G["nsa_out"])
                for c in range(8):
                    last = nc.tensor.transpose(tile_ps[k % 2][:, c * P:(c + 1) * P],
                                               x[:, k % 2 * 8 + c, k // 2 * P:(k // 2 + 1) * P], ident)
                last.then_inc(turned, 1)

        @block.scalar
        def _(act):
            own = Steps(act, act_step)
            f = nc.scalar.activation

            def cut(g, i, s_, p):
                act.wait_ge(landed[p % 4], LANDED[p] + per(i, 16 * g.body * g.kp // 4))
                if s_ >= 2:
                    act.wait_ge(piece_done, p - 1 + per(i, g.body * g.kp))
                f(w_hi[s_ % 2][:], w_raw[p % 4][:], ACT.Copy).then_inc(cut_hi, 1)

            def product(name, take=None):
                g = G[name]
                if g.split and not g.first_ahead:
                    cut(g, 0, g.s0, g.p0)
                for i, last in turns(act, g, peel_last=g.split and not g.ahead):
                    for tb in range(g.body):
                        if g.split:
                            for q in range(1, g.kp + 1):
                                e = tb * g.kp + q
                                if not (e == g.body * g.kp and last and not g.ahead):
                                    cut(g, i, g.s0 + e, g.p0 + e)
                        if take:
                            ps, tk = psum_tile(g, tb)
                            tile_is_done(act, g, i, tb)
                            take(i, tb, g, ps, tk)

            def copy_to(dst, func=ACT.Copy, scale=1.0, pre=()):
                def take(i, tb, g, ps, tk):
                    for s_, v_ in pre:
                        if tb == 0:
                            act.wait_ge(s_, v_)
                    d = dst(i, tb, g)
                    n = int(np.prod(d.shape[1:]))
                    src = ps[0:d.shape[0], 0:n]
                    if len(d.shape) == 3:
                        src = src.rearrange("p (a b) -> p a b", a=d.shape[1])
                    elif len(d.shape) == 4:
                        src = src.rearrange("p (a b c) -> p a b c", a=d.shape[1], b=d.shape[2])
                    f(d, src, func, scale=scale).then_inc(tk, 1)
                return take

            def chunks(t):
                return lambda i, tb, g: t[:, bass.ds(per(i, g.body * BLK) + tb * BLK, BLK), :]

            def columns(t):
                return lambda i, tb, g: t[:, :, bass.ds(per(i, g.body * NT) + tb * NT, NT)]

            def norm(name):
                n = N[name]
                sq = SCRATCH[name][0]
                src = SOURCE[name]
                for j in range(n.n // 2):
                    if j >= 2 or n.k:
                        act.wait_ge(nm_acc, n.a0 + j - 1 if j >= 2 else n.a0)
                    f(sq[:, j % 2, :].rearrange("p (a b) -> p a b", a=2), src(slice(2 * j, 2 * j + 2)),
                      ACT.Square).then_inc(nm_sq, 1)
                act.wait_ge(nm_var, n.k + 1)
                f(rstd[:], var[:], ACT.Sqrt).then_inc(nm_std, 1)
                if n.split:
                    tmp, hi = SCRATCH[name][1], DEST[name][0]
                    shift = SHIFT.get(name)
                    for c in range(n.n):
                        act.wait_ge(nm_t, n.c0 + c + 1)
                        f(hi[:, c, :], tmp[:, c % 2, :], ACT.Identity,
                          bias=shift[:, c:c + 1] if shift is not None else 0.0).then_inc(nm_hi, 1)

            def attention(name):
                us, u0 = UNITS[name], U0[name]
                n = len(us)
                for s_ in range(n + 2):
                    if s_ < n:
                        k = u0 + s_
                        p = probs[:, k % 3, 0:us[s_]["nk"]]
                        act.wait_ge(at_max, k + 1)
                        f(p, p, ACT.Exp, bias=stats[:, k % 4:k % 4 + 1],
                          accum_out=stats[:, 4 + k % 4:5 + k % 4]).then_inc(at_exp, 1)
                    if 0 <= s_ - 2 < n:
                        k, u = u0 + s_ - 2, us[s_ - 2]
                        act.wait_ge(at_t, k + 1)
                        if k >= 2:
                            act.wait_ge(at_o, k - 1)
                        nv = len(u["v"])
                        r = min(P, u["nk"])
                        f(probs_t[0:r, k % 2, 0:nv, :], bank[2][0:r, 0:nv * P].rearrange("p (a b) -> p a b", a=nv),
                          ACT.Copy).then_inc(at_pt, 1)

            def tables(k):
                act.wait_ge(tab_arg, k + 1)
                f(rope_sin[:], probs[:, 1, :], ACT.Sin).then_inc(tab_ready, 1)
                f(rope_cos[:], probs[:, 0, :], ACT.Sin, scale=-1.0, bias=half_pi).then_inc(tab_ready, 1)

            for k in range(8):
                if k % 2 == 0:
                    act.wait_ge(turned, k + 1)
                    dst = x if k >= 4 else mem_t
                    f(dst[:, k % 4 * 4:k % 4 * 4 + 4, :], tile_ps[0][:].rearrange("p (a b) -> p a b", a=4),
                      ACT.Copy).then_inc(turn_out[0], 1)
            act.wait_ge(vec_ready, 1)
            f(c_act[:], vec("c", 0, DC), ACT.Silu).then_inc(c_ready, 1)
            tables(0)
            act.wait_ge(turn_out[0], 4)
            act.wait_ge(turn_out[1], 4)
            norm("mem0")
            for li in range(2):
                if li:
                    norm("mem1")
                product(f"mem_k{li}", copy_to(lambda i, tb, g, li=li: mem_k_out[:, li]))
                product(f"mem_v{li}", copy_to(lambda i, tb, g, li=li: mem_v_out[:, li]))
            product("ada")
            norm("mix")
            stored = [(st_mkv, 64)]
            pair = lambda c0: (lambda i, tb, g: qk[:, bass.ds(per(i, 2 * g.body) + 2 * tb, 2), c0:c0 + 2, :])
            product("gla_q", copy_to(pair(0), scale=GLA_DK ** -0.5, pre=stored))
            product("gla_k", copy_to(pair(2)))
            product("gla_v", copy_to(columns(gla_v)))
            product("gla_gk", copy_to(lambda i, tb, g: gk_t[0:RANK, :]))
            for tt in range(TT):
                act.wait_ge(z_ready, tt + 1)
                la = log_a[:, tt, :]
                own.wait(f(la, misc_ps[tt][:], ACT.Abs))
                own.wait(f(la, la, ACT.Exp, scale=-1.0))
                f(la, la, ACT.Ln, bias=1.0).then_inc(z_abs, 1)
            for k in range(2 * GLA_H):
                for e in (2 * k, 2 * k + 1):
                    act.wait_ge(gl_e, e + 1)
                    if e >= 2:
                        act.wait_ge(gl_qk, e - 1)
                    if e < 2:
                        act.wait_ge(ld_gk, 32)
                    f(decay[e % 2][:], misc_ps[e % 2][:].rearrange("p (a b) -> p a b", a=GLA_SLOTS),
                      ACT.Exp).then_inc(gl_ex, 1)
                if k % 2 == 0 and k:
                    hd = k // 2 - 1
                    act.wait_ge(gl_o, hd + 1)
                    f(qk[:, hd], tile_ps[1][:].rearrange("p (a b) -> p a b", a=4), ACT.Copy).then_inc(gl_out, 1)
            act.wait_ge(gl_o, GLA_H)
            f(qk[:, GLA_H - 1], tile_ps[1][:].rearrange("p (a b) -> p a b", a=4), ACT.Copy).then_inc(gl_out, 1)
            act.wait_ge(gl_out, GLA_H)
            for hd in range(GLA_H):
                norm(f"gla{hd}")

            def silu_g(i, tb, g, ps, tk):
                if tb == 0:
                    act.wait_ge(nm_plain, PLAIN_BEFORE["gla3"] + 4)
                f(gla_tmp[:, tb % 2, :], ps[:], ACT.Silu).then_inc(silu_ready, 1)

            product("gla_g", silu_g)
            for_ga = [(nm_plain, PLAIN_BEFORE["gla3"] + 4)]
            product("gate_a", copy_to(chunks(merged), ACT.Sigmoid, pre=for_ga))
            product("gla_wo")
            product("mla_cq", copy_to(lambda i, tb, g: cq[:, :, :], pre=[(piece_done, G["gla_wo"].p1)]))
            product("mla_ckv", copy_to(lambda i, tb, g: ckv[:, :, :]))
            product("mla_kr", copy_to(lambda i, tb, g: k_rope[:, :]))
            product("gate_b", copy_to(chunks(gate_b), ACT.Sigmoid, pre=[(taken[b], (G["gla_g"].t1 - b + 1) // 2) for b in range(2)]))
            all_taken(act, G["mla_ckv"])
            norm("cq")
            norm("ckv")
            for hf in range(2):
                free = [(piece_done, G["gate_b"].p1)] if hf == 0 else [(at_o, U0["mla0"] + 2 * HALF_H)]
                product(f"mla_qn{hf}", copy_to(lambda i, tb, g: mla_q[:, 4 * tb:4 * tb + 4, :], pre=free))
                product(f"mla_qr{hf}", copy_to(lambda i, tb, g: mla_qr[:, :, :]))
                product(f"mla_k{hf}", copy_to(lambda i, tb, g: mla_k[:, 4 * tb:4 * tb + 4, :]))
                product(f"mla_v{hf}", copy_to(lambda i, tb, g: mla_v[:, :, tb * NT:(tb + 1) * NT]))
                attention(f"mla{hf}")
            product("mla_wo")
            product("w_out")
            all_taken(act, G["w_out"])
            norm("ffn")

            def silu_gate(part):
                def take(i, tb, g, ps, tk):
                    if tb % 2:
                        return
                    act.wait_ge(taken[(g.t0 + 1) % 2], (g.t0 + 1 + tb) // 2 + per(i, g.body // 2))
                    f(o_tmp[:, 0, :], ps[:], ACT.Silu).then_inc(tk, 1)
                return take

            product("ffn_in0", silu_gate(0))
            product("ffn_down0")
            product("ffn_in1", silu_gate(1))
            product("ffn_down1")
            all_taken(act, G["ffn_down1"])
            norm("final1")
            act.wait_ge(nm_plain, PLAIN_BEFORE["final1"] + DC)
            norm("pool")
            product("pool_u", copy_to(chunks(u_t), pre=[(piece_done, G["ffn_down1"].p1)]))
            product("pool_zu", copy_to(chunks(silu_z), ACT.Silu))
            act.wait_ge(pl_t, 1)
            f(pool_hi[:], run_b[:], ACT.Copy).then_inc(pl_hi, 1)
            product("pool_qm", copy_to(lambda i, tb, g: mem_q[:, :, :], pre=[(pl_lo, 1)]))
            product("pool_zm", copy_to(lambda i, tb, g: mem_z[:, :, :], ACT.Silu))
            product("pool_w")
            attention("mem_a")
            tables(1)
            product("pool_out")
            all_taken(act, G["pool_out"])
            norm("kv")
            product("nsa_kc", copy_to(lambda i, tb, g: kc[:, :, :], pre=[(at_fin, FIN0["nsa"])]))
            product("nsa_vc", copy_to(lambda i, tb, g: vc[:, :, :]))
            product("nsa_ks", copy_to(lambda i, tb, g: ks[:, :, :]))
            product("nsa_vs", copy_to(lambda i, tb, g: vs[:, :, :]))
            product("nsa_kw", copy_to(lambda i, tb, g: kw[:, :, :]))
            product("nsa_vw", copy_to(lambda i, tb, g: vw[:, :, :]))
            n60 = NSA_G * NCMP
            for n_, kv in enumerate("kv"):
                def hid(i, tb, g, ps, tk):
                    f(hidden[:], ps[:, 0:512].rearrange("p (a b) -> p a b", a=2)[:, :, 0:n60],
                      ACT.Silu).then_inc(tk, 1)
                product(f"cmp_{kv}1", hid)
                product(f"cmp_{kv}2", copy_to(lambda i, tb, g: k_cmp[:, :] if kv == "k" else v_cmp[:, :]))
            norm("nsa")
            product("nsa_q", copy_to(chunks(nsa_q)))

            def gate_take(i, tb, g, ps, tk):
                f(gates[:], ps[:].rearrange("p (a b) -> p a b", a=2)[:, :, 0:3 * NSA_H], ACT.Sigmoid).then_inc(tk, 1)

            product("nsa_gl", gate_take)
            product("nsa_zq", copy_to(chunks(silu_z), ACT.Silu))
            product("nsa_qm", copy_to(lambda i, tb, g: mem_q[:, :, :], pre=[(zp_ready, 2)]))
            product("nsa_zm", copy_to(lambda i, tb, g: mem_z[:, :, :], ACT.Silu))
            attention("nsa")
            attention("mem_b")
            product("nsa_out")
            all_taken(act, G["nsa_out"])
            norm("final2")
            for k in (0, 2):
                act.wait_ge(turned, 8 + k + 1)
                f(out_rows[:, k // 2, 0:1024], tile_ps[0][:], ACT.Copy).then_inc(turn_out[0], 1)

        @block.vector
        def _(dve):
            v = nc.vector
            own = Steps(dve, dve_step)

            def f32(t):
                return t.bitcast(F32)

            def cut(g, i, s_, p):
                dve.wait_ge(cut_hi, s_ + 1 + per(i, g.body * g.kp))
                v.tensor_tensor(w_lo[s_ % 2][:], w_raw[p % 4][:], f32(w_hi[s_ % 2][:]),
                                ALU.subtract).then_inc(cut_lo, 1)

            def product(name, take=None):
                g = G[name]
                if g.split and not g.first_ahead:
                    cut(g, 0, g.s0, g.p0)
                for i, last in turns(dve, g, peel_last=g.split and not g.ahead):
                    for tb in range(g.body):
                        if g.split:
                            for q in range(1, g.kp + 1):
                                e = tb * g.kp + q
                                if not (e == g.body * g.kp and last and not g.ahead):
                                    cut(g, i, g.s0 + e, g.p0 + e)
                        if take:
                            ps, tk = psum_tile(g, tb)
                            take(i, tb, g, ps, tk)

            def step(i, tb, g, j, ins):
                ins.then_inc(tile_step, 1)
                k = STEPS[g.name]
                dve.wait_ge(tile_step, STEP0[g.name] + k * tb + j + 1 + per(i, k * g.body))

            def in_chunks(t, n=BLK):
                return t.rearrange("p (a b) -> p a b", a=n)

            def some(t, i, tb, g, n=BLK):
                return t[:, bass.ds(per(i, g.body * n) + tb * n, n), :]

            def split_to(i, tb, g, j, src, hi, lo, tk):
                step(i, tb, g, j, v.tensor_copy(hi, src))
                v.tensor_tensor(lo, src, f32(hi), ALU.subtract).then_inc(tk, 1)

            def norm(name):
                n = N[name]
                src, gain = SOURCE[name], GAIN[name]
                dve.wait_ge(nm_acc, n.a0 + n.n // 2)
                if n.k:
                    dve.wait_ge(nm_std, n.k)
                v.tensor_scalar(var[:], bank[0][:, 0:S], 1.0 / (n.n * P), EPS, ALU.mult, ALU.add).then_inc(nm_var, 1)
                dve.wait_ge(nm_std, n.k + 1)
                own.wait(v.reciprocal(rstd[:], rstd[:]))
                if not n.split:
                    for c in range(n.n):
                        v.scalar_tensor_tensor(DEST[name][0][:, c, :], src(c), gain[:, c:c + 1], rstd[:],
                                               ALU.mult, ALU.mult).then_inc(nm_plain, 1)
                    return
                tmp, (hi, lo) = SCRATCH[name][1], DEST[name]
                shift = SHIFT.get(name)
                for c in range(n.n + 1):
                    if c < n.n:
                        if n.c0 + c:
                            dve.wait_ge(nm_lo, n.c0 + max(c - 1, 0))
                        v.scalar_tensor_tensor(tmp[:, c % 2, :], src(c), gain[:, c:c + 1], rstd[:],
                                               ALU.mult, ALU.mult).then_inc(nm_t, 1)
                    if c:
                        e = c - 1
                        dve.wait_ge(nm_hi, n.c0 + e + 1)
                        if shift is None:
                            ins = v.tensor_tensor(lo[:, e, :], tmp[:, e % 2, :], f32(hi[:, e, :]), ALU.subtract)
                        else:
                            ins = v.scalar_tensor_tensor(lo[:, e, :], tmp[:, e % 2, :], shift[:, e:e + 1],
                                                         f32(hi[:, e, :]), ALU.add, ALU.subtract)
                        ins.then_inc(nm_lo, 1)

            def rotate(name, chunks, cos=None, sin=None):
                for j, t in enumerate(chunks):
                    k = ROPE0[name] + j
                    n = t.shape[-1] if len(t.shape) == 2 else t.shape[1] * t.shape[2]
                    dve.wait_ge(rp_rot, k + 1)
                    if k:
                        dve.wait_ge(rp_done, k)
                    src = bank[1 + k % 2][:, 0:n]
                    tmp = var[:, 0:n]
                    if len(t.shape) == 3:
                        src, tmp = (a.rearrange("p (a b) -> p a b", a=t.shape[1]) for a in (src, tmp))
                    v.tensor_tensor(tmp, src, sin if sin is not None else rope_sin[:], ALU.mult)
                    own.wait(v.tensor_tensor(t, t, cos if cos is not None else rope_cos[:], ALU.mult))
                    v.tensor_tensor(t, t, tmp, ALU.add).then_inc(rp_done, 1)
                dve.wait_ge(rp_done, k + 1)

            def attention(name):
                us, u0, fins = UNITS[name], U0[name], FIN0[name]
                n = len(us)
                for s_ in range(n + 4):
                    if s_ < n:
                        u, k = us[s_], u0 + s_
                        p = probs[:, k % 3, 0:u["nk"]]
                        dve.wait_ge(at_s, k + 1)
                        if k >= 3:
                            dve.wait_ge(at_t, k - 2)
                        if u["add"] is None:
                            v.tensor_scalar(p, bank[s_ % 2][:, 0:u["nk"]], u["scale"], None, ALU.mult).then_inc(at_masked, 1)
                        else:
                            v.scalar_tensor_tensor(p, bank[s_ % 2][:, 0:u["nk"]], u["scale"], u["add"],
                                                   ALU.mult, ALU.add).then_inc(at_masked, 1)
                        dve.wait_ge(at_masked, k + 1)
                        v.tensor_reduce(stats[:, k % 4:k % 4 + 1], p, AX.X, ALU.max, negate=True).then_inc(at_max, 1)
                    if 0 <= s_ - 1 < n:
                        u, k = us[s_ - 1], u0 + s_ - 1
                        p = probs[:, k % 3, 0:u["nk"]]
                        r = stats[:, 8 + k % 2:9 + k % 2]
                        dve.wait_ge(at_exp, k + 1)
                        own.wait(v.reciprocal(r, stats[:, 4 + k % 4:5 + k % 4]))
                        if u["mul"] is not None:
                            rg = stats[:, 10 + k % 2:11 + k % 2]
                            own.wait(v.tensor_tensor(rg, r, u["gate"], ALU.mult))
                            v.scalar_tensor_tensor(p, p, rg, u["mul"], ALU.mult, ALU.mult).then_inc(at_p, 1)
                        elif u["gate"] is not None:
                            v.tensor_scalar(p, p, r, u["gate"], ALU.mult, ALU.mult).then_inc(at_p, 1)
                        else:
                            v.tensor_scalar(p, p, r, None, ALU.mult).then_inc(at_p, 1)
                    if 0 <= s_ - 4 < n and us[s_ - 4]["last"]:
                        u, k = us[s_ - 4], u0 + s_ - 4
                        dve.wait_ge(at_o, k + 1)
                        hi, lo = o_hi[:, u["chunk"], u["q"]], o_lo[:, u["chunk"], u["q"]]
                        src = bank[3][:, 0:P]
                        if fins:
                            dve.wait_ge(at_fin, fins)
                        fins += 1
                        if u["z"] is not None:
                            own.wait(v.tensor_tensor(var[:, 0:P], src, u["z"], ALU.mult))
                            src = var[:, 0:P]
                        own.wait(v.tensor_copy(hi, src))
                        v.tensor_tensor(lo, src, f32(hi), ALU.subtract).then_inc(at_fin, 1)

            def tables(k):
                dve.wait_ge(ld_pos, 16 * (k + 1))
                pos, a, t = probs[:, 2, :], probs[:, 1, :], probs[:, 0, :]
                own.wait(v.tensor_copy(a, pos.bitcast(I32)))
                own.wait(v.tensor_scalar(a, a, cst(("freq_mla", "freq_nsa")[k]), None, ALU.mult))
                big = 1.5 * 2.0 ** 23
                own.wait(v.tensor_scalar(t, a, 1.0 / (2 * math.pi), big, ALU.mult, ALU.add))
                own.wait(v.tensor_scalar(t, t, -big, None, ALU.add))
                hi = 6.28125
                mid = float(np.float32(round((2 * math.pi - hi) * 2 ** 20) / 2 ** 20))
                for c in (hi, mid, 2 * math.pi - hi - mid):
                    own.wait(v.scalar_tensor_tensor(a, t, -c, a, ALU.mult, ALU.add))
                pi = 3.1415925
                own.wait(v.tensor_scalar(a, a, pi, -pi, ALU.min, ALU.max))
                v.scalar_tensor_tensor(t, a, -1.0, a, ALU.mult, ALU.max).then_inc(tab_arg, 1)
                dve.wait_ge(tab_ready, 2 * k + 2)

            v.memset(half_pi, math.pi / 2).then_inc(dve_step, 1)
            own.n += 1
            dve.wait_ge(dve_step, 1)
            dve.wait_ge(vec_turned, 1)
            v.tensor_copy(cols[:], bank[0][:, 0:VEC_W]).then_inc(vec_ready, 1)
            for k in range(8):
                if k % 2:
                    dve.wait_ge(turned, k + 1)
                    dst = x if k >= 4 else mem_t
                    v.tensor_copy(dst[:, k % 4 * 4:k % 4 * 4 + 4, :], in_chunks(tile_ps[1][:])).then_inc(turn_out[1], 1)
            dve.wait_ge(ld_const, 16)
            tables(0)
            dve.wait_ge(turn_out[0], 4)
            dve.wait_ge(turn_out[1], 4)
            norm("mem0")
            for li in range(2):
                if li:
                    dve.wait_ge(piece_done, G["mem_v0"].p1)
                    norm("mem1")
                product(f"mem_k{li}")
                product(f"mem_v{li}")

            def ada_take(i, tb, g, ps, tk):
                tile_is_done(dve, g, i, tb)
                a = VECTORS["ada_b"][0]
                v.tensor_tensor(mod[:, bass.ds(per(i, 4 * g.body) + 4 * tb, 4)], ps[:, 0:4],
                                cols[:, bass.ds(per(i, 4 * g.body) + a + 4 * tb, 4)], ALU.add).then_inc(tk, 1)

            product("ada", ada_take)
            all_taken(dve, G["ada"])
            for k, (name, part) in enumerate((("norm_mix_g", 1), ("norm_ffn_g", 4))):
                own.wait(v.scalar_tensor_tensor(gain_eff[:, k, :], mod[:, part * DC:(part + 1) * DC], 1.0,
                                                vec(name, 0, DC), ALU.add, ALU.mult))
            norm("mix")
            product("gla_q")
            product("gla_k")
            product("gla_v")
            product("gla_gk")
            for tt in range(TT):
                dve.wait_ge(z_abs, tt + 1)
                v.scalar_tensor_tensor(log_a[:, tt, :], misc_ps[tt][:], 0.0, log_a[:, tt, :],
                                       ALU.min, ALU.subtract).then_inc(la_ready, 1)

            all_taken(dve, G["gla_gk"])
            for k in range(2 * GLA_H):
                hd, tt = k // 2, k % 2
                if k:
                    dve.wait_ge(gl_att, k)
                for d in range(2):
                    e = 2 * k + d
                    dve.wait_ge(gl_ex, e + 1)
                    ex = decay[e % 2]
                    q, kk = (qk[:, hd, c + d, tt * P:(tt + 1) * P].unsqueeze(1) for c in (0, 2))
                    v.tensor_tensor(q_lev[:, d], q.broadcast_to([P, GLA_SLOTS, P]), ex[:], ALU.mult)
                    if tt == 0:
                        v.tensor_tensor(k_across[:, d, :], kk[:, 0, :], ex[:, LEVELS, :], ALU.mult)
                    v.tensor_tensor(k_lev[:, d, 0:LEVELS, :], kk.broadcast_to([P, LEVELS, P]), ex[:, 0:LEVELS, :],
                                    ALU.mult).then_inc(gl_qk, 1)
                dve.wait_ge(gl_att, k + 1)
                if tt == 0 and hd:
                    dve.wait_ge(gl_o, hd)
                sc = tile_ps[0][:].rearrange("p (l i) -> p l i", l=GLA_SLOTS)
                own.wait(v.tensor_tensor(sc, sc, gla_const[:, 2], ALU.mult))
                if tt:
                    v.tensor_copy(gla_att[:, 1, :], tile_ps[1][:, 0:P])
                v.tensor_reduce(gla_att[:, 2 * tt, :], tile_ps[0][:].rearrange("p (l i) -> p i l", l=GLA_SLOTS),
                                AX.X, ALU.add).then_inc(gl_red, 1)
            dve.wait_ge(gl_out, GLA_H)
            for hd in range(GLA_H):
                norm(f"gla{hd}")
            dve.wait_ge(nm_plain, PLAIN_BEFORE["gla3"] + 4)

            def gated(i, tb, g, ps, tk):
                dve.wait_ge(silu_ready, g.t0 - G["gla_g"].t0 + tb + 1 + per(i, g.body))
                o4 = qk[:, bass.ds(per(i, g.body) + tb, 1), :, :].rearrange("p a c n -> p (a c n)")
                step(i, tb, g, 0, v.tensor_tensor(o4, o4, gla_tmp[:, tb % 2, :], ALU.mult))
                split_to(i, tb, g, 1, in_chunks(o4), some(o_hi, i, tb, g), some(o_lo, i, tb, g), tk)

            product("gla_g", gated)
            product("gate_a")

            def gla_merge(i, tb, g, ps, tk):
                tile_is_done(dve, g, i, tb)
                m = some(merged, i, tb, g)
                v.tensor_tensor(m, m, in_chunks(ps[:]), ALU.mult).then_inc(tk, 1)

            all_taken(dve, G["gate_a"])
            product("gla_wo", gla_merge)
            product("mla_cq")
            product("mla_ckv")
            product("mla_kr")
            product("gate_b")
            all_taken(dve, G["mla_kr"])
            norm("cq")
            norm("ckv")
            rotate("mla_kr", [k_rope[:, :]])
            for hf in range(2):
                product(f"mla_qn{hf}")
                product(f"mla_qr{hf}")
                rotate(f"mla_q{hf}", [mla_qr[:, c, :] for c in range(BLK)])
                product(f"mla_k{hf}")
                product(f"mla_v{hf}")
                attention(f"mla{hf}")

            def both_merge(i, tb, g, ps, tk):
                tile_is_done(dve, g, i, tb)
                last_taken(dve, g, i, tb)
                t = in_chunks(mla_tmp[:])
                step(i, tb, g, 0, v.tensor_tensor(t, in_chunks(ps[:]), some(gate_b, i, tb, g), ALU.mult))
                step(i, tb, g, 1, v.tensor_tensor(t, t, some(merged, i, tb, g), ALU.add))
                split_to(i, tb, g, 2, t, some(h_hi, i, tb, g), some(h_lo, i, tb, g), tk)

            all_taken(dve, G["gate_b"])
            product("mla_wo", both_merge)

            def residual(tmp, part=None):
                def take(i, tb, g, ps, tk):
                    tile_is_done(dve, g, i, tb)
                    xx = some(x, i, tb, g)
                    if part is None:
                        v.tensor_tensor(xx, xx, in_chunks(ps[:]), ALU.add).then_inc(tk, 1)
                        return
                    gate = mod[:, bass.ds(per(i, g.body * BLK) + part * DC + tb * BLK, BLK)].unsqueeze(2)
                    last_taken(dve, g, i, tb)
                    t = in_chunks(tmp)
                    step(i, tb, g, 0, v.tensor_tensor(t, in_chunks(ps[:]), gate.broadcast_to([P, BLK, S]), ALU.mult))
                    v.tensor_tensor(xx, xx, t, ALU.add).then_inc(tk, 1)
                return take

            product("w_out", residual(o_tmp[:, 0, :], 2))
            all_taken(dve, G["w_out"])
            norm("ffn")

            def up(i, tb, g, ps, tk):
                if tb % 2 == 0:
                    return
                if g.name == "ffn_in1":
                    dve.wait_ge(piece_done, G["ffn_down0"].p1)
                tile_is_done(dve, g, i, tb)
                dve.wait_ge(taken[g.t0 % 2], (g.t0 + tb - 1) // 2 + 1 + per(i, g.body // 2))
                t = o_tmp[:, 0, :]
                n = g.body // 2
                k = STEPS[g.name]
                s0 = STEP0[g.name] + k * (tb // 2)
                v.tensor_tensor(t, ps[:], t, ALU.mult).then_inc(tile_step, 1)
                dve.wait_ge(tile_step, s0 + 1 + per(i, k * n))
                at_ = bass.ds(per(i, n * BLK) + tb // 2 * BLK, BLK)
                hi, lo = sw_hi[:, at_, :], sw_lo[:, at_, :]
                v.tensor_copy(hi, in_chunks(t)).then_inc(tile_step, 1)
                dve.wait_ge(tile_step, s0 + 2 + per(i, k * n))
                v.tensor_tensor(lo, in_chunks(t), f32(hi), ALU.subtract).then_inc(tk, 1)

            for part in range(2):
                product(f"ffn_in{part}", up)
                product(f"ffn_down{part}", residual(o_tmp[:, 1, :], 5))
            all_taken(dve, G["ffn_down1"])
            norm("final1")
            dve.wait_ge(nm_plain, PLAIN_BEFORE["final1"] + DC)
            norm("pool")

            product("pool_u")
            all_taken(dve, G["pool_u"])
            src, bufs = u_t, (run_a, run_b)
            for j in range(POOL_G):
                d, sh, c0 = bufs[j % 2], 2 ** j, 3 * j
                own.wait(v.tensor_copy(d[:, c0:, 0:sh], src[:, c0:, 0:sh]))
                own.wait(v.tensor_tensor(d[:, c0:, sh:], src[:, c0:, sh:], src[:, c0:, 0:S - sh], ALU.add))
                src = d
            for g_ in range(POOL_G):
                cs = slice(3 * g_, 3 * g_ + 3)
                s_ = bufs[g_ % 2]
                a = CONST["pool_head"][0] + 16 * g_
                head = const[:, a:a + 16].unsqueeze(1).broadcast_to([P, 3, 16])
                own.wait(v.tensor_tensor(s_[:, cs, 0:16], s_[:, cs, 0:16], head, ALU.mult))
                ins = v.scalar_tensor_tensor(run_b[:, cs, :], s_[:, cs, :], 0.5 ** (g_ + 1), u_t[:, cs, :],
                                             ALU.mult, ALU.subtract)
                if g_ == POOL_G - 1:
                    ins.then_inc(pl_t, 1)
                else:
                    own.wait(ins)
            product("pool_zu")
            dve.wait_ge(pl_hi, 1)
            v.tensor_tensor(pool_lo[:], run_b[:], f32(pool_hi[:]), ALU.subtract).then_inc(pl_lo, 1)
            product("pool_qm")
            product("pool_zm")

            def pool_take(i, tb, g, ps, tk):
                tile_is_done(dve, g, i, tb)
                last_taken(dve, g, i, tb)
                t = in_chunks(pool_tmp[:], 3)
                a = VECTORS["a_pool_scale_2"][0] + 3 * tb
                scale = cols[:, a:a + 3].unsqueeze(2).broadcast_to([P, 3, S])
                step(i, tb, g, 0, v.tensor_tensor(t, in_chunks(ps[:, 0:3 * S], 3), scale, ALU.mult))
                step(i, tb, g, 1, v.tensor_tensor(t, t, silu_z[:, 3 * tb:3 * tb + 3, :], ALU.mult))
                split_to(i, tb, g, 2, t, o_hi[:, 3 * tb:3 * tb + 3, :], o_lo[:, 3 * tb:3 * tb + 3, :], tk)

            all_taken(dve, G["pool_zm"])
            dve.wait_ge(pl_lo, 1)
            product("pool_w", pool_take)
            attention("mem_a")
            tables(1)
            product("pool_out", residual(None))
            all_taken(dve, G["pool_out"])
            norm("kv")
            for name in ("kc", "vc", "ks", "vs", "kw", "vw"):
                product(f"nsa_{name}")
            all_taken(dve, G["nsa_vw"])
            for n_, (kv, t) in enumerate((("k", kc), ("v", vc))):
                if n_:
                    dve.wait_ge(piece_done, G["cmp_k1"].p1)
                for a in range(2):
                    z = t[:].rearrange("p g (n b) -> p b g n", b=CMP_STRIDE)[:, :, :, a:a + NCMP]
                    for gg in range(NSA_G):
                        pe_ = vec("cmp_pe_2", n_ * CMP_LEN + 16 * a, 16).unsqueeze(2).broadcast_to([P, 16, NCMP])
                        ins = v.tensor_tensor(z_pe[:, 16 * a:16 * a + 16, gg * NCMP:(gg + 1) * NCMP], z[:, :, gg, :],
                                              pe_, ALU.add)
                ins.then_inc(zp_ready, 1)
                product(f"cmp_{kv}1")
                product(f"cmp_{kv}2")
            rotate("nsa_ks", [ks[:, c, :] for c in range(NSA_G)])
            rotate("nsa_kw", [kw[:, c, :] for c in range(NSA_G)])
            at_end = slice(CMP_LEN - 1, S, CMP_STRIDE)
            all_taken(dve, G["cmp_k2"])
            rotate("cmp_k", [k_cmp[:].rearrange("p (g n) -> p g n", g=NSA_G)],
                   rope_cos[:, at_end].unsqueeze(1).broadcast_to([P, NSA_G, NCMP]),
                   rope_sin[:, at_end].unsqueeze(1).broadcast_to([P, NSA_G, NCMP]))
            dve.wait_ge(piece_done, G["nsa_vw"].p1)
            norm("nsa")
            product("nsa_q")
            product("nsa_gl")
            product("nsa_zq")
            all_taken(dve, G["nsa_q"])
            rotate("nsa_q", [nsa_q[:, c, :] for c in range(NSA_H)])
            product("nsa_qm")
            product("nsa_zm")
            all_taken(dve, G["nsa_zm"])
            attention("nsa")
            attention("mem_b")
            product("nsa_out", residual(None))
            all_taken(dve, G["nsa_out"])
            norm("final2")
            for k in (1, 3):
                dve.wait_ge(turned, 8 + k + 1)
                v.tensor_copy(out_rows[:, k // 2, 1024:2048], tile_ps[1][:]).then_inc(turn_out[1], 1)


IN_NAMES = ("x", "c", "positions", "ada_w", "ada_b", "norm_mix_g", "w_in", "gla_gk_w", "gla_gk_b", "gla_onorm_g",
            "gla_wo", "mla_q_norm_g", "mla_wuq", "mla_kv_norm_g", "mla_wukv", "mla_wo", "w_out", "norm_ffn_g",
            "ffn_w_in", "ffn_w_down", "final_norm_g", "mem_2", "positions_2", "norm_g_2", "mem_norm_g_2",
            "w_mem_kv_2", "w_out_2", "a_w_in_2", "a_w_pool_2", "a_pool_scale_2", "b_w_in_2", "kv_norm_g_2",
            "w_kv_2", "cmp_pe_2", "cmp_w1_2", "cmp_w2_2", "final_g_2")


def kernel(**inputs):
    import concourse.bacc as bacc
    from concourse.bass_utils import run_bass_kernel_spmd

    nc = bacc.Bacc("TRN2", target_bir_lowering=False, num_devices=1)
    const, gla_const = constants()
    arrays = {"in_const": const, "in_gla_const": gla_const}
    for name in IN_NAMES:
        arrays[f"in_{name}"] = np.ascontiguousarray(inputs[name])
    A = {name[3:]: nc.dram_tensor(name, a.shape, mybir.dt.from_np(a.dtype), kind="ExternalInput").ap()
         for name, a in arrays.items()}
    out = nc.dram_tensor("out", (1, S, D), F32, kind="ExternalOutput").ap()
    program(nc, A, out)
    r = run_bass_kernel_spmd(nc, [arrays], core_ids=[0])
    return r.results[0]["out"]
```

```python
import math
from contextlib import ExitStack

import numpy as np

import concourse.bass as bass
from concourse import mybir

F32 = mybir.dt.float32
F32R = mybir.dt.float32r
I32 = mybir.dt.int32
ALU = mybir.AluOpType
ACT = mybir.ActivationFunctionType
AX = mybir.AxisListType

P = 128
S = 256
TT = S // P
D = 2048
DC = D // P
NT = 512
BLK = NT // P
EPS = 1e-6

GLA_H, GLA_DK, GLA_DV, RANK = 4, 256, 512, 16
LEVELS = 7
MLA_H, NOPE, ROPE, QR, KVR = 16, 128, 64, 512, 512
HALF_H = MLA_H // 2
FFN = 5632
FFN_PARTS = (6, 5)
MEM_H, HD = 4, 128
POOL_W, POOL_G, POOL_GC = 1536, 4, 384
NSA_H, NSA_G = 12, 4
CMP_LEN, CMP_STRIDE, CMP_HID = 32, 16, 256
NCMP = (S - CMP_LEN) // CMP_STRIDE + 1
NEG = -1e30

W_Q, W_K, W_V, W_G = 0, 1024, 2048, 4096
W_GK = 6144
W_CQ = W_GK + RANK
W_CKV = W_CQ + QR
W_KR = W_CKV + KVR
W_GA = W_KR + ROPE
W_GB = W_GA + D
B_Q, B_GL = 0, NSA_H * HD
B_ZQ = B_GL + 3 * NSA_H
B_QM = B_ZQ + NSA_H * HD
B_ZM = B_QM + MEM_H * HD

CONST = {}
_at = 0
for _n, _w in (("ident", P), ("ones", P), ("rot_mla", P), ("rot_nsa", P), ("causal", 2 * P),
               ("cmp_add", 2 * NCMP), ("cmp_mul", 2 * NCMP), ("freq_mla", 1), ("freq_nsa", 1),
               ("pool_head", POOL_G * 16)):
    CONST[_n] = (_at, _w)
    _at += _w
CONST_W = _at
GLA_SLOTS = LEVELS + 1
GLA_CONST_W = 3 * GLA_SLOTS * P

VECTORS = {}
_at = 0
for _n, _w in (("norm_mix_g", DC), ("ada_b", 6 * DC), ("gla_onorm_g", GLA_DV // P), ("mla_q_norm_g", QR // P),
               ("mla_kv_norm_g", KVR // P), ("norm_ffn_g", DC), ("final_norm_g", DC), ("norm_g_2", 2 * DC),
               ("mem_norm_g_2", 2 * DC), ("a_pool_scale_2", POOL_W // P), ("kv_norm_g_2", DC),
               ("final_g_2", DC), ("c", DC), ("cmp_pe_2", 2 * CMP_LEN)):
    VECTORS[_n] = (_at, _w)
    _at += _w
VEC_W = _at


def constants():
    t = np.arange(P)
    c = np.zeros((P, CONST_W), np.float32)

    def put(name, a):
        at, w = CONST[name]
        c[:, at:at + w] = a

    put("ident", np.eye(P))
    put("ones", 1.0)
    rot = np.zeros((P, P))
    for m in range(P):
        rot[(m + 32, m) if m % 64 < 32 else (m - 32, m)] = -1.0 if m % 64 < 32 else 1.0
    put("rot_mla", rot)
    rot = np.zeros((P, P))
    for m in range(32):
        rot[(m + 16, m) if m < 16 else (m - 16, m)] = -1.0 if m < 16 else 1.0
    put("rot_nsa", rot)
    put("causal", np.concatenate([np.zeros((P, P)), np.where(t[None, :] <= t[:, None], 0.0, NEG)], 1))
    ends = np.arange(NCMP) * CMP_STRIDE + CMP_LEN - 1
    seen = np.concatenate([ends[None, :] <= (t[:, None] + tt * P) for tt in range(TT)], 1)
    put("cmp_add", np.where(seen, 0.0, NEG))
    put("cmp_mul", seen)
    put("freq_mla", (10000.0 ** (-(t % 32) * 2.0 / ROPE))[:, None])
    put("freq_nsa", np.where(t < 32, 500000.0 ** (-(t % 16) * 2.0 / 32), 0.0)[:, None])
    head = [2.0 ** (g + 1) / np.minimum(np.arange(16) + 1, 2.0 ** (g + 1)) for g in range(POOL_G)]
    put("pool_head", np.concatenate(head)[None, :])

    g = np.zeros((P, 3, GLA_SLOTS, P), np.float32)
    s, i = np.meshgrid(t, t, indexing="ij")
    for l in range(LEVELS):
        m = 2 ** l
        mid = i // (2 * m) * (2 * m) + m
        right = i % (2 * m) >= m
        g[:, 0, l] = g[:, 1, l] = np.where(right, (s >= mid) & (s <= i), (s > i) & (s < mid)) / 16.0
        g[:, 2, l] = (s // (2 * m) == i // (2 * m)) & (s % (2 * m) < m) & right
    g[:, 0, LEVELS] = (s > i) / 16.0
    g[:, 1, LEVELS] = (s <= i) / 16.0
    g[:, 2, LEVELS] = s == i
    return c, g.reshape(P, GLA_CONST_W)


class Product:

    def __init__(self, name, tiles, kp, kc=4, width=NT, split=True, mode="T", dmas=1, rider=False,
                 used=None):
        self.name, self.tiles, self.kp, self.kc, self.width = name, tiles, kp, kc, width
        self.split, self.mode, self.dmas, self.rider = split, mode, dmas, rider
        self.used = used or width
        self.slots = kp * (2 if rider and mode != "A" else 1)
        for b in (2, 4):
            if (b * kp) % 4 == 0 and tiles % b == 0:
                break
        self.body, self.turns = (b, tiles // b) if tiles % b == 0 and (b * kp) % 4 == 0 and mode != "A" else (tiles, 1)


PRODUCTS = [Product("ada0", 2, 4, split=False, mode="A", rider=True),
            Product("mem_k0", 1, 4, rider=True), Product("mem_v0", 1, 4, mode="N", rider=True),
            Product("mem_k1", 1, 4), Product("mem_v1", 1, 4, mode="N", rider=True),
            Product("ada1", 3, 4, split=False, mode="A", rider=True),
            Product("gla_q", 2, 4), Product("gla_k", 2, 4), Product("gla_v", 4, 4, mode="N"),
            Product("gla_gk", 1, 1, kc=16, width=P),
            Product("gla_g", 4, 4, rider=True), Product("gate_a", 4, 4, rider=True),
            Product("gla_wo", 4, 4, rider=True),
            Product("mla_cq", 1, 4), Product("mla_ckv", 1, 4),
            Product("mla_kr", 1, 1, kc=16, width=P, dmas=2),
            Product("gate_b", 4, 4, rider=True)]
for _h in range(2):
    PRODUCTS += [Product(f"mla_qn{_h}", 2, 1, dmas=4), Product(f"mla_qr{_h}", 1, 1, dmas=4),
                 Product(f"mla_k{_h}", 2, 1, dmas=4), Product(f"mla_v{_h}", 2, 1, mode="N", dmas=4)]
PRODUCTS += [Product("mla_wo", 4, 4), Product("w_out", 4, 4)]
for _h, _n in enumerate(FFN_PARTS):
    PRODUCTS += [Product(f"ffn_in{_h}", 2 * _n, 4), Product(f"ffn_down{_h}", 4, _n)]
PRODUCTS += [Product("pool_u", 3, 4), Product("pool_zu", 3, 4), Product("pool_qm", 1, 4), Product("pool_zm", 1, 4),
             Product("pool_w", 4, 1, kc=3, width=POOL_GC), Product("pool_out", 4, 4),
             Product("nsa_kc", 1, 4), Product("nsa_vc", 1, 4),
             Product("nsa_ks", 1, 4), Product("nsa_vs", 1, 4, mode="N"),
             Product("nsa_kw", 1, 4), Product("nsa_vw", 1, 4, mode="N"),
             Product("cmp_k1", 1, 4, kc=8, width=CMP_HID, split=False),
             Product("cmp_k2", 1, 1, kc=2, width=HD, split=False),
             Product("cmp_v1", 1, 4, kc=8, width=CMP_HID, split=False),
             Product("cmp_v2", 1, 1, kc=2, width=HD, split=False, mode="C"),
             Product("nsa_q", 3, 4), Product("nsa_gl", 1, 1, kc=16, width=P, mode="N", used=3 * NSA_H),
             Product("nsa_zq", 3, 4), Product("nsa_qm", 1, 4), Product("nsa_zm", 1, 4),
             Product("nsa_out", 4, 4)]
AT_START = {0: -1, 1: -1, 2: 9, 3: 13}
CUT_IN_NORM = {"mem_k1": ("mem1", AT_START), "gla_q": ("mix", {0: 1, 1: 4, 2: 9, 3: 13}),
               "gla_g": ("gla", {0: -1, 1: -1}), "gate_b": ("cq", {0: -1, 1: -1}),
               "ffn_in0": ("ffn", AT_START), "pool_u": ("pool", AT_START), "nsa_kc": ("kv", AT_START)}
G = {}
LANDED = []
KIND = []
BEFORE = {"split": [0], "plain": [0], "ada": [0]}
_in_slot = [0] * 4
_p = _s = _t = _a = 0
for _i, _g in enumerate(PRODUCTS):
    _g.r0, _g.p0, _g.s0, _g.t0, _g.a0 = len(LANDED), _p, _s, _t, _a
    for _k in range(_g.tiles * _g.slots):
        _ada = _g.mode == "A" or (_g.rider and _k % 2 == 1)
        _in_slot[len(LANDED) % 4] += 16 * (1 if _ada else _g.dmas)
        LANDED.append(_in_slot[len(LANDED) % 4])
        KIND.append("ada" if _ada else "split" if _g.split else "plain")
        for _kind, _is in (("split", _g.split and not _ada), ("plain", not _ada), ("ada", _ada)):
            BEFORE[_kind].append(BEFORE[_kind][-1] + _is)
    if _g.mode != "A":
        _p += _g.tiles * _g.kp
        _s += _g.tiles * _g.kp * _g.split
        _t += _g.tiles
    _a += _g.tiles * _g.rider
    _g.p1, _g.t1 = _p, _t
    _next = PRODUCTS[_i + 1] if _i + 1 < len(PRODUCTS) else None
    _g.ahead = bool(_g.split and _next and _next.split and (_g.turns == 1 or _next.dmas == 1))
    _g.first_ahead = _i > 0 and PRODUCTS[_i - 1].ahead
    _g.precut = len(CUT_IN_NORM[_g.name][1]) if _g.name in CUT_IN_NORM else int(_g.first_ahead)
    G[_g.name] = _g
ADA_TILES = _a


class Norm:

    def __init__(self, name, n, split=True, sums="pairs"):
        self.name, self.n, self.split, self.sums = name, n, split, sums


NORMS = [Norm("mem0", DC), Norm("mem1", DC, sums="shared"), Norm("mix", DC), Norm("gla", DC, split=False, sums="heads"),
         Norm("cq", QR // P), Norm("ckv", KVR // P), Norm("ffn", DC, sums="tiles"),
         Norm("final1", DC, split=False, sums="tiles"), Norm("pool", DC), Norm("kv", DC, sums="tiles"),
         Norm("nsa", DC, sums="shared"), Norm("final2", DC, split=False, sums="tiles")]
N = {}
_a = _c = _k = _m = _pt = _pl = 0
for _g in NORMS:
    _g.k, _g.a0, _g.m0, _g.part0, _g.c0, _g.plain0 = _k, _a, _m, _pt, _c, _pl
    _k += _g.sums != "shared"
    _a += {"pairs": _g.n // 2, "tiles": 4, "shared": 0, "heads": GLA_H}[_g.sums]
    _m += {"pairs": _g.n // 2, "tiles": 1, "shared": 0, "heads": 1}[_g.sums]
    _pt += 3 * (_g.sums == "tiles")
    _c += _g.n * _g.split
    _pl += _g.n * (not _g.split)
    N[_g.name] = _g

ROPES = [("mla_kr", 1), ("mla_q0", BLK), ("mla_q1", BLK), ("nsa_ks", BLK), ("nsa_kw", BLK), ("cmp_k", 1), ("nsa_q", NSA_H)]
ROPE0 = {}
_a = 0
for _n, _w in ROPES:
    ROPE0[_n] = _a
    _a += _w


STEPS = {"gla_g": 2, "mla_wo": 3, "w_out": 1, "ffn_in0": 2, "ffn_down0": 1, "ffn_in1": 2, "ffn_down1": 1, "pool_w": 3}
STEP0 = {}
_a = 0
for _g in PRODUCTS:
    if _g.name in STEPS:
        STEP0[_g.name] = _a
        _a += STEPS[_g.name] * (_g.tiles // 2 if _g.name.startswith("ffn_in") else _g.tiles)

N_VEC_DMA = sum((a + w - 1) // P - a // P + 1 for a, w in VECTORS.values())
TURNS_BEFORE_OUT = 4


class Steps:

    def __init__(self, eng, sem):
        self.eng, self.sem, self.n = eng, sem, 0

    def wait(self, ins):
        self.n += 1
        ins.then_inc(self.sem, 1)
        self.eng.wait_ge(self.sem, self.n)


def program(nc, A, out):
    with ExitStack() as ctx:
        def sem(name):
            return ctx.enter_context(nc.semaphore(name))

        base = (nc.sbuf_base + 63) // 64 * 64
        arena = ctx.enter_context(nc.sbuf_tensor("arena", [P, (nc.sbuf_usable_end - base - 64) // 4], F32))
        KB = 1024
        RAW, WHI, WLO, XB, HB, OB, BIG, SMALL = (k * KB for k in (0, 32, 48, 64, 80, 112, 144, 192))

        def at(name, off, shape, dt=F32):
            return nc.alloc_sbuf_tensor_at(name, shape, dt, offset=base + off)

        w_raw = [at(f"w_raw{i}", RAW + 8 * KB * i, [P, 2048]) for i in range(4)]
        w_hi = [at(f"w_hi{i}", WHI + 8 * KB * i, [P, 2048], F32R) for i in range(2)]
        w_lo = [at(f"w_lo{i}", WLO + 8 * KB * i, [P, 2048], F32R) for i in range(2)]
        x = at("x", XB, [P, DC, S])
        h_hi = at("h_hi", HB, [P, DC, S], F32R)
        h_lo = at("h_lo", HB + 16 * KB, [P, DC, S], F32R)
        o_hi = at("o_hi", OB, [P, DC, S], F32R)
        o_lo = at("o_lo", OB + 16 * KB, [P, DC, S], F32R)
        x_rows = at("x_rows", OB, [P, TT, D])
        mem_rows = at("mem_rows", OB + 16 * KB, [P, TT, D])
        mem_t = at("mem_t", BIG, [P, DC, S])
        mem_k_out = at("mem_k_out", BIG + 16 * KB, [P, 2, BLK, S])
        mem_v_out = at("mem_v_out", BIG + 24 * KB, [P, 2, TT, NT])
        vec_rows = at("vec_rows", BIG + 32 * KB, [P, 3, P])
        nscratch_b = at("nscratch_b", BIG + 40 * KB, [P, 2, 2 * S])
        ntmp_b = at("ntmp_b", BIG + 44 * KB, [P, 2, S])
        rstd_mix = at("rstd_mix", BIG + 46 * KB, [P, S])
        mem_hi = at("mem_hi", OB, [P, DC, S], F32R)
        mem_lo = at("mem_lo", OB + 16 * KB, [P, DC, S], F32R)
        qk = at("qk", BIG, [P, GLA_H, 4, S])
        gla_v = at("gla_v", BIG + 16 * KB, [P, TT, D])
        log_a = at("log_a", BIG + 32 * KB, [P, TT, GLA_H * GLA_DK])
        gla_const = at("gla_const", OB, [P, 3, GLA_SLOTS, P])
        q_lev = at("q_lev", OB + 12 * KB, [P, 2, GLA_SLOTS, P])
        k_lev = at("k_lev", OB + 20 * KB, [P, 2, GLA_SLOTS, P])
        gk_w = at("gk_w", OB + 12 * KB, [RANK, GLA_H * GLA_DK])
        gk_b = at("gk_b", OB + 20 * KB, [1, GLA_H * GLA_DK])
        decay = [at("decay0", OB + 28 * KB, [P, GLA_SLOTS, P]), at("decay1", BIG + 40 * KB, [P, GLA_SLOTS, P])]
        gla_att = at("gla_att", BIG + 44 * KB, [P, 3, P])
        k_across = at("k_across", BIG + 44 * KB + 1536, [P, 2, P])
        gk_t = at("gk_t", BIG + 46 * KB + 512, [P, S])
        gla_sq = at("gla_sq", OB + 12 * KB, [P, GLA_H, BLK * S])
        gla_var = at("gla_var", OB, [P, GLA_H, S])
        gla_tmp = at("gla_tmp", BIG + 40 * KB, [P, 2, BLK * S])
        merged = at("merged", BIG + 16 * KB, [P, DC, S])
        gate_b = at("gate_b", BIG, [P, DC, S])
        cq = at("cq", OB, [P, BLK, S])
        ckv = at("ckv", OB + 4 * KB, [P, BLK, S])
        cq_hi = at("cq_hi", BIG + 32 * KB, [P, BLK, S], F32R)
        cq_lo = at("cq_lo", BIG + 36 * KB, [P, BLK, S], F32R)
        ckv_hi = at("ckv_hi", BIG + 40 * KB, [P, BLK, S], F32R)
        ckv_lo = at("ckv_lo", BIG + 44 * KB, [P, BLK, S], F32R)
        mla_q = at("mla_q", HB, [P, HALF_H, S])
        mla_k = at("mla_k", HB + 8 * KB, [P, HALF_H, S])
        mla_qr = at("mla_qr", HB + 16 * KB, [P, BLK, S])
        mla_v = at("mla_v", HB + 20 * KB, [P, TT, HALF_H * P])
        probs = at("probs", HB + 28 * KB, [P, 2, 2 * S])
        mla_tmp = at("mla_tmp", BIG + 32 * KB, [P, BLK * S])
        nscratch_o = at("nscratch_o", OB + 8 * KB, [P, 2, 2 * S])
        ntmp_o = at("ntmp_o", OB + 12 * KB, [P, 2, S])
        sq_o, sq_h = at("sq_o", OB + 16 * KB, [P, DC, S]), at("sq_h", HB, [P, DC, S])
        part_o, part_h = at("part_o", OB + 8 * KB, [P, 3, S]), at("part_h", HB + 16 * KB, [P, 3, S])
        o_tmp = at("o_tmp", OB, [P, 2, BLK * S])
        h_tmp = at("h_tmp", HB, [P, BLK * S])
        sw_hi = at("sw_hi", BIG, [P, 24, S], F32R)
        sw_lo = at("sw_lo", BIG + 24 * KB, [P, 24, S], F32R)
        u_t = at("u_t", BIG, [P, 12, S])
        pool_hi = at("pool_hi", BIG + 12 * KB, [P, 12, S], F32R)
        pool_lo = at("pool_lo", BIG + 24 * KB, [P, 12, S], F32R)
        silu_z = at("silu_z", BIG + 36 * KB, [P, 12, S])
        run_a = at("run_a", OB, [P, 12, S])
        run_b = at("run_b", OB + 12 * KB, [P, 12, S])
        mem_q = at("mem_q", BIG, [P, MEM_H, S])
        mem_z = at("mem_z", BIG + 4 * KB, [P, MEM_H, S])
        pool_tmp = at("pool_tmp", BIG + 8 * KB, [P, 3 * S])
        mem_k = at("mem_k", HB + 8 * KB, [P, MEM_H, S])
        mem_v = at("mem_v", HB + 12 * KB, [P, TT, NT])
        kc = at("kc", BIG, [P, NSA_G, S])
        vc = at("vc", BIG + 4 * KB, [P, NSA_G, S])
        ks = at("ks", BIG + 8 * KB, [P, NSA_G, S])
        vs = at("vs", BIG + 12 * KB, [P, TT, NT])
        kw = at("kw", BIG + 16 * KB, [P, NSA_G, S])
        vw = at("vw", BIG + 20 * KB, [P, TT, NT])
        nsa_q = at("nsa_q", BIG + 24 * KB, [P, NSA_H, S])
        z_pe = at("z_pe", OB, [P, CMP_LEN, NSA_G * NCMP])
        hidden = at("hidden", OB + 8 * KB, [P, 2, NSA_G * NCMP])
        k_cmp = at("k_cmp", OB + 16 * KB + 13 * KB, [P, NSA_G * NCMP])
        v_cmp = at("v_cmp", OB + 16 * KB + 14 * KB, [NCMP, NSA_G * HD])
        out_rows = at("out_rows", BIG, [P, TT, D])
        small = [SMALL]

        def keep(name, shape, dt=F32):
            off = small[0]
            small[0] += (4 * int(np.prod(shape[1:])) + 31) // 32 * 32
            assert base + small[0] <= nc.sbuf_usable_end, small[0]
            return at(name, off, shape, dt)

        const = keep("const", [P, CONST_W])
        cols = keep("cols", [P, VEC_W])
        mod = keep("mod", [P, 6 * DC])
        gain_eff = keep("gain_eff", [P, 2, DC])
        c_act = keep("c_act", [P, DC])
        rope_cos = keep("rope_cos", [P, S])
        rope_sin = keep("rope_sin", [P, S])
        rstd = keep("rstd", [P, S])
        var = keep("var", [P, S])
        probs_t = keep("probs_t", [P, 2, 2 * TT * P])
        angles = at("angles", small[0] - 4 * KB, [P, 3, S])
        stats = keep("stats", [P, 20])
        ada_acc = [probs_t[:, i, :] for i in range(2)]
        gates = keep("gates", [P, TT, 3 * NSA_H])
        k_rope = keep("k_rope", [P, S])
        assert small[0] <= (nc.sbuf_usable_end - base), small

        tile_ps = [ctx.enter_context(nc.psum_tensor(f"tile_ps{i}", [P, 1024], F32)) for i in range(2)]
        misc_ps = [ctx.enter_context(nc.psum_tensor(f"misc_ps{i}", [P, 1024], F32)) for i in range(2)]
        bank = [misc_ps[i // 2][:, (i % 2) * 512:(i % 2 + 1) * 512] for i in range(4)]

        def cst(name):
            a, w = CONST[name]
            return const[:, a:a + w]

        def vec(name, i=0, n=1):
            a, _ = VECTORS[name]
            return cols[:, a + i:a + i + n]

        ident, ones = cst("ident"), cst("ones")
        half_pi = stats[:, 16:17]

        b_scr, o_scr = (nscratch_b, ntmp_b), (nscratch_o, ntmp_o)
        H_OUT = (h_hi, h_lo)
        SCRATCH, SOURCE, DEST, GAIN = {}, {}, {}, {}
        SHIFT = {"mix": mod[:, 0:DC], "ffn": mod[:, 3 * DC:4 * DC]}
        RSTD = {"mix": rstd_mix}
        SQUARES = {"ffn": (sq_o, part_o), "final1": (sq_o, part_o), "kv": (sq_h, part_h), "final2": (sq_h, part_h)}
        for name_, scr, src_, dst_, gain_ in (
                ("mem0", b_scr, mem_t[:], H_OUT, vec("mem_norm_g_2", 0, DC)),
                ("mem1", b_scr, mem_t[:], (mem_hi, mem_lo), vec("mem_norm_g_2", DC, DC)),
                ("mix", b_scr, x[:], H_OUT, gain_eff[:, 0, :]),
                ("cq", o_scr, cq[:], (cq_hi, cq_lo), vec("mla_q_norm_g", 0, 4)),
                ("ckv", o_scr, ckv[:], (ckv_hi, ckv_lo), vec("mla_kv_norm_g", 0, 4)),
                ("ffn", o_scr, x[:], H_OUT, gain_eff[:, 1, :]),
                ("final1", o_scr, x[:], (x,), vec("final_norm_g", 0, DC)),
                ("pool", o_scr, x[:], H_OUT, vec("norm_g_2", 0, DC)),
                ("kv", o_scr, x[:], H_OUT, vec("kv_norm_g_2", 0, DC)),
                ("nsa", o_scr, x[:], H_OUT, vec("norm_g_2", DC, DC)),
                ("final2", o_scr, x[:], (x,), vec("final_g_2", 0, DC))):
            SCRATCH[name_], DEST[name_], GAIN[name_] = scr, dst_, gain_
            SOURCE[name_] = lambda c, t=src_: t[:, c, :]
        mem_store = [nc.dram_tensor(f"mem_store{i}", (P, 2, 1024), F32, kind="Internal").ap() for i in range(2)]

        landed = [sem(f"landed{i}") for i in range(4)]
        cut_hi = sem("cut_hi")
        cut_lo = sem("cut_lo")
        piece_done = sem("piece_done")
        taken = [sem(f"taken{i}") for i in range(2)]
        silu_ready = sem("silu_ready")
        ada_step = sem("ada_step")
        ada_done = sem("ada_done")
        ada_sum = sem("ada_sum")
        tile_step = sem("tile_step")
        act_step, dve_step = sem("act_step"), sem("dve_step")
        ld_const, ld_vec, ld_x, ld_mem = sem("ld_const"), sem("ld_vec"), sem("ld_x"), sem("ld_mem")
        ld_pos, ld_gla, ld_gk = sem("ld_pos"), sem("ld_gla"), sem("ld_gk")
        ld_mkv, st_mkv, st_out = sem("ld_mkv"), sem("st_mkv"), sem("st_out")
        vec_turned, vec_ready, c_ready = sem("vec_turned"), sem("vec_ready"), sem("c_ready")
        turned = sem("turned")
        turn_out = [sem(f"turn_out{i}") for i in range(2)]
        nm_sq, nm_acc, nm_var, nm_std = sem("nm_sq"), sem("nm_acc"), sem("nm_var"), sem("nm_std")
        nm_part = sem("nm_part")
        nm_t, nm_hi, nm_lo, nm_plain = sem("nm_t"), sem("nm_hi"), sem("nm_lo"), sem("nm_plain")
        tab_arg, tab_ready = sem("tab_arg"), sem("tab_ready")
        rp_rot, rp_done = sem("rp_rot"), sem("rp_done")
        z_ready, z_abs, la_ready = sem("z_ready"), sem("z_abs"), sem("la_ready")
        gl_e, gl_ex, gl_qk, gl_att = sem("gl_e"), sem("gl_ex"), sem("gl_qk"), sem("gl_att")
        gl_red, gl_o, gl_out = sem("gl_red"), sem("gl_o"), sem("gl_out")
        at_s, at_masked, at_max, at_exp = sem("at_s"), sem("at_masked"), sem("at_max"), sem("at_exp")
        at_p, at_t, at_pt, at_o, at_fin = (sem(f"at_{n}") for n in ("p", "t", "pt", "o", "fin"))
        pl_t, pl_hi, pl_lo = sem("pl_t"), sem("pl_hi"), sem("pl_lo")
        zp_ready = sem("zp_ready")

        def rows(w, chunks=None):
            return w.rearrange("(c p) n -> p c n", p=P)

        w_in = rows(A["w_in"][0])
        ada_w, w_out = rows(A["ada_w"][0]), rows(A["w_out"][0])
        gla_wo, mla_wo = rows(A["gla_wo"][0]), rows(A["mla_wo"][0])
        wuq = A["mla_wuq"][0].rearrange("(c p) (h e) -> p c h e", p=P, e=NOPE + ROPE)
        wukv = A["mla_wukv"][0].rearrange("(c p) (h e) -> p c h e", p=P, e=2 * P)
        ffn_in, ffn_down = rows(A["ffn_w_in"][0]), rows(A["ffn_w_down"][0])
        mem_kv = [rows(A["w_mem_kv_2"][i]) for i in range(2)]
        out_2 = [rows(A["w_out_2"][i]) for i in range(2)]
        a_in, b_in, w_kv = rows(A["a_w_in_2"][0]), rows(A["b_w_in_2"][0]), rows(A["w_kv_2"])

        def plain(w, col):
            return lambda i, tb, g, q: (w[:, g.kc * q:g.kc * (q + 1), bass.ds(i * (g.body * NT) + col + tb * NT, NT)]
                                        if g.turns > 1 else w[:, g.kc * q:g.kc * (q + 1), col + tb * NT:col + tb * NT + NT])

        def ffn_cols(part):
            first = sum(FFN_PARTS[:part]) * NT
            return lambda i, tb, g, q: ffn_in[:, 4 * q:4 * q + 4,
                                              bass.ds(i * (g.body // 2 * NT) + first + tb // 2 * NT + tb % 2 * FFN, NT)]

        def ffn_rows(part):
            c0 = sum(FFN_PARTS[:part]) * BLK

            def src(i, tb, g, q):
                cs = slice(c0 + 4 * q, c0 + 4 * q + 4)
                if g.turns > 1:
                    return ffn_down[:, cs, bass.ds(i * (g.body * NT) + tb * NT, NT)]
                return ffn_down[:, cs, tb * NT:tb * NT + NT]
            return src

        SRC = {"mem_k0": plain(mem_kv[0], 0), "mem_v0": plain(mem_kv[0], NT),
               "mem_k1": plain(mem_kv[1], 0), "mem_v1": plain(mem_kv[1], NT),
               "gla_q": plain(w_in, W_Q), "gla_k": plain(w_in, W_K),
               "gla_v": plain(w_in, W_V), "gla_g": plain(w_in, W_G), "gate_a": plain(w_in, W_GA),
               "gla_gk": lambda i, tb, g, q: w_in[:, :, W_GK:W_GK + P],
               "gla_wo": plain(gla_wo, 0), "mla_cq": plain(w_in, W_CQ), "mla_ckv": plain(w_in, W_CKV),
               "mla_kr": lambda i, tb, g, q: w_in[:, :, W_KR:W_KR + ROPE],
               "gate_b": plain(w_in, W_GB), "mla_wo": plain(mla_wo, 0), "w_out": plain(w_out, 0),
               "pool_u": plain(a_in, 0), "pool_zu": plain(a_in, POOL_W), "pool_qm": plain(a_in, 2 * POOL_W),
               "pool_zm": plain(a_in, 2 * POOL_W + MEM_H * HD),
               "pool_w": lambda i, tb, g, q: rows(A["a_w_pool_2"][0, tb]),
               "pool_out": plain(out_2[0], 0), "nsa_out": plain(out_2[1], 0),
               "cmp_k1": lambda i, tb, g, q: rows(A["cmp_w1_2"][0])[:, 8 * q:8 * q + 8],
               "cmp_v1": lambda i, tb, g, q: rows(A["cmp_w1_2"][1])[:, 8 * q:8 * q + 8],
               "cmp_k2": lambda i, tb, g, q: rows(A["cmp_w2_2"][0]),
               "cmp_v2": lambda i, tb, g, q: rows(A["cmp_w2_2"][1]),
               "nsa_q": plain(b_in, B_Q), "nsa_zq": plain(b_in, B_ZQ), "nsa_qm": plain(b_in, B_QM),
               "nsa_zm": plain(b_in, B_ZM), "nsa_gl": lambda i, tb, g, q: b_in[:, :, B_GL:B_GL + P]}
        for n_, name in enumerate(("nsa_kc", "nsa_vc", "nsa_ks", "nsa_vs", "nsa_kw", "nsa_vw")):
            SRC[name] = plain(w_kv, n_ * NT)
        for hf in range(2):
            h0 = hf * HALF_H
            SRC[f"mla_qn{hf}"] = lambda i, tb, g, q, h0=h0: wuq[:, :, h0 + 4 * tb:h0 + 4 * tb + 4, 0:NOPE]
            SRC[f"mla_qr{hf}"] = lambda i, tb, g, q, h0=h0: wuq[:, :, h0:h0 + 8, NOPE:NOPE + ROPE]
            SRC[f"mla_k{hf}"] = lambda i, tb, g, q, h0=h0: wukv[:, :, h0 + 4 * tb:h0 + 4 * tb + 4, 0:P]
            SRC[f"mla_v{hf}"] = lambda i, tb, g, q, h0=h0: wukv[:, :, h0 + 4 * tb:h0 + 4 * tb + 4, P:2 * P]
            SRC[f"ffn_in{hf}"] = ffn_cols(hf)
            SRC[f"ffn_down{hf}"] = ffn_rows(hf)

        def turns(eng, g, peel_last=False, peel_first=False, flat=False):
            n = g.turns - 1 if peel_last else g.turns
            if g.turns == 1 or flat:
                for i in range(g.turns):
                    yield i, i == g.turns - 1
                return
            if peel_first:
                yield 0, False
            with eng.Fori(int(peel_first), n) as i:
                yield i, not peel_last
            if peel_last:
                yield g.turns - 1, True

        def per(i, n):
            return 0 if isinstance(i, int) and i == 0 else i * n

        def all_taken(eng, g):
            for b in range(2):
                n = (g.t1 - b + 1) // 2
                if n:
                    eng.wait_ge(taken[b], n)

        def tile_is_done(eng, g, i, tb):
            eng.wait_ge(piece_done, g.p0 + (tb + 1) * g.kp + per(i, g.body * g.kp))

        def last_taken(eng, g, i, tb):
            t = g.t0 + tb - 1
            eng.wait_ge(taken[t % 2], t // 2 + 1 + per(i, g.body // 2))

        def ring(g, tb, q):
            return g.r0 + tb * g.slots + q * (g.slots // g.kp)

        def ring_ada(g, tb, q):
            return ring(g, tb, q) + (g.mode != "A")

        def psum_tile(g, tb):
            return tile_ps[(g.t0 + tb) % 2], taken[(g.t0 + tb) % 2]

        def pair_unit(h, tt, nk, scores, v, apart=1, **rest):
            unit = dict(nk=nk, scale=HD ** -0.5, add=None, mul=None, gate=None, z=None, first=True, last=True,
                        q=slice(tt * P, tt * P + P), apart=apart,
                        scores=[scores(h + e * apart) for e in range(2)], v=[v(h + e * apart) for e in range(2)])
            unit.update(rest)
            return unit

        def mla_units(hf):
            def unit(h, tt):
                q, nk = slice(tt * P, tt * P + P), (tt + 1) * P

                def scores(h):
                    r = slice(64 * (h % 2), 64 * (h % 2) + 64)
                    return [(mla_q[:, h, q], mla_k[:, h, 0:nk]), (mla_qr[r, h // 2, q], k_rope[r, 0:nk])]
                return pair_unit(h, tt, nk, scores, lambda h: [mla_v[:, j, h * P:(h + 1) * P] for j in range(tt + 1)],
                                 scale=(NOPE + ROPE) ** -0.5, add=cst("causal")[:, 2 * P - nk:2 * P],
                                 apart=2, chunk=hf * HALF_H + h)
            return [unit(h, tt) for h in range(HALF_H) if h % 4 < 2 for tt in range(TT)]

        def mem_units():
            def unit(h, tt):
                q = slice(tt * P, tt * P + P)
                return pair_unit(h, tt, S, lambda h: [(mem_q[:, h, q], mem_k[:, h, :])],
                                 lambda h: [mem_v[:, j, h * P:(h + 1) * P] for j in range(TT)],
                                 chunk=12 + h, z=mem_z[:, h:h + 2, q])
            return [unit(h, tt) for h in range(0, MEM_H, 2) for tt in range(TT)]

        def nsa_units():
            units = []
            group = lambda h: h // (NSA_H // NSA_G)
            gv = lambda h: slice(group(h) * HD, (group(h) + 1) * HD)
            for h in range(0, NSA_H, 2):
                for tt in range(TT):
                    q, nk = slice(tt * P, tt * P + P), (tt + 1) * P
                    gate = lambda b: gates[:, tt, 3 * h + b:3 * h + b + 4:3]
                    rest = dict(chunk=h, z=silu_z[:, h:h + 2, q])
                    at_ = slice(tt * NCMP, (tt + 1) * NCMP)
                    units.append(pair_unit(
                        h, tt, NCMP, lambda h: [(nsa_q[:, h, q], k_cmp[:, group(h) * NCMP:(group(h) + 1) * NCMP])],
                        lambda h: [v_cmp[:, gv(h)]], add=cst("cmp_add")[:, at_], mul=cst("cmp_mul")[:, at_],
                        gate=gate(0), last=False, **rest))
                    for b, (k, v) in enumerate(((ks, vs), (kw, vw))):
                        units.append(pair_unit(
                            h, tt, nk, lambda h: [(nsa_q[:, h, q], k[:, group(h), 0:nk])],
                            lambda h: [v[:, j, gv(h)] for j in range(tt + 1)],
                            add=cst("causal")[:, 2 * P - nk:2 * P], gate=gate(1 + b), first=False, last=b == 1, **rest))
            return units

        UNITS = {"mla0": mla_units(0), "mla1": mla_units(1), "mem_a": mem_units(), "nsa": nsa_units(),
                 "mem_b": mem_units()}
        U0, FIN0 = {}, {}
        n_u = n_f = 0
        for name, us in UNITS.items():
            U0[name], FIN0[name] = n_u, n_f
            n_u += len(us)
            n_f += sum(u["last"] for u in us)
            UNITS[name] = us

        block = ctx.enter_context(nc.Block())

        @block.sync
        def _(sp):
            x_in, mem_in = A["x"][0], A["mem_2"][0]
            sp.dma_start(const[:], A["const"]).then_inc(ld_const, 16)
            n_vec = 0
            for name, (at0, w) in VECTORS.items():
                v = A[name]
                v = v.rearrange(" ".join(f"a{k}" for k in range(len(v.shape))) + " -> (" +
                                " ".join(f"a{k}" for k in range(len(v.shape))) + ")") if len(v.shape) > 1 else v
                v = v.rearrange("(r p) -> r p", p=P)
                done = 0
                while done < w:
                    r, t = (at0 + done) % P, (at0 + done) // P
                    n = min(P - r, w - done)
                    sp.dma_start(vec_rows[r:r + n, t, :], v[done:done + n]).then_inc(ld_vec, 16)
                    n_vec += 1
                    done += n
            assert n_vec == N_VEC_DMA
            sp.dma_start(mem_rows[:], mem_in.rearrange("(t p) d -> p t d", p=P)).then_inc(ld_mem, 16)
            sp.dma_start(x_rows[:], x_in.rearrange("(t p) d -> p t d", p=P)).then_inc(ld_x, 16)

            def free_slot(g, i, r):
                for kind, s_, n in (("split", cut_lo, g.body * g.kp * g.split),
                                    ("plain", piece_done, g.body * g.kp), ("ada", ada_done, g.body * g.kp * g.rider)):
                    r1 = r + g.body * g.slots
                    now = r >= 4 and KIND[r - 4] == kind
                    later = g.turns > 1 and KIND[r1 - 4] == kind
                    if later:
                        sp.wait_ge(s_, max(BEFORE[kind][r - 3] * now, BEFORE[kind][r1 - 3] - n) + per(i, n))
                    elif now:
                        sp.wait_ge(s_, BEFORE[kind][r - 3])

            def load_ada(g, i, tb, q):
                r = ring_ada(g, tb, q)
                col = bass.ds(per(i, g.body * NT) + (g.a0 + tb) * NT, NT)
                sp.dma_start(w_raw[r % 4][:].rearrange("p (c n) -> p c n", c=4),
                             ada_w[:, 4 * q:4 * q + 4, col]).then_inc(landed[r % 4], 16)

            def load(name):
                g = G[name]
                for i, _ in turns(sp, g):
                    for tb in range(g.body):
                        for q in range(g.kp):
                            free_slot(g, i, ring(g, tb, q))
                            if g.mode == "A":
                                load_ada(g, i, tb, q)
                                continue
                            slot = ring(g, tb, q) % 4
                            src = SRC[name](i, tb, g, q)
                            dst = w_raw[slot][:, 0:g.kc * g.width].rearrange("p (c n) -> p c n", c=g.kc)
                            parts = [(dst, src)]
                            if len(src.shape) == 4:
                                dst = dst.rearrange("p c (h e) -> p c h e", h=src.shape[2])
                                parts = [(dst[:, c], src[:, c]) for c in range(g.kc)]
                            elif name == "mla_kr":
                                parts = [(dst[:, :, k * ROPE:(k + 1) * ROPE], src) for k in range(2)]
                            assert len(parts) == g.dmas
                            for d_, s_ in parts:
                                sp.dma_start(d_, s_).then_inc(landed[slot], 16)
                            if g.rider:
                                free_slot(g, i, ring(g, tb, q) + 1)
                                load_ada(g, i, tb, q)

            def mem_kv_load(i, name, after):
                sp.wait_ge(piece_done, G[after].p1)
                if i == 0:
                    sp.wait_ge(st_mkv, 64)
                sp.dma_start(mem_k[:].rearrange("p h n -> p (h n)"), mem_store[i][:, 0]).then_inc(ld_mkv, 16)
                sp.dma_start(mem_v[:].rearrange("p t n -> p (t n)"), mem_store[i][:, 1]).then_inc(ld_mkv, 16)

            for name in ("ada0", "mem_k0", "mem_v0", "mem_k1", "mem_v1", "ada1"):
                load(name)
            load("gla_q")
            load("gla_k")
            load("gla_v")
            load("gla_gk")
            sp.wait_ge(nm_lo, N["mix"].c0 + DC)
            sp.dma_start(gla_const[:].rearrange("p a b c -> p (a b c)"), A["gla_const"]).then_inc(ld_gla, 16)
            sp.dma_start(gk_w[:], A["gla_gk_w"][0]).then_inc(ld_gk, 16)
            sp.dma_start(gk_b[:], A["gla_gk_b"]).then_inc(ld_gk, 16)
            for name in ("gla_g", "gate_a", "gla_wo", "mla_cq", "mla_ckv", "mla_kr", "gate_b"):
                load(name)
            for hf in range(2):
                for name in ("mla_qn", "mla_qr", "mla_k", "mla_v"):
                    load(f"{name}{hf}")
            for name in ("mla_wo", "w_out", "ffn_in0", "ffn_down0", "ffn_in1", "ffn_down1",
                         "pool_u", "pool_zu", "pool_qm", "pool_zm"):
                load(name)
            load("pool_w")
            mem_kv_load(0, "mem_a", "pool_zm")
            for name in ("pool_out", "nsa_kc", "nsa_vc", "nsa_ks", "nsa_vs", "nsa_kw", "nsa_vw",
                         "cmp_k1", "cmp_k2", "cmp_v1", "cmp_v2", "nsa_q", "nsa_gl", "nsa_zq", "nsa_qm", "nsa_zm"):
                load(name)
            mem_kv_load(1, "mem_b", "nsa_zm")
            load("nsa_out")
            for tt in range(TT):
                for b in range(2):
                    sp.wait_ge(turn_out[b], TURNS_BEFORE_OUT + tt + 1)
                sp.dma_start(out[0, tt * P:(tt + 1) * P, :], out_rows[:, tt]).then_inc(st_out, 16)
            sp.wait_ge(st_out, 32)
            sp.wait_ge(st_mkv, 64)

        @block.gpsimd
        def _(pool):
            for i, name in enumerate(("positions", "positions_2")):
                if i:
                    all_taken(pool, G["mem_v1"])
                    for j in range(2):
                        pool.dma_start(mem_store[j][:, 0], mem_k_out[:, j].rearrange("p h n -> p (h n)")).then_inc(st_mkv, 16)
                        pool.dma_start(mem_store[j][:, 1], mem_v_out[:, j].rearrange("p t n -> p (t n)")).then_inc(st_mkv, 16)
                    pool.wait_ge(at_o, U0["mem_a"] + len(UNITS["mem_a"]))
                pool.dma_start(angles[:, 2, :].bitcast(I32), A[name].broadcast_to([P, S])).then_inc(ld_pos, 16)

        @block.tensor
        def _(pe):
            def mm(o, l, r, start, stop):
                return nc.tensor.matmul(o, l, r, start=start, stop=stop, skip_group_check=True)

            def product(name, x_hi, x_lo=None, ready=(), chunk_ready=None):
                g = G[name]
                for s_, v_ in ready:
                    pe.wait_ge(s_, v_)
                for i, _ in turns(pe, g):
                    for tb in range(g.body):
                        ps, tk = psum_tile(g, tb)
                        use = (g.t0 + tb) // 2
                        if use:
                            pe.wait_ge(tk, use + per(i, g.body // 2))
                        for q in range(g.kp):
                            p = g.p0 + tb * g.kp + q
                            if g.split:
                                s_ = g.s0 + tb * g.kp + q
                                pe.wait_ge(cut_lo, s_ + 1 + per(i, g.body * g.kp))
                                slots = [w_hi[s_ % 2], w_lo[s_ % 2]]
                                passes = [(0, x_hi), (1, x_hi), (0, x_lo)]
                            else:
                                r = ring(g, tb, q)
                                pe.wait_ge(landed[r % 4], LANDED[r] + per(i, 16 * g.body * g.slots // 4))
                                slots, passes = [w_raw[r % 4]], [(0, x_hi)] + ([(0, x_lo)] if x_lo else [])
                            w = [t[:, 0:g.kc * g.width].rearrange("p (c n) -> p c n", c=g.kc) for t in slots]
                            for c in range(g.kc):
                                k = q * g.kc + c
                                begin, end = k == 0, k == g.kp * g.kc - 1
                                if tb == 0 and chunk_ready:
                                    for s_, v_ in chunk_ready(k):
                                        pe.wait_ge(s_, v_)
                                for a, (wi, xx) in enumerate(passes):
                                    first, final = begin and a == 0, end and a == len(passes) - 1
                                    xk = xx(tb, k)
                                    if g.mode == "T":
                                        n = xk.shape[-1]
                                        pad = 1 if n == 1 else S
                                        for b in range((g.width + P - 1) // P):
                                            m = min(P, g.width - b * P)
                                            last = mm(ps[0:m, b * pad:b * pad + n], w[wi][:, c, b * P:b * P + m], xk,
                                                      first and (b * pad) % 512 == 0, final)
                                    elif g.mode == "N":
                                        for tt in range(TT):
                                            last = mm(ps[:, tt * 512:tt * 512 + g.used],
                                                      xk[:, tt * P:(tt + 1) * P], w[wi][:, c, 0:g.used], first, final)
                                    else:
                                        for gg in range(NSA_G):
                                            last = mm(ps[0:NCMP, gg * HD:(gg + 1) * HD],
                                                      xk[:, gg * NCMP:(gg + 1) * NCMP], w[wi][:, c, :],
                                                      first and gg == 0, final)
                            last.then_inc(piece_done, 1)
                        if g.rider:
                            ada_total(g, i, tb)

            def ada_total(g, i, tb):
                a = g.a0 + tb
                pe.wait_ge(ada_done, 4 * (a + 1) + per(i, 4 * g.body))
                for b in range(BLK):
                    last = mm(bank[3][:, bass.ds(per(i, BLK * g.body) + BLK * a + b, 1)],
                              ada_acc[a % 2][:, b * P:(b + 1) * P], ones[:, 0:1], True, True)
                last.then_inc(ada_sum, 1)

            def of(t, c0=0):
                return lambda tb, k: t[:, c0 + k, :]

            def norm(name):
                n = N[name]
                if n.sums == "pairs":
                    for j in range(n.n // 2):
                        pe.wait_ge(nm_sq, n.a0 + j + 1)
                        if j == 0 and n.k:
                            pe.wait_ge(nm_var, n.k)
                        for e in range(2):
                            last = mm(bank[0][:, 0:S], ones, SCRATCH[name][0][:, j % 2, e * S:(e + 1) * S],
                                      j == 0 and e == 0, j == n.n // 2 - 1 and e == 1)
                        last.then_inc(nm_acc, 1)
                elif n.sums == "tiles":
                    sq, part = SQUARES[name]
                    pe.wait_ge(nm_var, n.k)
                    for t in range(3):
                        pe.wait_ge(nm_part, n.part0 + t + 1)
                        mm(bank[0][:, 0:S], ones, part[:, t, :], t == 0, False)
                    pe.wait_ge(nm_sq, n.a0 + 4)
                    for c in range(3 * BLK, DC):
                        last = mm(bank[0][:, 0:S], ones, sq[:, c, :], False, c == DC - 1)
                    last.then_inc(nm_acc, 1)

            def rotate(name, rot, chunks):
                for j, t in enumerate(chunks):
                    k = ROPE0[name] + j
                    if k >= 2:
                        pe.wait_ge(rp_done, k - 1)
                    mm(bank[1 + k % 2][:, 0:t.shape[-1]], rot, t, True, True).then_inc(rp_rot, 1)

            def attention(name):
                us, u0, f0 = UNITS[name], U0[name], FIN0[name]
                n, fins = len(us), f0
                for s_ in range(n + 3):
                    if s_ < n:
                        u, nk = us[s_], us[s_]["nk"]
                        if u0 + s_ >= 2:
                            pe.wait_ge(at_masked, u0 + s_ - 1)
                        for hd, pairs in enumerate(u["scores"]):
                            for e, (l, r) in enumerate(pairs):
                                last = mm(bank[s_ % 2][:, hd * nk:(hd + 1) * nk], l, r, hd == 0 and e == 0,
                                          e == len(pairs) - 1)
                        last.then_inc(at_s, 1)
                    if 0 <= s_ - 2 < n:
                        e, u = s_ - 2, us[s_ - 2]
                        pe.wait_ge(at_p, u0 + e + 1)
                        if u0 + e:
                            pe.wait_ge(at_pt, u0 + e)
                        nk, nv = u["nk"], len(u["v"][0])
                        for hd in range(2):
                            for j in range(nv):
                                k = min(P, nk - j * P)
                                a = hd * nv + j
                                last = nc.tensor.transpose(bank[2][0:k, a * P:(a + 1) * P],
                                                           probs[:, (u0 + e) % 2, hd * nk + j * P:hd * nk + j * P + k], ident)
                        last.then_inc(at_t, 1)
                    if 0 <= s_ - 3 < n:
                        e, u = s_ - 3, us[s_ - 3]
                        pe.wait_ge(at_pt, u0 + e + 1)
                        if u["first"] and fins:
                            pe.wait_ge(at_fin, fins)
                        nv = len(u["v"][0])
                        for hd, vs_ in enumerate(u["v"]):
                            for j, v in enumerate(vs_):
                                k = min(P, u["nk"] - j * P)
                                a = hd * nv + j
                                last = mm(bank[3][:, hd * P:(hd + 1) * P], v, probs_t[0:k, (u0 + e) % 2, a * P:(a + 1) * P],
                                          u["first"] and a == 0, u["last"] and j == nv - 1)
                        fins += u["last"]
                        last.then_inc(at_o, 1)

            pe.wait_ge(ld_const, 16)
            pe.wait_ge(ld_vec, 16 * N_VEC_DMA)
            for t in range(3):
                n = min(P, VEC_W - t * P)
                last = nc.tensor.transpose(bank[0][:, t * P:t * P + n], vec_rows[0:n, t, :], ident[0:n, 0:n])
            last.then_inc(vec_turned, 1)
            for k in range(8):
                if k % 4 == 0:
                    pe.wait_ge(ld_x if k else ld_mem, 16)
                src = x_rows if k >= 4 else mem_rows
                if k >= 2:
                    pe.wait_ge(turn_out[k % 2], k // 2)
                for c in range(4):
                    for tt in range(TT):
                        last = nc.tensor.transpose(tile_ps[k % 2][:, c * S + tt * P:c * S + (tt + 1) * P],
                                                   src[:, tt, (k % 4 * 4 + c) * P:(k % 4 * 4 + c + 1) * P], ident)
                last.then_inc(turned, 1)
            pe.wait_ge(vec_ready, 1)
            for b in range(2):
                pe.wait_ge(turn_out[b], 4)
            norm("mem0")
            for tb in range(G["ada0"].tiles):
                ada_total(G["ada0"], 0, tb)
            norm("mix")
            h, h_mem = (of(h_hi), of(h_lo)), (of(mem_hi), of(mem_lo))
            o = (of(o_hi), of(o_lo))
            done = lambda n: [(nm_lo, N[n].c0 + N[n].n)]
            as_normed = lambda n: (lambda k: [(nm_lo, N[n].c0 + k + 1)])
            product("mem_k0", *h, chunk_ready=as_normed("mem0"))
            product("mem_v0", *h)
            product("mem_k1", *h_mem, chunk_ready=as_normed("mem1"))
            product("mem_v1", *h_mem)
            for tb in range(G["ada1"].tiles):
                ada_total(G["ada1"], 0, tb)
            product("gla_q", *h, chunk_ready=as_normed("mix"))
            product("gla_k", *h)
            product("gla_v", *h)
            product("gla_gk", *h)
            all_taken(pe, G["gla_gk"])
            pe.wait_ge(ld_gk, 32)
            for tt in range(TT):
                for e in range(2):
                    half = slice(e * 512, (e + 1) * 512)
                    mm(misc_ps[tt][:, half], gk_t[0:RANK, tt * P:(tt + 1) * P], gk_w[:, half], True, False)
                    last = mm(misc_ps[tt][:, half], ones[0:1, :], gk_b[:, half], False, True)
                last.then_inc(z_ready, 1)

            def decays(e):
                hd, tt, d = e // 4, e // 2 % 2, e % 2
                if e == 0:
                    pe.wait_ge(la_ready, 2)
                    pe.wait_ge(ld_gla, 16)
                if e >= 2:
                    pe.wait_ge(gl_ex, e - 1)
                for c in range(2):
                    last = mm(misc_ps[e % 2][:, c * 512:(c + 1) * 512],
                              log_a[:, tt, (2 * hd + d) * P:(2 * hd + d + 1) * P],
                              gla_const[:, tt, 4 * c:4 * c + 4, :], True, True)
                last.then_inc(gl_e, 1)

            def gla_scores(k):
                hd, tt = k // 2, k % 2
                pe.wait_ge(gl_qk, 2 * k + 2)
                if k:
                    pe.wait_ge(gl_red, k)
                for l in range(GLA_SLOTS):
                    for d in range(2):
                        if l < LEVELS:
                            kk, qq = k_lev[:, d, l, :], q_lev[:, d, l, :]
                        else:
                            kk, qq = (qk[:, hd, c + d, tt * P:(tt + 1) * P] for c in (2, 0))
                        last = mm(tile_ps[0][:, l * P:(l + 1) * P], kk, qq, l % 4 == 0 and d == 0, d == 1)
                if tt:
                    if hd:
                        pe.wait_ge(gl_out, hd)
                    for d in range(2):
                        last = mm(tile_ps[1][:, 0:P], k_across[:, d, :], q_lev[:, d, LEVELS, :], d == 0, d == 1)
                last.then_inc(gl_att, 1)

            def gla_output(hd):
                pe.wait_ge(gl_red, 2 * hd + 2)
                for c in range(BLK):
                    v = slice(hd * GLA_DV + c * P, hd * GLA_DV + (c + 1) * P)
                    mm(tile_ps[1][:, c * S:(c + 1) * S], gla_v[:, 0, v], gla_att[:, 0:2, :], c % 2 == 0, False)
                    last = mm(tile_ps[1][:, c * S + P:(c + 1) * S], gla_v[:, 1, v], gla_att[:, 2, :], False, True)
                last.then_inc(gl_o, 1)

            decays(0)
            decays(1)
            for k in range(2 * GLA_H):
                for e in (2 * k + 2, 2 * k + 3):
                    if e < 4 * GLA_H:
                        decays(e)
                gla_scores(k)
                if k % 2:
                    gla_output(k // 2)
            for hd in range(GLA_H):
                pe.wait_ge(nm_sq, N["gla"].a0 + hd + 1)
                for c in range(BLK):
                    last = mm(misc_ps[0][:, hd * S:(hd + 1) * S], ones, gla_sq[:, hd, c * S:(c + 1) * S],
                              c == 0 and hd % 2 == 0, c == BLK - 1)
            last.then_inc(nm_acc, 1)
            pe.wait_ge(gl_out, GLA_H)
            product("gla_g", *h)
            product("gate_a", *h)
            for b in range(2):
                pe.wait_ge(taken[b], (G["gla_g"].t1 - b + 1) // 2)
            product("gla_wo", *o)
            product("mla_cq", *h)
            product("mla_ckv", *h)
            product("mla_kr", *h)
            norm("cq")
            norm("ckv")
            product("gate_b", *h)
            all_taken(pe, G["mla_kr"])
            rotate("mla_kr", cst("rot_mla"), [k_rope[:, :]])
            for hf in range(2):
                q_op, kv_op = (of(cq_hi), of(cq_lo)), (of(ckv_hi), of(ckv_lo))
                product(f"mla_qn{hf}", *q_op, ready=done("cq"))
                product(f"mla_qr{hf}", *q_op)
                all_taken(pe, G[f"mla_qr{hf}"])
                rotate(f"mla_q{hf}", cst("rot_mla"), [mla_qr[:, c, :] for c in range(BLK)])
                product(f"mla_k{hf}", *kv_op, ready=done("ckv"))
                product(f"mla_v{hf}", *kv_op)
                all_taken(pe, G[f"mla_v{hf}"])
                pe.wait_ge(rp_done, ROPE0[f"mla_q{hf}"] + BLK)
                attention(f"mla{hf}")
            fin = lambda a: [(at_fin, FIN0[a] + sum(u["last"] for u in UNITS[a]))]
            product("mla_wo", *o, ready=fin("mla1"))
            def as_taken(t0, step=1):
                return lambda k: [(taken[(t0 + k // BLK * step) % 2], (t0 + k // BLK * step) // 2 + 1)] if k % BLK == 0 else []

            product("w_out", *h, chunk_ready=as_taken(G["mla_wo"].t0))
            norm("ffn")
            product("ffn_in0", *h, chunk_ready=as_normed("ffn"))
            product("ffn_down0", of(sw_hi), of(sw_lo), chunk_ready=as_taken(G["ffn_in0"].t0 + 1, 2))
            product("ffn_in1", *h)
            product("ffn_down1", of(sw_hi), of(sw_lo), chunk_ready=as_taken(G["ffn_in1"].t0 + 1, 2))
            norm("final1")
            norm("pool")
            product("pool_u", *h, chunk_ready=as_normed("pool"))
            product("pool_zu", *h)
            product("pool_qm", *h)
            product("pool_zm", *h)
            pe.wait_ge(pl_lo, 1)
            product("pool_w", lambda tb, k: pool_hi[:, 3 * tb + k, :], lambda tb, k: pool_lo[:, 3 * tb + k, :])
            all_taken(pe, G["pool_zm"])
            pe.wait_ge(ld_mkv, 32)
            attention("mem_a")
            all_taken(pe, G["pool_w"])
            product("pool_out", *o, ready=fin("mem_a"))
            norm("kv")
            product("nsa_kc", *h, chunk_ready=as_normed("kv"))
            for name in ("vc", "ks", "vs", "kw", "vw"):
                product(f"nsa_{name}", *h)
            for n_, kv in enumerate("kv"):
                product(f"cmp_{kv}1", of(z_pe), ready=[(zp_ready, n_ + 1)])
                all_taken(pe, G[f"cmp_{kv}1"])
                product(f"cmp_{kv}2", of(hidden))
            rotate("nsa_ks", cst("rot_nsa"), [ks[:, c, :] for c in range(NSA_G)])
            rotate("nsa_kw", cst("rot_nsa"), [kw[:, c, :] for c in range(NSA_G)])
            all_taken(pe, G["cmp_k2"])
            rotate("cmp_k", cst("rot_nsa"), [k_cmp[:, :]])
            product("nsa_q", *h, chunk_ready=as_normed("nsa"))
            product("nsa_gl", *h)
            product("nsa_zq", *h)
            rotate("nsa_q", cst("rot_nsa"), [nsa_q[:, c, :] for c in range(NSA_H)])
            product("nsa_qm", *h)
            product("nsa_zm", *h)
            all_taken(pe, G["nsa_zm"])
            pe.wait_ge(rp_done, ROPE0["nsa_q"] + NSA_H)
            attention("nsa")
            pe.wait_ge(ld_mkv, 64)
            attention("mem_b")
            product("nsa_out", *o, ready=fin("mem_b"))
            norm("final2")
            pe.wait_ge(nm_plain, N["final2"].plain0 + DC)
            for k in range(4):
                pe.wait_ge(turn_out[k % 2], TURNS_BEFORE_OUT + k // 2)
                if k < 2:
                    all_taken(pe, G["nsa_out"])
                for c in range(8):
                    last = nc.tensor.transpose(tile_ps[k % 2][:, c * P:(c + 1) * P],
                                               x[:, k % 2 * 8 + c, k // 2 * P:(k // 2 + 1) * P], ident)
                last.then_inc(turned, 1)

        @block.scalar
        def _(act):
            own = Steps(act, act_step)
            f = nc.scalar.activation

            def cut(g, i, s_, p, r):
                act.wait_ge(landed[r % 4], LANDED[r] + per(i, 16 * g.body * g.slots // 4))
                if s_ >= 2:
                    act.wait_ge(piece_done, p - 1 + per(i, g.body * g.kp))
                f(w_hi[s_ % 2][:], w_raw[r % 4][:], ACT.Copy).then_inc(cut_hi, 1)

            def cut_first(g, e):
                cut(g, 0, g.s0 + e, g.p0 + e, g.r0 + e * (g.slots // g.kp))

            def cut_in_norm(name, chunk):
                for product_, (norm_, when) in CUT_IN_NORM.items():
                    for e, c in when.items():
                        if norm_ == name and c == chunk and not (e == 0 and G[product_].first_ahead):
                            cut_first(G[product_], e)

            def product(name, take=None, flat=False):
                g = G[name]
                if g.split and not g.precut:
                    cut_first(g, 0)
                for i, last in turns(act, g, peel_last=g.split and not g.ahead, peel_first=g.precut > 1, flat=flat):
                    for tb in range(g.body):
                        if g.split:
                            for q in range(1, g.kp + 1):
                                e = tb * g.kp + q
                                done = isinstance(i, int) and i == 0 and e < g.precut
                                if not done and not (e == g.body * g.kp and last and not g.ahead):
                                    cut(g, i, g.s0 + e, g.p0 + e, g.r0 + e * (g.slots // g.kp))
                        if take:
                            ps, tk = psum_tile(g, tb)
                            tile_is_done(act, g, i, tb)
                            take(i, tb, g, ps, tk)

            def copy_to(dst, func=ACT.Copy, scale=1.0, pre=()):
                def take(i, tb, g, ps, tk):
                    for s_, v_ in pre:
                        if tb == 0:
                            act.wait_ge(s_, v_)
                    d = dst(i, tb, g)
                    n = int(np.prod(d.shape[1:]))
                    src = ps[0:d.shape[0], 0:n]
                    if len(d.shape) == 3:
                        src = src.rearrange("p (a b) -> p a b", a=d.shape[1])
                    elif len(d.shape) == 4:
                        src = src.rearrange("p (a b c) -> p a b c", a=d.shape[1], b=d.shape[2])
                    f(d, src, func, scale=scale).then_inc(tk, 1)
                return take

            def chunks(t):
                return lambda i, tb, g: t[:, bass.ds(per(i, g.body * BLK) + tb * BLK, BLK), :]

            def columns(t):
                return lambda i, tb, g: t[:, :, bass.ds(per(i, g.body * NT) + tb * NT, NT)]

            def norm(name):
                sums(name)
                apply(name)

            def sums(name):
                n = N[name]
                src = SOURCE[name]
                if n.sums == "shared":
                    return
                if n.sums == "pairs":
                    sq = SCRATCH[name][0]
                    for j in range(n.n // 2):
                        if j >= 2 or n.m0:
                            act.wait_ge(nm_acc, n.m0 + max(j - 1, 0))
                        if name == "pool":
                            act.wait_ge(nm_plain, N["final1"].plain0 + 2 * j + 2)
                        f(sq[:, j % 2, :].rearrange("p (a b) -> p a b", a=2), src(slice(2 * j, 2 * j + 2)),
                          ACT.Square).then_inc(nm_sq, 1)
                act.wait_ge(nm_var, n.k + 1)
                f(RSTD.get(name, rstd)[:], var[:], ACT.Sqrt).then_inc(nm_std, 1)

            def apply(name):
                n = N[name]
                cut_in_norm(name, -1)
                if n.split:
                    tmp, hi = SCRATCH[name][1], DEST[name][0]
                    shift = SHIFT.get(name)
                    for c in range(n.n):
                        act.wait_ge(nm_t, n.c0 + c + 1)
                        f(hi[:, c, :], tmp[:, c % 2, :], ACT.Identity,
                          bias=shift[:, c:c + 1] if shift is not None else 0.0).then_inc(nm_hi, 1)
                        cut_in_norm(name, c)

            def squares(name):
                n = N[name]
                sq = SQUARES[name][0]

                def take(i, tb, g, ps, tk):
                    t = g.t0 + tb
                    act.wait_ge(taken[t % 2], t // 2 + 1 + per(i, g.body // 2))
                    cs = slice(i * g.body * BLK + tb * BLK, i * g.body * BLK + tb * BLK + BLK)
                    f(sq[:, cs, :], x[:, cs, :], ACT.Square).then_inc(nm_sq, 1)
                return take

            def attention(name):
                us, u0 = UNITS[name], U0[name]
                n = len(us)
                for s_ in range(n + 2):
                    if s_ < n:
                        k, nk = u0 + s_, us[s_]["nk"]
                        act.wait_ge(at_max, k + 1)
                        for hd in range(2):
                            p = probs[:, k % 2, hd * nk:(hd + 1) * nk]
                            c = 2 * (k % 2) + hd
                            last = f(p, p, ACT.Exp, bias=stats[:, c:c + 1], accum_out=stats[:, 4 + c:5 + c])
                        last.then_inc(at_exp, 1)
                    if 0 <= s_ - 2 < n:
                        k, u = u0 + s_ - 2, us[s_ - 2]
                        act.wait_ge(at_t, k + 1)
                        if k >= 2:
                            act.wait_ge(at_o, k - 1)
                        w = 2 * len(u["v"][0]) * P
                        r = min(P, u["nk"])
                        f(probs_t[0:r, k % 2, 0:w], bank[2][0:r, 0:w], ACT.Copy).then_inc(at_pt, 1)

            def tables(k):
                act.wait_ge(tab_arg, k + 1)
                f(rope_sin[:], angles[:, 1, :], ACT.Sin).then_inc(tab_ready, 1)
                f(rope_cos[:], angles[:, 0, :], ACT.Sin, scale=-1.0, bias=half_pi).then_inc(tab_ready, 1)

            for k in range(8):
                if k % 2 == 0:
                    act.wait_ge(turned, k + 1)
                    dst = x if k >= 4 else mem_t
                    f(dst[:, k % 4 * 4:k % 4 * 4 + 4, :], tile_ps[0][:].rearrange("p (a b) -> p a b", a=4),
                      ACT.Copy).then_inc(turn_out[0], 1)
            act.wait_ge(vec_ready, 1)
            f(c_act[:], vec("c", 0, DC), ACT.Silu).then_inc(c_ready, 1)
            tables(0)
            act.wait_ge(turn_out[0], 4)
            act.wait_ge(turn_out[1], 4)
            norm("mem0")
            sums("mix")
            for li in range(2):
                if li:
                    norm("mem1")
                product(f"mem_k{li}", copy_to(lambda i, tb, g, li=li: mem_k_out[:, li]))
                product(f"mem_v{li}", copy_to(lambda i, tb, g, li=li: mem_v_out[:, li]))
            apply("mix")
            stored = [(st_mkv, 64)]
            pair = lambda c0: (lambda i, tb, g: qk[:, bass.ds(per(i, 2 * g.body) + 2 * tb, 2), c0:c0 + 2, :])
            product("gla_q", copy_to(pair(0), scale=GLA_DK ** -0.5, pre=stored))
            product("gla_k", copy_to(pair(2)))
            product("gla_v", copy_to(columns(gla_v)))
            product("gla_gk", copy_to(lambda i, tb, g: gk_t[0:RANK, :]))
            for tt in range(TT):
                act.wait_ge(z_ready, tt + 1)
                la = log_a[:, tt, :]
                own.wait(f(la, misc_ps[tt][:], ACT.Abs))
                own.wait(f(la, la, ACT.Exp, scale=-1.0))
                f(la, la, ACT.Ln, bias=1.0).then_inc(z_abs, 1)
            for k in range(2 * GLA_H):
                for e in (2 * k, 2 * k + 1):
                    act.wait_ge(gl_e, e + 1)
                    if e >= 2:
                        act.wait_ge(gl_qk, e - 1)
                    if e < 2:
                        act.wait_ge(ld_gk, 32)
                    f(decay[e % 2][:], misc_ps[e % 2][:].rearrange("p (a b) -> p a b", a=GLA_SLOTS),
                      ACT.Exp).then_inc(gl_ex, 1)
                if k % 2 == 0 and k:
                    hd = k // 2 - 1
                    act.wait_ge(gl_o, hd + 1)
                    f(qk[:, hd], tile_ps[1][:].rearrange("p (a b) -> p a b", a=4), ACT.Copy).then_inc(gl_out, 1)
            act.wait_ge(gl_o, GLA_H)
            f(qk[:, GLA_H - 1], tile_ps[1][:].rearrange("p (a b) -> p a b", a=4), ACT.Copy).then_inc(gl_out, 1)
            act.wait_ge(gl_out, GLA_H)
            for hd in range(GLA_H):
                f(gla_sq[:, hd, :], qk[:, hd].rearrange("p a b -> p (a b)"), ACT.Square).then_inc(nm_sq, 1)
            cut_in_norm("gla", -1)
            act.wait_ge(nm_var, N["gla"].k + 1)
            f(gla_var[:], gla_var[:], ACT.Sqrt).then_inc(nm_std, 1)

            def silu_g(i, tb, g, ps, tk):
                if tb == 0:
                    act.wait_ge(nm_plain, N["gla"].plain0 + DC)
                f(gla_tmp[:, tb % 2, :], ps[:], ACT.Silu).then_inc(silu_ready, 1)

            product("gla_g", silu_g, flat=True)
            for_ga = [(nm_plain, N["gla"].plain0 + DC)]
            product("gate_a", copy_to(chunks(merged), ACT.Sigmoid, pre=for_ga))
            product("gla_wo")
            product("mla_cq", copy_to(lambda i, tb, g: cq[:, :, :], pre=[(piece_done, G["gla_wo"].p1)]))
            product("mla_ckv", copy_to(lambda i, tb, g: ckv[:, :, :]))
            product("mla_kr", copy_to(lambda i, tb, g: k_rope[:, :]))
            all_taken(act, G["mla_ckv"])
            norm("cq")
            norm("ckv")
            product("gate_b", copy_to(chunks(gate_b), ACT.Sigmoid, pre=[(taken[b], (G["gla_g"].t1 - b + 1) // 2) for b in range(2)]), flat=True)
            for hf in range(2):
                free = [(piece_done, G["gate_b"].p1)] if hf == 0 else [(at_o, U0["mla0"] + len(UNITS["mla0"]))]
                product(f"mla_qn{hf}", copy_to(lambda i, tb, g: mla_q[:, 4 * tb:4 * tb + 4, :], pre=free))
                product(f"mla_qr{hf}", copy_to(lambda i, tb, g: mla_qr[:, :, :]))
                product(f"mla_k{hf}", copy_to(lambda i, tb, g: mla_k[:, 4 * tb:4 * tb + 4, :]))
                product(f"mla_v{hf}", copy_to(lambda i, tb, g: mla_v[:, :, tb * NT:(tb + 1) * NT]))
                attention(f"mla{hf}")
            product("mla_wo")
            product("w_out", squares("ffn"), flat=True)
            norm("ffn")

            def silu_gate(part):
                def take(i, tb, g, ps, tk):
                    if tb % 2:
                        return
                    act.wait_ge(taken[(g.t0 + 1) % 2], (g.t0 + 1 + tb) // 2 + per(i, g.body // 2))
                    f(o_tmp[:, 0, :], ps[:], ACT.Silu).then_inc(tk, 1)
                return take

            product("ffn_in0", silu_gate(0))
            product("ffn_down0")
            product("ffn_in1", silu_gate(1))
            product("ffn_down1", squares("final1"), flat=True)
            norm("final1")
            norm("pool")
            product("pool_u", copy_to(chunks(u_t), pre=[(piece_done, G["ffn_down1"].p1)]))
            product("pool_zu", copy_to(chunks(silu_z), ACT.Silu))
            act.wait_ge(pl_t, 1)
            f(pool_hi[:], run_b[:], ACT.Copy).then_inc(pl_hi, 1)
            product("pool_qm", copy_to(lambda i, tb, g: mem_q[:, :, :], pre=[(pl_lo, 1)]))
            product("pool_zm", copy_to(lambda i, tb, g: mem_z[:, :, :], ACT.Silu))
            product("pool_w")
            attention("mem_a")
            tables(1)
            product("pool_out", squares("kv"), flat=True)
            norm("kv")
            product("nsa_kc", copy_to(lambda i, tb, g: kc[:, :, :], pre=[(at_fin, FIN0["nsa"])]))
            product("nsa_vc", copy_to(lambda i, tb, g: vc[:, :, :]))
            product("nsa_ks", copy_to(lambda i, tb, g: ks[:, :, :]))
            product("nsa_vs", copy_to(lambda i, tb, g: vs[:, :, :]))
            product("nsa_kw", copy_to(lambda i, tb, g: kw[:, :, :]))
            product("nsa_vw", copy_to(lambda i, tb, g: vw[:, :, :]))
            norm("nsa")
            n60 = NSA_G * NCMP
            for n_, kv in enumerate("kv"):
                def hid(i, tb, g, ps, tk):
                    f(hidden[:], ps[:, 0:512].rearrange("p (a b) -> p a b", a=2)[:, :, 0:n60],
                      ACT.Silu).then_inc(tk, 1)
                product(f"cmp_{kv}1", hid)
                product(f"cmp_{kv}2", copy_to(lambda i, tb, g: k_cmp[:, :] if kv == "k" else v_cmp[:, :]))
            product("nsa_q", copy_to(chunks(nsa_q)))

            def gate_take(i, tb, g, ps, tk):
                f(gates[:], ps[:].rearrange("p (a b) -> p a b", a=2)[:, :, 0:3 * NSA_H], ACT.Sigmoid).then_inc(tk, 1)

            product("nsa_gl", gate_take)
            product("nsa_zq", copy_to(chunks(silu_z), ACT.Silu))
            product("nsa_qm", copy_to(lambda i, tb, g: mem_q[:, :, :], pre=[(zp_ready, 2)]))
            product("nsa_zm", copy_to(lambda i, tb, g: mem_z[:, :, :], ACT.Silu))
            attention("nsa")
            attention("mem_b")
            product("nsa_out", squares("final2"), flat=True)
            norm("final2")
            for k in (0, 2):
                act.wait_ge(turned, 8 + k + 1)
                f(out_rows[:, k // 2, 0:1024], tile_ps[0][:], ACT.Copy).then_inc(turn_out[0], 1)

        @block.vector
        def _(dve):
            v = nc.vector
            own = Steps(dve, dve_step)

            def f32(t):
                return t.bitcast(F32)

            def cut(g, i, s_, p, r):
                dve.wait_ge(cut_hi, s_ + 1 + per(i, g.body * g.kp))
                v.tensor_tensor(w_lo[s_ % 2][:], w_raw[r % 4][:], f32(w_hi[s_ % 2][:]),
                                ALU.subtract).then_inc(cut_lo, 1)

            def cut_first(g, e):
                cut(g, 0, g.s0 + e, g.p0 + e, g.r0 + e * (g.slots // g.kp))

            def cut_in_norm(name, chunk):
                for product_, (norm_, when) in CUT_IN_NORM.items():
                    for e, c in when.items():
                        if norm_ == name and c == chunk and not (e == 0 and G[product_].first_ahead):
                            cut_first(G[product_], e)

            def product(name, take=None, flat=False):
                g = G[name]
                if g.split and not g.precut:
                    cut_first(g, 0)
                for i, last in turns(dve, g, peel_last=g.split and not g.ahead, peel_first=g.precut > 1, flat=flat):
                    for tb in range(g.body):
                        if g.split:
                            for q in range(1, g.kp + 1):
                                if g.rider:
                                    ada_piece(g, i, tb, q - 1)
                                e = tb * g.kp + q
                                done = isinstance(i, int) and i == 0 and e < g.precut
                                if not done and not (e == g.body * g.kp and last and not g.ahead):
                                    cut(g, i, g.s0 + e, g.p0 + e, g.r0 + e * (g.slots // g.kp))
                        if take:
                            ps, tk = psum_tile(g, tb)
                            take(i, tb, g, ps, tk)

            def ada_piece(g, i, tb, q):
                a, r = g.a0 + tb, ring_ada(g, tb, q)
                w = w_raw[r % 4][:].rearrange("p (c n) -> p c n", c=4)
                acc = ada_acc[a % 2]
                dve.wait_ge(landed[r % 4], LANDED[r] + per(i, 16 * g.body * g.slots // 4))
                if q == 0 and a >= 2:
                    dve.wait_ge(ada_sum, a - 1 + per(i, g.body))
                for c in range(4):
                    k = 4 * q + c
                    if k == 0:
                        ins = v.tensor_scalar(acc, w[:, c, :], c_act[:, 0:1], None, ALU.mult)
                    else:
                        if c == 0:
                            dve.wait_ge(ada_done, 4 * a + q + per(i, 4 * g.body))
                        else:
                            dve.wait_ge(ada_step, 12 * a + 3 * q + c + per(i, 12 * g.body))
                        ins = v.scalar_tensor_tensor(acc, w[:, c, :], c_act[:, k:k + 1], acc, ALU.mult, ALU.add)
                    if c < 3:
                        ins.then_inc(ada_step, 1)
                    else:
                        ins.then_inc(ada_done, 1)

            def take_mod(a0, a1):
                dve.wait_ge(ada_sum, a1)
                m = slice(BLK * a0, BLK * a1)
                own.wait(v.tensor_tensor(mod[:, m], bank[3][:, m], vec("ada_b", 0, 6 * DC)[:, m], ALU.add))

            def gain(name, k, part):
                own.wait(v.scalar_tensor_tensor(gain_eff[:, k, :], mod[:, part * DC:(part + 1) * DC], 1.0,
                                                vec(name, 0, DC), ALU.add, ALU.mult))

            def step(i, tb, g, j, ins):
                ins.then_inc(tile_step, 1)
                k = STEPS[g.name]
                dve.wait_ge(tile_step, STEP0[g.name] + k * tb + j + 1 + per(i, k * g.body))

            def in_chunks(t, n=BLK):
                return t.rearrange("p (a b) -> p a b", a=n)

            def some(t, i, tb, g, n=BLK):
                return t[:, bass.ds(per(i, g.body * n) + tb * n, n), :]

            def split_to(i, tb, g, j, src, hi, lo, tk):
                step(i, tb, g, j, v.tensor_copy(hi, src))
                v.tensor_tensor(lo, src, f32(hi), ALU.subtract).then_inc(tk, 1)

            def norm(name):
                sums(name)
                apply(name)

            def root_mean_square(n, rs, var_, src):
                dve.wait_ge(nm_acc, n.m0 + {"pairs": n.n // 2}.get(n.sums, 1))
                if n.k:
                    dve.wait_ge(nm_std, n.k)
                width = P * (n.n // GLA_H if n.sums == "heads" else n.n)
                v.tensor_scalar(var_, src, 1.0 / width, EPS, ALU.mult, ALU.add).then_inc(nm_var, 1)
                dve.wait_ge(nm_std, n.k + 1)
                own.wait(v.reciprocal(rs, rs))

            def sums(name):
                n = N[name]
                if n.sums != "shared":
                    rs = RSTD.get(name, rstd)[:]
                    root_mean_square(n, rs, var[:], bank[0][:, 0:S])

            def apply(name):
                n = N[name]
                src, gain, rs = SOURCE[name], GAIN[name], RSTD.get(name, rstd)[:]
                cut_in_norm(name, -1)
                if not n.split:
                    for c in range(n.n):
                        v.scalar_tensor_tensor(DEST[name][0][:, c, :], src(c), gain[:, c:c + 1], rs,
                                               ALU.mult, ALU.mult).then_inc(nm_plain, 1)
                    return
                tmp, (hi, lo) = SCRATCH[name][1], DEST[name]
                shift = SHIFT.get(name)
                for c in range(n.n + 1):
                    if c < n.n:
                        if n.c0 + c:
                            dve.wait_ge(nm_lo, n.c0 + max(c - 1, 0))
                        v.scalar_tensor_tensor(tmp[:, c % 2, :], src(c), gain[:, c:c + 1], rs,
                                               ALU.mult, ALU.mult).then_inc(nm_t, 1)
                    if c:
                        e = c - 1
                        dve.wait_ge(nm_hi, n.c0 + e + 1)
                        if shift is None:
                            ins = v.tensor_tensor(lo[:, e, :], tmp[:, e % 2, :], f32(hi[:, e, :]), ALU.subtract)
                        else:
                            ins = v.scalar_tensor_tensor(lo[:, e, :], tmp[:, e % 2, :], shift[:, e:e + 1],
                                                         f32(hi[:, e, :]), ALU.add, ALU.subtract)
                        ins.then_inc(nm_lo, 1)
                        cut_in_norm(name, e)

            def rotate(name, chunks, cos=None, sin=None):
                for j, t in enumerate(chunks):
                    k = ROPE0[name] + j
                    n = t.shape[-1] if len(t.shape) == 2 else t.shape[1] * t.shape[2]
                    dve.wait_ge(rp_rot, k + 1)
                    if k:
                        dve.wait_ge(rp_done, k)
                    src = bank[1 + k % 2][:, 0:n]
                    tmp = var[:, 0:n]
                    if len(t.shape) == 3:
                        src, tmp = (a.rearrange("p (a b) -> p a b", a=t.shape[1]) for a in (src, tmp))
                    v.tensor_tensor(tmp, src, sin if sin is not None else rope_sin[:], ALU.mult)
                    own.wait(v.tensor_tensor(t, t, cos if cos is not None else rope_cos[:], ALU.mult))
                    v.tensor_tensor(t, t, tmp, ALU.add).then_inc(rp_done, 1)
                dve.wait_ge(rp_done, k + 1)

            def both(t):
                return t.unsqueeze(1).broadcast_to([P, 2, t.shape[-1]])

            def attention(name):
                us, u0, fins = UNITS[name], U0[name], FIN0[name]
                n = len(us)
                for s_ in range(n + 4):
                    if 0 <= s_ - 4 < n and us[s_ - 4]["last"]:
                        u, k = us[s_ - 4], u0 + s_ - 4
                        dve.wait_ge(at_o, k + 1)
                        pair = slice(u["chunk"], u["chunk"] + u["apart"] + 1, u["apart"])
                        hi, lo = o_hi[:, pair, u["q"]], o_lo[:, pair, u["q"]]
                        src = in_chunks(bank[3][:, 0:2 * P], 2)
                        if fins:
                            dve.wait_ge(at_fin, fins)
                        fins += 1
                        if u["z"] is not None:
                            own.wait(v.tensor_tensor(in_chunks(var[:], 2), src, u["z"], ALU.mult))
                            src = in_chunks(var[:], 2)
                        own.wait(v.tensor_copy(hi, src))
                        v.tensor_tensor(lo, src, f32(hi), ALU.subtract).then_inc(at_fin, 1)
                    if s_ < n:
                        u, k = us[s_], u0 + s_
                        w = 2 * u["nk"]
                        p, sc = in_chunks(probs[:, k % 2, 0:w], 2), in_chunks(bank[s_ % 2][:, 0:w], 2)
                        dve.wait_ge(at_s, k + 1)
                        if k >= 2:
                            dve.wait_ge(at_t, k - 1)
                        if u["add"] is None:
                            ins = v.tensor_scalar(p, sc, u["scale"], None, ALU.mult)
                        else:
                            ins = v.scalar_tensor_tensor(p, sc, u["scale"], both(u["add"]), ALU.mult, ALU.add)
                        ins.then_inc(at_masked, 1)
                        dve.wait_ge(at_masked, k + 1)
                        c = 2 * (k % 2)
                        v.tensor_reduce(stats[:, c:c + 2], p, AX.X, ALU.max, negate=True).then_inc(at_max, 1)
                    if 0 <= s_ - 1 < n:
                        u, k = us[s_ - 1], u0 + s_ - 1
                        c = 2 * (k % 2)
                        p = in_chunks(probs[:, k % 2, 0:2 * u["nk"]], 2)
                        r = stats[:, 8 + c:10 + c]
                        dve.wait_ge(at_exp, k + 1)
                        own.wait(v.reciprocal(r, stats[:, 4 + c:6 + c]))
                        if u["gate"] is not None:
                            rg = stats[:, 12 + c:14 + c]
                            own.wait(v.tensor_tensor(rg, r, u["gate"], ALU.mult))
                            r = rg
                        rr = r.unsqueeze(2).broadcast_to([P, 2, u["nk"]])
                        ins = v.tensor_tensor(p, p, rr, ALU.mult)
                        if u["mul"] is not None:
                            own.wait(ins)
                            ins = v.tensor_tensor(p, p, both(u["mul"]), ALU.mult)
                        ins.then_inc(at_p, 1)

            def tables(k):
                dve.wait_ge(ld_pos, 16 * (k + 1))
                pos, a, t = angles[:, 2, :], angles[:, 1, :], angles[:, 0, :]
                own.wait(v.tensor_copy(a, pos.bitcast(I32)))
                own.wait(v.tensor_scalar(a, a, cst(("freq_mla", "freq_nsa")[k]), None, ALU.mult))
                big = 1.5 * 2.0 ** 23
                own.wait(v.tensor_scalar(t, a, 1.0 / (2 * math.pi), big, ALU.mult, ALU.add))
                own.wait(v.tensor_scalar(t, t, -big, None, ALU.add))
                hi = 6.28125
                mid = float(np.float32(round((2 * math.pi - hi) * 2 ** 20) / 2 ** 20))
                for c in (hi, mid, 2 * math.pi - hi - mid):
                    own.wait(v.scalar_tensor_tensor(a, t, -c, a, ALU.mult, ALU.add))
                pi = 3.1415925
                own.wait(v.tensor_scalar(a, a, pi, -pi, ALU.min, ALU.max))
                v.scalar_tensor_tensor(t, a, -1.0, a, ALU.mult, ALU.max).then_inc(tab_arg, 1)
                dve.wait_ge(tab_ready, 2 * k + 2)

            v.memset(half_pi, math.pi / 2).then_inc(dve_step, 1)
            own.n += 1
            dve.wait_ge(dve_step, 1)
            dve.wait_ge(vec_turned, 1)
            v.tensor_copy(cols[:], bank[0][:, 0:VEC_W]).then_inc(vec_ready, 1)
            for k in range(8):
                if k % 2:
                    dve.wait_ge(turned, k + 1)
                    dst = x if k >= 4 else mem_t
                    v.tensor_copy(dst[:, k % 4 * 4:k % 4 * 4 + 4, :], in_chunks(tile_ps[1][:])).then_inc(turn_out[1], 1)
            dve.wait_ge(ld_const, 16)
            tables(0)
            dve.wait_ge(turn_out[0], 4)
            dve.wait_ge(turn_out[1], 4)
            dve.wait_ge(c_ready, 1)
            for tb in range(2):
                for q in range(4):
                    ada_piece(G["ada0"], 0, tb, q)
            norm("mem0")
            sums("mix")
            for li in range(2):
                if li:
                    norm("mem1")
                product(f"mem_k{li}")
                product(f"mem_v{li}")
            for tb in range(G["ada1"].tiles):
                for q in range(4):
                    ada_piece(G["ada1"], 0, tb, q)
            take_mod(0, 2 * DC // BLK)
            gain("norm_mix_g", 0, 1)
            apply("mix")
            product("gla_q")
            product("gla_k")
            product("gla_v")
            product("gla_gk")
            for tt in range(TT):
                dve.wait_ge(z_abs, tt + 1)
                v.scalar_tensor_tensor(log_a[:, tt, :], misc_ps[tt][:], 0.0, log_a[:, tt, :],
                                       ALU.min, ALU.subtract).then_inc(la_ready, 1)

            all_taken(dve, G["gla_gk"])
            for k in range(2 * GLA_H):
                hd, tt = k // 2, k % 2
                if k:
                    dve.wait_ge(gl_att, k)
                for d in range(2):
                    e = 2 * k + d
                    dve.wait_ge(gl_ex, e + 1)
                    ex = decay[e % 2]
                    q, kk = (qk[:, hd, c + d, tt * P:(tt + 1) * P].unsqueeze(1) for c in (0, 2))
                    v.tensor_tensor(q_lev[:, d], q.broadcast_to([P, GLA_SLOTS, P]), ex[:], ALU.mult)
                    if tt == 0:
                        v.tensor_tensor(k_across[:, d, :], kk[:, 0, :], ex[:, LEVELS, :], ALU.mult)
                    v.tensor_tensor(k_lev[:, d, 0:LEVELS, :], kk.broadcast_to([P, LEVELS, P]), ex[:, 0:LEVELS, :],
                                    ALU.mult).then_inc(gl_qk, 1)
                dve.wait_ge(gl_att, k + 1)
                if tt == 0 and hd:
                    dve.wait_ge(gl_o, hd)
                sc = tile_ps[0][:].rearrange("p (l i) -> p l i", l=GLA_SLOTS)
                own.wait(v.tensor_tensor(sc, sc, gla_const[:, 2], ALU.mult))
                if tt:
                    v.tensor_copy(gla_att[:, 1, :], tile_ps[1][:, 0:P])
                v.tensor_reduce(gla_att[:, 2 * tt, :], tile_ps[0][:].rearrange("p (l i) -> p i l", l=GLA_SLOTS),
                                AX.X, ALU.add).then_inc(gl_red, 1)
            dve.wait_ge(gl_out, GLA_H)
            n_gla = N["gla"]
            cut_in_norm("gla", -1)
            root_mean_square(n_gla, gla_var[:], gla_var[:], misc_ps[0][:].rearrange("p (a b) -> p a b", a=GLA_H))
            for hd in range(GLA_H):
                for c in range(BLK):
                    v.scalar_tensor_tensor(qk[:, hd, c, :], qk[:, hd, c, :], vec("gla_onorm_g", c), gla_var[:, hd, :],
                                           ALU.mult, ALU.mult).then_inc(nm_plain, 1)
            dve.wait_ge(nm_plain, N["gla"].plain0 + DC)

            def gated(i, tb, g, ps, tk):
                dve.wait_ge(silu_ready, g.t0 - G["gla_g"].t0 + tb + 1 + per(i, g.body))
                o4 = qk[:, bass.ds(per(i, g.body) + tb, 1), :, :].rearrange("p a c n -> p (a c n)")
                step(i, tb, g, 0, v.tensor_tensor(o4, o4, gla_tmp[:, tb % 2, :], ALU.mult))
                split_to(i, tb, g, 1, in_chunks(o4), some(o_hi, i, tb, g), some(o_lo, i, tb, g), tk)

            product("gla_g", gated, flat=True)
            product("gate_a")

            def gla_merge(i, tb, g, ps, tk):
                tile_is_done(dve, g, i, tb)
                m = some(merged, i, tb, g)
                v.tensor_tensor(m, m, in_chunks(ps[:]), ALU.mult).then_inc(tk, 1)

            all_taken(dve, G["gate_a"])
            product("gla_wo", gla_merge)
            product("mla_cq")
            product("mla_ckv")
            product("mla_kr")
            norm("cq")
            norm("ckv")
            product("gate_b", flat=True)
            take_mod(2 * DC // BLK, ADA_TILES)
            gain("norm_ffn_g", 1, 4)
            all_taken(dve, G["mla_kr"])
            rotate("mla_kr", [k_rope[:, :]])
            for hf in range(2):
                product(f"mla_qn{hf}")
                product(f"mla_qr{hf}")
                rotate(f"mla_q{hf}", [mla_qr[:, c, :] for c in range(BLK)])
                product(f"mla_k{hf}")
                product(f"mla_v{hf}")
                attention(f"mla{hf}")

            def both_merge(i, tb, g, ps, tk):
                tile_is_done(dve, g, i, tb)
                last_taken(dve, g, i, tb)
                t = in_chunks(mla_tmp[:])
                step(i, tb, g, 0, v.tensor_tensor(t, in_chunks(ps[:]), some(gate_b, i, tb, g), ALU.mult))
                step(i, tb, g, 1, v.tensor_tensor(t, t, some(merged, i, tb, g), ALU.add))
                split_to(i, tb, g, 2, t, some(h_hi, i, tb, g), some(h_lo, i, tb, g), tk)

            all_taken(dve, G["gate_b"])
            product("mla_wo", both_merge)

            def residual(tmp, part=None, squared=None):
                def take(i, tb, g, ps, tk):
                    add(i, tb, g, ps, tk)
                    t = i * g.body + tb if squared else 0
                    if t:
                        dve.wait_ge(nm_sq, N[squared].a0 + t)
                        sq, sums_ = SQUARES[squared]
                        v.tensor_reduce(sums_[:, t - 1, :], sq[:, (t - 1) * BLK:t * BLK, :].rearrange("p c n -> p n c"),
                                        AX.X, ALU.add).then_inc(nm_part, 1)

                def add(i, tb, g, ps, tk):
                    tile_is_done(dve, g, i, tb)
                    xx = some(x, i, tb, g)
                    if part is None:
                        v.tensor_tensor(xx, xx, in_chunks(ps[:]), ALU.add).then_inc(tk, 1)
                        return
                    gate = mod[:, bass.ds(per(i, g.body * BLK) + part * DC + tb * BLK, BLK)].unsqueeze(2)
                    last_taken(dve, g, i, tb)
                    t = in_chunks(tmp)
                    step(i, tb, g, 0, v.tensor_tensor(t, in_chunks(ps[:]), gate.broadcast_to([P, BLK, S]), ALU.mult))
                    v.tensor_tensor(xx, xx, t, ALU.add).then_inc(tk, 1)
                return take

            product("w_out", residual(o_tmp[:, 0, :], 2, "ffn"), flat=True)
            norm("ffn")

            def up(i, tb, g, ps, tk):
                if tb % 2 == 0:
                    return
                if g.name == "ffn_in1":
                    dve.wait_ge(piece_done, G["ffn_down0"].p1)
                tile_is_done(dve, g, i, tb)
                dve.wait_ge(taken[g.t0 % 2], (g.t0 + tb - 1) // 2 + 1 + per(i, g.body // 2))
                t = o_tmp[:, 0, :]
                n = g.body // 2
                k = STEPS[g.name]
                s0 = STEP0[g.name] + k * (tb // 2)
                v.tensor_tensor(t, ps[:], t, ALU.mult).then_inc(tile_step, 1)
                dve.wait_ge(tile_step, s0 + 1 + per(i, k * n))
                at_ = bass.ds(per(i, n * BLK) + tb // 2 * BLK, BLK)
                hi, lo = sw_hi[:, at_, :], sw_lo[:, at_, :]
                v.tensor_copy(hi, in_chunks(t)).then_inc(tile_step, 1)
                dve.wait_ge(tile_step, s0 + 2 + per(i, k * n))
                v.tensor_tensor(lo, in_chunks(t), f32(hi), ALU.subtract).then_inc(tk, 1)

            for part in range(2):
                product(f"ffn_in{part}", up)
                product(f"ffn_down{part}", residual(o_tmp[:, 1, :], 5, "final1" if part else None), flat=part == 1)
            norm("final1")
            norm("pool")

            product("pool_u")
            all_taken(dve, G["pool_u"])
            src, bufs = u_t, (run_a, run_b)
            for j in range(POOL_G):
                d, sh, c0 = bufs[j % 2], 2 ** j, 3 * j
                own.wait(v.tensor_copy(d[:, c0:, 0:sh], src[:, c0:, 0:sh]))
                own.wait(v.tensor_tensor(d[:, c0:, sh:], src[:, c0:, sh:], src[:, c0:, 0:S - sh], ALU.add))
                src = d
            for g_ in range(POOL_G):
                cs = slice(3 * g_, 3 * g_ + 3)
                s_ = bufs[g_ % 2]
                a = CONST["pool_head"][0] + 16 * g_
                head = const[:, a:a + 16].unsqueeze(1).broadcast_to([P, 3, 16])
                own.wait(v.tensor_tensor(s_[:, cs, 0:16], s_[:, cs, 0:16], head, ALU.mult))
                ins = v.scalar_tensor_tensor(run_b[:, cs, :], s_[:, cs, :], 0.5 ** (g_ + 1), u_t[:, cs, :],
                                             ALU.mult, ALU.subtract)
                if g_ == POOL_G - 1:
                    ins.then_inc(pl_t, 1)
                else:
                    own.wait(ins)
            product("pool_zu")
            dve.wait_ge(pl_hi, 1)
            v.tensor_tensor(pool_lo[:], run_b[:], f32(pool_hi[:]), ALU.subtract).then_inc(pl_lo, 1)
            product("pool_qm")
            product("pool_zm")

            def pool_take(i, tb, g, ps, tk):
                tile_is_done(dve, g, i, tb)
                last_taken(dve, g, i, tb)
                t = in_chunks(pool_tmp[:], 3)
                a = VECTORS["a_pool_scale_2"][0] + 3 * tb
                scale = cols[:, a:a + 3].unsqueeze(2).broadcast_to([P, 3, S])
                step(i, tb, g, 0, v.tensor_tensor(t, in_chunks(ps[:, 0:3 * S], 3), scale, ALU.mult))
                step(i, tb, g, 1, v.tensor_tensor(t, t, silu_z[:, 3 * tb:3 * tb + 3, :], ALU.mult))
                split_to(i, tb, g, 2, t, o_hi[:, 3 * tb:3 * tb + 3, :], o_lo[:, 3 * tb:3 * tb + 3, :], tk)

            all_taken(dve, G["pool_zm"])
            dve.wait_ge(pl_lo, 1)
            product("pool_w", pool_take)
            attention("mem_a")
            tables(1)
            product("pool_out", residual(None, squared="kv"), flat=True)
            norm("kv")
            for name in ("kc", "vc", "ks", "vs", "kw", "vw"):
                product(f"nsa_{name}")
            all_taken(dve, G["nsa_vw"])
            for n_, (kv, t) in enumerate((("k", kc), ("v", vc))):
                if n_:
                    dve.wait_ge(piece_done, G["cmp_k1"].p1)
                for a in range(2):
                    z = t[:].rearrange("p g (n b) -> p b g n", b=CMP_STRIDE)[:, :, :, a:a + NCMP]
                    for gg in range(NSA_G):
                        pe_ = vec("cmp_pe_2", n_ * CMP_LEN + 16 * a, 16).unsqueeze(2).broadcast_to([P, 16, NCMP])
                        ins = v.tensor_tensor(z_pe[:, 16 * a:16 * a + 16, gg * NCMP:(gg + 1) * NCMP], z[:, :, gg, :],
                                              pe_, ALU.add)
                ins.then_inc(zp_ready, 1)
                if n_ == 0:
                    dve.wait_ge(piece_done, G["nsa_vw"].p1)
                    norm("nsa")
                product(f"cmp_{kv}1")
                product(f"cmp_{kv}2")
            rotate("nsa_ks", [ks[:, c, :] for c in range(NSA_G)])
            rotate("nsa_kw", [kw[:, c, :] for c in range(NSA_G)])
            at_end = slice(CMP_LEN - 1, S, CMP_STRIDE)
            all_taken(dve, G["cmp_k2"])
            rotate("cmp_k", [k_cmp[:].rearrange("p (g n) -> p g n", g=NSA_G)],
                   rope_cos[:, at_end].unsqueeze(1).broadcast_to([P, NSA_G, NCMP]),
                   rope_sin[:, at_end].unsqueeze(1).broadcast_to([P, NSA_G, NCMP]))
            product("nsa_q")
            product("nsa_gl")
            product("nsa_zq")
            all_taken(dve, G["nsa_q"])
            rotate("nsa_q", [nsa_q[:, c, :] for c in range(NSA_H)])
            product("nsa_qm")
            product("nsa_zm")
            all_taken(dve, G["nsa_zm"])
            attention("nsa")
            attention("mem_b")
            product("nsa_out", residual(None, squared="final2"), flat=True)
            norm("final2")
            for k in (1, 3):
                dve.wait_ge(turned, 8 + k + 1)
                v.tensor_copy(out_rows[:, k // 2, 1024:2048], tile_ps[1][:]).then_inc(turn_out[1], 1)


IN_NAMES = ("x", "c", "positions", "ada_w", "ada_b", "norm_mix_g", "w_in", "gla_gk_w", "gla_gk_b", "gla_onorm_g",
            "gla_wo", "mla_q_norm_g", "mla_wuq", "mla_kv_norm_g", "mla_wukv", "mla_wo", "w_out", "norm_ffn_g",
            "ffn_w_in", "ffn_w_down", "final_norm_g", "mem_2", "positions_2", "norm_g_2", "mem_norm_g_2",
            "w_mem_kv_2", "w_out_2", "a_w_in_2", "a_w_pool_2", "a_pool_scale_2", "b_w_in_2", "kv_norm_g_2",
            "w_kv_2", "cmp_pe_2", "cmp_w1_2", "cmp_w2_2", "final_g_2")


def kernel(**inputs):
    import concourse.bacc as bacc
    from concourse.bass_utils import run_bass_kernel_spmd

    nc = bacc.Bacc("TRN2", target_bir_lowering=False, num_devices=1)
    const, gla_const = constants()
    arrays = {"in_const": const, "in_gla_const": gla_const}
    for name in IN_NAMES:
        arrays[f"in_{name}"] = np.ascontiguousarray(inputs[name])
    A = {name[3:]: nc.dram_tensor(name, a.shape, mybir.dt.from_np(a.dtype), kind="ExternalInput").ap()
         for name, a in arrays.items()}
    out = nc.dram_tensor("out", (1, S, D), F32, kind="ExternalOutput").ap()
    program(nc, A, out)
    r = run_bass_kernel_spmd(nc, [arrays], core_ids=[0])
    return r.results[0]["out"]
```

```python
import math
from contextlib import ExitStack

import numpy as np

import concourse.bass as bass
from concourse import mybir

F32 = mybir.dt.float32
F32R = mybir.dt.float32r
I32 = mybir.dt.int32
ALU = mybir.AluOpType
ACT = mybir.ActivationFunctionType
AX = mybir.AxisListType

P = 128
S = 256
TT = S // P
D = 2048
DC = D // P
NT = 512
BLK = NT // P
EPS = 1e-6

GLA_H, GLA_DK, GLA_DV, RANK = 4, 256, 512, 16
LEVELS = 7
MLA_H, NOPE, ROPE, QR, KVR = 16, 128, 64, 512, 512
HALF_H = MLA_H // 2
FFN = 5632
FFN_PARTS = (6, 5)
MEM_H, HD = 4, 128
POOL_W, POOL_G, POOL_GC = 1536, 4, 384
NSA_H, NSA_G = 12, 4
CMP_LEN, CMP_STRIDE, CMP_HID = 32, 16, 256
NCMP = (S - CMP_LEN) // CMP_STRIDE + 1
NEG = -1e30

W_Q, W_K, W_V, W_G = 0, 1024, 2048, 4096
W_GK = 6144
W_CQ = W_GK + RANK
W_CKV = W_CQ + QR
W_KR = W_CKV + KVR
W_GA = W_KR + ROPE
W_GB = W_GA + D
B_Q, B_GL = 0, NSA_H * HD
B_ZQ = B_GL + 3 * NSA_H
B_QM = B_ZQ + NSA_H * HD
B_ZM = B_QM + MEM_H * HD

CONST = {}
_at = 0
for _n, _w in (("ident", P), ("ones", P), ("rot_mla", P), ("rot_nsa", P), ("causal", 2 * P),
               ("cmp_add", 2 * NCMP), ("cmp_mul", 2 * NCMP), ("freq_mla", 1), ("freq_nsa", 1),
               ("pool_head", POOL_G * 16)):
    CONST[_n] = (_at, _w)
    _at += _w
CONST_W = _at
GLA_SLOTS = LEVELS + 1
GLA_CONST_W = 3 * GLA_SLOTS * P

VECTORS = {}
_at = 0
for _n, _w in (("norm_mix_g", DC), ("ada_b", 6 * DC), ("gla_onorm_g", GLA_DV // P), ("mla_q_norm_g", QR // P),
               ("mla_kv_norm_g", KVR // P), ("norm_ffn_g", DC), ("final_norm_g", DC), ("norm_g_2", 2 * DC),
               ("mem_norm_g_2", 2 * DC), ("a_pool_scale_2", POOL_W // P), ("kv_norm_g_2", DC),
               ("final_g_2", DC), ("c", DC), ("cmp_pe_2", 2 * CMP_LEN)):
    VECTORS[_n] = (_at, _w)
    _at += _w
VEC_W = _at


def constants():
    t = np.arange(P)
    c = np.zeros((P, CONST_W), np.float32)

    def put(name, a):
        at, w = CONST[name]
        c[:, at:at + w] = a

    put("ident", np.eye(P))
    put("ones", 1.0)
    rot = np.zeros((P, P))
    for m in range(P):
        rot[(m + 32, m) if m % 64 < 32 else (m - 32, m)] = -1.0 if m % 64 < 32 else 1.0
    put("rot_mla", rot)
    rot = np.zeros((P, P))
    for m in range(32):
        rot[(m + 16, m) if m < 16 else (m - 16, m)] = -1.0 if m < 16 else 1.0
    put("rot_nsa", rot)
    put("causal", np.concatenate([np.zeros((P, P)), np.where(t[None, :] <= t[:, None], 0.0, NEG)], 1))
    ends = np.arange(NCMP) * CMP_STRIDE + CMP_LEN - 1
    seen = np.concatenate([ends[None, :] <= (t[:, None] + tt * P) for tt in range(TT)], 1)
    put("cmp_add", np.where(seen, 0.0, NEG))
    put("cmp_mul", seen)
    put("freq_mla", (10000.0 ** (-(t % 32) * 2.0 / ROPE))[:, None])
    put("freq_nsa", np.where(t < 32, 500000.0 ** (-(t % 16) * 2.0 / 32), 0.0)[:, None])
    head = [2.0 ** (g + 1) / np.minimum(np.arange(16) + 1, 2.0 ** (g + 1)) for g in range(POOL_G)]
    put("pool_head", np.concatenate(head)[None, :])

    g = np.zeros((P, 3, GLA_SLOTS, P), np.float32)
    s, i = np.meshgrid(t, t, indexing="ij")
    for l in range(LEVELS):
        m = 2 ** l
        mid = i // (2 * m) * (2 * m) + m
        right = i % (2 * m) >= m
        g[:, 0, l] = g[:, 1, l] = np.where(right, (s >= mid) & (s <= i), (s > i) & (s < mid)) / 16.0
        g[:, 2, l] = (s // (2 * m) == i // (2 * m)) & (s % (2 * m) < m) & right
    g[:, 0, LEVELS] = (s > i) / 16.0
    g[:, 1, LEVELS] = (s <= i) / 16.0
    g[:, 2, LEVELS] = s == i
    return c, g.reshape(P, GLA_CONST_W)


class Product:

    def __init__(self, name, tiles, kp, kc=4, width=NT, split=True, mode="T", dmas=1, rider=0):
        self.name, self.tiles, self.kp, self.kc, self.width = name, tiles, kp, kc, width
        self.split, self.mode, self.dmas, self.rider = split, mode, dmas, rider
        self.slots = kp + (kp // rider if rider and mode != "A" else 0)
        for b in (2, 4):
            if (b * kp) % 4 == 0 and tiles % b == 0:
                break
        self.body, self.turns = (b, tiles // b) if tiles % b == 0 and (b * kp) % 4 == 0 and mode != "A" else (tiles, 1)

    def ada_tiles(self, n):
        return n // self.rider if self.rider else 0


PRODUCTS = [Product("ada0", 3, 4, split=False, mode="A", rider=1),
            Product("mem_k0", 1, 4, rider=1), Product("mem_v0", 1, 4, mode="N", rider=1),
            Product("mem_k1", 1, 4, rider=1), Product("mem_v1", 1, 4, mode="N", rider=1),
            Product("ada1", 1, 4, split=False, mode="A", rider=1),
            Product("gla_q", 2, 4, rider=2), Product("gla_gk", 1, 1, kc=16, width=P), Product("gla_k", 2, 4, rider=2), Product("gla_v", 4, 4, mode="N", rider=2),
            Product("gla_g", 4, 4, rider=2), Product("gate_a", 4, 4, rider=2),
            Product("gla_wo", 4, 4, rider=2),
            Product("mla_cq", 1, 4), Product("mla_ckv", 1, 4),
            Product("mla_kr", 1, 1, kc=16, width=P, dmas=2),
            Product("gate_b", 4, 4, rider=2)]
for _h in range(2):
    PRODUCTS += [Product(f"mla_qn{_h}", 2, 1, dmas=4), Product(f"mla_qr{_h}", 1, 1, dmas=4),
                 Product(f"mla_k{_h}", 2, 1, dmas=4), Product(f"mla_v{_h}", 2, 1, mode="N", dmas=4)]
PRODUCTS += [Product("mla_wo", 4, 4, rider=2), Product("w_out", 4, 4, rider=2)]
for _h, _n in enumerate(FFN_PARTS):
    PRODUCTS += [Product(f"ffn_in{_h}", 2 * _n, 4), Product(f"ffn_down{_h}", 4, _n)]
PRODUCTS += [Product("pool_u", 3, 4), Product("pool_zu", 3, 4), Product("pool_qm", 1, 4), Product("pool_zm", 1, 4),
             Product("pool_w", 4, 1, kc=3, width=POOL_GC), Product("pool_out", 4, 4),
             Product("nsa_kc", 1, 4), Product("nsa_vc", 1, 4),
             Product("nsa_ks", 1, 4), Product("nsa_vs", 1, 4, mode="N"),
             Product("nsa_kw", 1, 4), Product("nsa_vw", 1, 4, mode="N"),
             Product("cmp_k1", 1, 4, kc=8, width=CMP_HID, mode="R"),
             Product("cmp_v1", 1, 4, kc=8, width=CMP_HID, mode="R"),
             Product("cmp_k2", 1, 1, kc=2, width=HD, split=False),
             Product("cmp_v2", 1, 1, kc=2, width=HD, split=False, mode="C"),
             Product("nsa_q", 3, 4), Product("nsa_gl", 1, 1, kc=16, width=P),
             Product("nsa_zq", 3, 4), Product("nsa_qm", 1, 4), Product("nsa_zm", 1, 4),
             Product("nsa_out", 4, 4)]
AT_START = {0: -1, 1: -1, 2: 9, 3: 13}
CUT_IN_NORM = {"mem_k1": ("mem1", {0: -1, 1: -1, 2: 7, 3: 12}), "gla_q": ("mix", {0: 1, 1: 4, 2: 9, 3: 13}),
               "gla_g": ("gla", {0: -1, 1: -1}), "gate_b": ("ckv", {0: -1, 1: -1}),
               "ffn_in0": ("ffn", AT_START), "pool_u": ("pool", AT_START), "nsa_kc": ("kv", AT_START),
               "nsa_q": ("nsa", {0: 0, 1: 2, 2: 9, 3: 13})}
G = {}
LANDED = []
KIND = []
BEFORE = {"split": [0], "plain": [0], "ada": [0]}
_in_slot = [0] * 4
_p = _s = _t = _a = 0
for _i, _g in enumerate(PRODUCTS):
    _g.r0, _g.p0, _g.s0, _g.t0, _g.a0 = len(LANDED), _p, _s, _t, _a
    for _k in range(_g.tiles * _g.slots):
        _ada = _g.mode == "A" or (_g.rider > 0 and _k % (_g.rider + 1) == _g.rider)
        _in_slot[len(LANDED) % 4] += 16 * (1 if _ada else _g.dmas)
        LANDED.append(_in_slot[len(LANDED) % 4])
        KIND.append("ada" if _ada else "split" if _g.split else "plain")
        for _kind, _is in (("split", _g.split and not _ada), ("plain", not _ada), ("ada", _ada)):
            BEFORE[_kind].append(BEFORE[_kind][-1] + _is)
    if _g.mode != "A":
        _p += _g.tiles * _g.kp
        _s += _g.tiles * _g.kp * _g.split
        _t += _g.tiles
    _a += _g.ada_tiles(_g.tiles)
    _g.p1, _g.t1 = _p, _t
    _next = PRODUCTS[_i + 1] if _i + 1 < len(PRODUCTS) else None
    _g.ahead = bool(_g.split and _next and _next.split and (_g.turns == 1 or _next.dmas == 1))
    _g.first_ahead = _i > 0 and PRODUCTS[_i - 1].ahead
    _g.precut = len(CUT_IN_NORM[_g.name][1]) if _g.name in CUT_IN_NORM else int(_g.first_ahead)
    G[_g.name] = _g
ADA_TILES = _a


class Norm:

    def __init__(self, name, n, split=True, sums="pairs"):
        self.name, self.n, self.split, self.sums = name, n, split, sums


NORMS = [Norm("mem0", DC), Norm("mem1", DC, sums="shared"), Norm("mix", DC), Norm("gla", DC, split=False, sums="heads"),
         Norm("cq", QR // P), Norm("ckv", KVR // P), Norm("ffn", DC, sums="tiles"),
         Norm("final1", DC, split=False, sums="tiles"), Norm("pool", DC), Norm("kv", DC, sums="tiles"),
         Norm("nsa", DC, sums="shared"), Norm("final2", DC, split=False, sums="tiles")]
N = {}
_a = _c = _k = _m = _pt = _pl = 0
for _g in NORMS:
    _g.k, _g.a0, _g.m0, _g.part0, _g.c0, _g.plain0 = _k, _a, _m, _pt, _c, _pl
    _k += _g.sums != "shared"
    _a += {"pairs": _g.n // 2, "tiles": 4, "shared": 0, "heads": GLA_H}[_g.sums]
    _m += {"pairs": _g.n // 2, "tiles": 1, "shared": 0, "heads": 1}[_g.sums]
    _pt += 3 * (_g.sums == "tiles")
    _c += _g.n * _g.split
    _pl += _g.n * (not _g.split)
    N[_g.name] = _g

ROPES = [("mla_kr", 1), ("mla_q0", BLK), ("mla_q1", BLK), ("nsa_ks", BLK), ("nsa_kw", BLK), ("cmp_k", 1), ("nsa_q", NSA_H)]
ROPE0 = {}
_a = 0
for _n, _w in ROPES:
    ROPE0[_n] = _a
    _a += _w


STEPS = {"gla_g": 2, "mla_wo": 3, "ffn_in0": 2, "ffn_in1": 2, "pool_w": 3}
STEP0 = {}
_a = 0
for _g in PRODUCTS:
    if _g.name in STEPS:
        STEP0[_g.name] = _a
        _a += STEPS[_g.name] * (_g.tiles // 2 if _g.name.startswith("ffn_in") else _g.tiles)

N_VEC_DMA = sum((a + w - 1) // P - a // P + 1 for a, w in VECTORS.values())
TURNS_BEFORE_OUT = 4


class Steps:

    def __init__(self, eng, sem):
        self.eng, self.sem, self.n = eng, sem, 0

    def wait(self, ins):
        self.n += 1
        ins.then_inc(self.sem, 1)
        self.eng.wait_ge(self.sem, self.n)


def program(nc, A, out):
    with ExitStack() as ctx:
        def sem(name):
            return ctx.enter_context(nc.semaphore(name))

        base = (nc.sbuf_base + 63) // 64 * 64
        arena = ctx.enter_context(nc.sbuf_tensor("arena", [P, (nc.sbuf_usable_end - base - 64) // 4], F32))
        KB = 1024
        RAW, WHI, WLO, XB, HB, OB, BIG, SMALL = (k * KB for k in (0, 32, 48, 64, 80, 112, 144, 192))

        def at(name, off, shape, dt=F32):
            return nc.alloc_sbuf_tensor_at(name, shape, dt, offset=base + off)

        w_raw = [at(f"w_raw{i}", RAW + 8 * KB * i, [P, 2048]) for i in range(4)]
        w_hi = [at(f"w_hi{i}", WHI + 8 * KB * i, [P, 2048], F32R) for i in range(2)]
        w_lo = [at(f"w_lo{i}", WLO + 8 * KB * i, [P, 2048], F32R) for i in range(2)]
        x = at("x", XB, [P, DC, S])
        h_hi = at("h_hi", HB, [P, DC, S], F32R)
        h_lo = at("h_lo", HB + 16 * KB, [P, DC, S], F32R)
        o_hi = at("o_hi", OB, [P, DC, S], F32R)
        o_lo = at("o_lo", OB + 16 * KB, [P, DC, S], F32R)
        x_rows = at("x_rows", OB, [P, TT, D])
        mem_rows = at("mem_rows", OB + 16 * KB, [P, TT, D])
        mem_t = at("mem_t", BIG, [P, DC, S])
        mem_k_out = at("mem_k_out", BIG + 16 * KB, [P, 2, BLK, S])
        mem_v_out = at("mem_v_out", BIG + 24 * KB, [P, 2, TT, NT])
        vec_rows = at("vec_rows", BIG + 32 * KB, [P, 3, P])
        nscratch_b = at("nscratch_b", BIG + 40 * KB, [P, 2, 2 * S])
        ntmp_b = at("ntmp_b", BIG + 44 * KB, [P, 2, S])
        rstd_mix = at("rstd_mix", BIG + 46 * KB, [P, S])
        mem_hi = at("mem_hi", OB, [P, DC, S], F32R)
        mem_lo = at("mem_lo", OB + 16 * KB, [P, DC, S], F32R)
        qk = at("qk", BIG, [P, GLA_H, 4, S])
        gla_v = at("gla_v", BIG + 16 * KB, [P, TT, D])
        log_a = at("log_a", BIG + 32 * KB, [P, TT, GLA_H * GLA_DK])
        gla_const = at("gla_const", OB, [P, 3, GLA_SLOTS, P])
        q_lev = at("q_lev", OB + 12 * KB, [P, 2, GLA_SLOTS, P])
        k_lev = at("k_lev", OB + 20 * KB, [P, 2, GLA_SLOTS, P])
        gk_w = at("gk_w", OB + 12 * KB, [RANK + 1, GLA_H * GLA_DK])
        decay = [at("decay0", OB + 28 * KB, [P, GLA_SLOTS, P]), at("decay1", BIG + 40 * KB, [P, GLA_SLOTS, P])]
        gla_att = at("gla_att", BIG + 44 * KB, [P, 3, P])
        k_across = at("k_across", BIG + 44 * KB + 1536, [P, 2, P])
        gk_t = at("gk_t", BIG + 46 * KB + 512, [P, S])
        gla_sq = at("gla_sq", OB + 12 * KB, [P, GLA_H, BLK * S])
        gla_var = at("gla_var", BIG + 32 * KB, [P, GLA_H, S])
        gla_tmp = at("gla_tmp", BIG + 40 * KB, [P, 2, BLK * S])
        merged = at("merged", BIG + 16 * KB, [P, DC, S])
        gate_b = at("gate_b", BIG, [P, DC, S])
        cq = at("cq", OB, [P, BLK, S])
        ckv = at("ckv", OB + 4 * KB, [P, BLK, S])
        cq_hi = at("cq_hi", BIG + 32 * KB, [P, BLK, S], F32R)
        cq_lo = at("cq_lo", BIG + 36 * KB, [P, BLK, S], F32R)
        ckv_hi = at("ckv_hi", BIG + 40 * KB, [P, BLK, S], F32R)
        ckv_lo = at("ckv_lo", BIG + 44 * KB, [P, BLK, S], F32R)
        mla_q = at("mla_q", HB, [P, HALF_H, S])
        mla_k = at("mla_k", HB + 8 * KB, [P, HALF_H, S])
        mla_qr = at("mla_qr", HB + 16 * KB, [P, BLK, S])
        mla_v = at("mla_v", HB + 20 * KB, [P, TT, HALF_H * P])
        probs = [at("probs0", HB + 28 * KB, [P, 2 * S]), at("probs1", HB + 30 * KB, [P, 2 * S])]
        probs_2 = at("probs_2", HB, [P, 2 * S])
        mla_tmp = at("mla_tmp", BIG + 32 * KB, [P, BLK * S])
        nscratch_o = at("nscratch_o", OB + 8 * KB, [P, 2, 2 * S])
        ntmp_o = at("ntmp_o", OB + 12 * KB, [P, 2, S])
        sq_o, sq_h = at("sq_o", OB + 16 * KB, [P, DC, S]), at("sq_h", HB, [P, DC, S])
        part_o, part_h = at("part_o", OB + 8 * KB, [P, 3, S]), at("part_h", HB + 16 * KB, [P, 3, S])
        o_tmp = at("o_tmp", OB, [P, 2, BLK * S])
        h_tmp = at("h_tmp", HB, [P, BLK * S])
        sw_hi = at("sw_hi", BIG, [P, 24, S], F32R)
        sw_lo = at("sw_lo", BIG + 24 * KB, [P, 24, S], F32R)
        u_t = at("u_t", BIG, [P, 12, S])
        pool_hi = at("pool_hi", BIG + 12 * KB, [P, 12, S], F32R)
        pool_lo = at("pool_lo", BIG + 24 * KB, [P, 12, S], F32R)
        silu_z = at("silu_z", BIG + 36 * KB, [P, 12, S])
        run_a = at("run_a", OB, [P, 12, S])
        run_b = at("run_b", OB + 12 * KB, [P, 12, S])
        mem_q = at("mem_q", BIG, [P, MEM_H, S])
        mem_z = at("mem_z", BIG + 4 * KB, [P, MEM_H, S])
        pool_tmp = at("pool_tmp", BIG + 8 * KB, [P, 3 * S])
        mem_k = at("mem_k", HB + 8 * KB, [P, MEM_H, S])
        mem_v = at("mem_v", HB + 12 * KB, [P, TT, NT])
        kc = at("kc", BIG, [P, NSA_G, S])
        vc = at("vc", BIG + 4 * KB, [P, NSA_G, S])
        ks = at("ks", BIG + 8 * KB, [P, NSA_G, S])
        vs = at("vs", BIG + 12 * KB, [P, TT, NT])
        kw = at("kw", BIG + 16 * KB, [P, NSA_G, S])
        vw = at("vw", BIG + 20 * KB, [P, TT, NT])
        nsa_q = at("nsa_q", BIG + 24 * KB, [P, NSA_H, S])
        z_pe = at("z_pe", OB, [P, CMP_LEN, NSA_G * NCMP])
        z_hi = [at(f"z_hi{i}", BIG + (24, 40)[i] * KB, [P, CMP_LEN, NSA_G * NCMP], F32R) for i in range(2)]
        z_lo = [at("z_lo0", BIG + 32 * KB, [P, CMP_LEN, NSA_G * NCMP], F32R),
                at("z_lo1", OB + 16 * KB, [P, CMP_LEN, NSA_G * NCMP], F32R)]
        hidden = at("hidden", OB + 8 * KB, [P, 4, NSA_G * NCMP])
        hid_rows = at("hid_rows", OB + 24 * KB, [NSA_G * NCMP, 2, CMP_HID])
        gate_rows = at("gate_rows", OB + 26 * KB, [3 * NSA_H, S])
        k_cmp = at("k_cmp", OB + 16 * KB + 13 * KB, [P, NSA_G * NCMP])
        v_cmp = at("v_cmp", OB + 16 * KB + 14 * KB, [NCMP, NSA_G * HD])
        out_rows = at("out_rows", BIG, [P, TT, D])
        small = [SMALL]

        def keep(name, shape, dt=F32):
            off = small[0]
            small[0] += (4 * int(np.prod(shape[1:])) + 31) // 32 * 32
            assert base + small[0] <= nc.sbuf_usable_end, small[0]
            return at(name, off, shape, dt)

        const = keep("const", [P, CONST_W])
        cols = keep("cols", [P, VEC_W])
        mod = keep("mod", [P, 6 * DC])
        gain_eff = keep("gain_eff", [P, 2, DC])
        c_act = keep("c_act", [P, DC])
        rope_cos = keep("rope_cos", [P, S])
        rope_sin = keep("rope_sin", [P, S])
        mla_probs_2 = at("mla_probs_2", small[0], [P, 2 * S])
        rstd = keep("rstd", [P, S])
        var = keep("var", [P, S])
        probs_t = keep("probs_t", [P, 2, 2 * TT * P])
        angles = at("angles", small[0] - 4 * KB, [P, 3, S])
        stats = keep("stats", [P, 20])
        ada_acc = [probs_t[:, i, :] for i in range(2)]
        gates = keep("gates", [P, TT, 3 * NSA_H])
        k_rope = keep("k_rope", [P, S])
        assert small[0] <= (nc.sbuf_usable_end - base), small

        tile_ps = [ctx.enter_context(nc.psum_tensor(f"tile_ps{i}", [P, 1024], F32)) for i in range(2)]
        misc_ps = [ctx.enter_context(nc.psum_tensor(f"misc_ps{i}", [P, 1024], F32)) for i in range(2)]
        bank = [misc_ps[i // 2][:, (i % 2) * 512:(i % 2 + 1) * 512] for i in range(4)]

        def cst(name):
            a, w = CONST[name]
            return const[:, a:a + w]

        def vec(name, i=0, n=1):
            a, _ = VECTORS[name]
            return cols[:, a + i:a + i + n]

        ident, ones = cst("ident"), cst("ones")
        half_pi = stats[:, 16:17]

        b_scr, o_scr = (nscratch_b, ntmp_b), (nscratch_o, ntmp_o)
        H_OUT = (h_hi, h_lo)
        SCRATCH, SOURCE, DEST, GAIN = {}, {}, {}, {}
        SHIFT = {"mix": mod[:, 0:DC], "ffn": mod[:, 3 * DC:4 * DC]}
        RSTD = {"mix": rstd_mix}
        SQUARES = {"ffn": (sq_o, part_o), "final1": (sq_o, part_o), "kv": (sq_h, part_h), "final2": (sq_h, part_h)}
        for name_, scr, src_, dst_, gain_ in (
                ("mem0", b_scr, mem_t[:], H_OUT, vec("mem_norm_g_2", 0, DC)),
                ("mem1", b_scr, mem_t[:], (mem_hi, mem_lo), vec("mem_norm_g_2", DC, DC)),
                ("mix", b_scr, x[:], H_OUT, gain_eff[:, 0, :]),
                ("cq", o_scr, cq[:], (cq_hi, cq_lo), vec("mla_q_norm_g", 0, 4)),
                ("ckv", o_scr, ckv[:], (ckv_hi, ckv_lo), vec("mla_kv_norm_g", 0, 4)),
                ("ffn", o_scr, x[:], H_OUT, gain_eff[:, 1, :]),
                ("final1", o_scr, x[:], (x,), vec("final_norm_g", 0, DC)),
                ("pool", o_scr, x[:], H_OUT, vec("norm_g_2", 0, DC)),
                ("kv", o_scr, x[:], H_OUT, vec("kv_norm_g_2", 0, DC)),
                ("nsa", o_scr, x[:], H_OUT, vec("norm_g_2", DC, DC)),
                ("final2", o_scr, x[:], (x,), vec("final_g_2", 0, DC))):
            SCRATCH[name_], DEST[name_], GAIN[name_] = scr, dst_, gain_
            SOURCE[name_] = lambda c, t=src_: t[:, c, :]
        mem_store = [nc.dram_tensor(f"mem_store{i}", (P, 2, 1024), F32, kind="Internal").ap() for i in range(2)]

        def probs_of(name, k):
            return (probs + [mla_probs_2 if name.startswith("mla") else probs_2])[k % 3]

        landed = [sem(f"landed{i}") for i in range(4)]
        cut_hi = sem("cut_hi")
        cut_lo = sem("cut_lo")
        piece_done = sem("piece_done")
        taken = [sem(f"taken{i}") for i in range(2)]
        silu_ready = sem("silu_ready")
        ada_step = sem("ada_step")
        ada_done = sem("ada_done")
        ada_sum = sem("ada_sum")
        mod_ready = sem("mod_ready")
        tile_step = sem("tile_step")
        act_step, dve_step = sem("act_step"), sem("dve_step")
        ld_const, ld_vec, ld_x, ld_mem = sem("ld_const"), sem("ld_vec"), sem("ld_x"), sem("ld_mem")
        ld_pos, ld_gla, ld_gk = sem("ld_pos"), sem("ld_gla"), sem("ld_gk")
        ld_mkv, st_mkv, st_out = sem("ld_mkv"), sem("st_mkv"), sem("st_out")
        vec_turned, vec_ready, c_ready = sem("vec_turned"), sem("vec_ready"), sem("c_ready")
        turned = sem("turned")
        turn_out = [sem(f"turn_out{i}") for i in range(2)]
        nm_sq, nm_acc, nm_var, nm_std = sem("nm_sq"), sem("nm_acc"), sem("nm_var"), sem("nm_std")
        nm_part = sem("nm_part")
        nm_t, nm_hi, nm_lo, nm_plain = sem("nm_t"), sem("nm_hi"), sem("nm_lo"), sem("nm_plain")
        tab_arg, tab_ready = sem("tab_arg"), sem("tab_ready")
        rp_rot, rp_done = sem("rp_rot"), sem("rp_done")
        gk_ones = sem("gk_ones")
        z_ready, z_abs, la_ready = sem("z_ready"), sem("z_abs"), sem("la_ready")
        gl_e, gl_ex, gl_qk, gl_att = sem("gl_e"), sem("gl_ex"), sem("gl_qk"), sem("gl_att")
        gl_red, gl_o, gl_out = sem("gl_red"), sem("gl_o"), sem("gl_out")
        at_s, at_masked, at_max, at_exp = sem("at_s"), sem("at_masked"), sem("at_max"), sem("at_exp")
        at_p, at_t, at_pt, at_o, at_fin = (sem(f"at_{n}") for n in ("p", "t", "pt", "o", "fin"))
        pl_t, pl_hi, pl_lo = sem("pl_t"), sem("pl_hi"), sem("pl_lo")
        zp_sum, zp_hi, zp_ready = sem("zp_sum"), sem("zp_hi"), sem("zp_ready")
        hid_turned, hid_ready = sem("hid_turned"), sem("hid_ready")
        gates_turned, gates_ready = sem("gates_turned"), sem("gates_ready")

        def rows(w, chunks=None):
            return w.rearrange("(c p) n -> p c n", p=P)

        w_in = rows(A["w_in"][0])
        ada_w, w_out = rows(A["ada_w"][0]), rows(A["w_out"][0])
        gla_wo, mla_wo = rows(A["gla_wo"][0]), rows(A["mla_wo"][0])
        wuq = A["mla_wuq"][0].rearrange("(c p) (h e) -> p c h e", p=P, e=NOPE + ROPE)
        wukv = A["mla_wukv"][0].rearrange("(c p) (h e) -> p c h e", p=P, e=2 * P)
        ffn_in, ffn_down = rows(A["ffn_w_in"][0]), rows(A["ffn_w_down"][0])
        mem_kv = [rows(A["w_mem_kv_2"][i]) for i in range(2)]
        out_2 = [rows(A["w_out_2"][i]) for i in range(2)]
        a_in, b_in, w_kv = rows(A["a_w_in_2"][0]), rows(A["b_w_in_2"][0]), rows(A["w_kv_2"])

        def plain(w, col):
            return lambda i, tb, g, q: (w[:, g.kc * q:g.kc * (q + 1), bass.ds(i * (g.body * NT) + col + tb * NT, NT)]
                                        if g.turns > 1 else w[:, g.kc * q:g.kc * (q + 1), col + tb * NT:col + tb * NT + NT])

        def ffn_cols(part):
            first = sum(FFN_PARTS[:part]) * NT
            return lambda i, tb, g, q: ffn_in[:, 4 * q:4 * q + 4,
                                              bass.ds(i * (g.body // 2 * NT) + first + tb // 2 * NT + tb % 2 * FFN, NT)]

        def ffn_rows(part):
            c0 = sum(FFN_PARTS[:part]) * BLK

            def src(i, tb, g, q):
                cs = slice(c0 + 4 * q, c0 + 4 * q + 4)
                if g.turns > 1:
                    return ffn_down[:, cs, bass.ds(i * (g.body * NT) + tb * NT, NT)]
                return ffn_down[:, cs, tb * NT:tb * NT + NT]
            return src

        SRC = {"mem_k0": plain(mem_kv[0], 0), "mem_v0": plain(mem_kv[0], NT),
               "mem_k1": plain(mem_kv[1], 0), "mem_v1": plain(mem_kv[1], NT),
               "gla_q": plain(w_in, W_Q), "gla_k": plain(w_in, W_K),
               "gla_v": plain(w_in, W_V), "gla_g": plain(w_in, W_G), "gate_a": plain(w_in, W_GA),
               "gla_gk": lambda i, tb, g, q: w_in[:, :, W_GK:W_GK + P],
               "gla_wo": plain(gla_wo, 0), "mla_cq": plain(w_in, W_CQ), "mla_ckv": plain(w_in, W_CKV),
               "mla_kr": lambda i, tb, g, q: w_in[:, :, W_KR:W_KR + ROPE],
               "gate_b": plain(w_in, W_GB), "mla_wo": plain(mla_wo, 0), "w_out": plain(w_out, 0),
               "pool_u": plain(a_in, 0), "pool_zu": plain(a_in, POOL_W), "pool_qm": plain(a_in, 2 * POOL_W),
               "pool_zm": plain(a_in, 2 * POOL_W + MEM_H * HD),
               "pool_w": lambda i, tb, g, q: rows(A["a_w_pool_2"][0, tb]),
               "pool_out": plain(out_2[0], 0), "nsa_out": plain(out_2[1], 0),
               "cmp_k1": lambda i, tb, g, q: rows(A["cmp_w1_2"][0])[:, 8 * q:8 * q + 8],
               "cmp_v1": lambda i, tb, g, q: rows(A["cmp_w1_2"][1])[:, 8 * q:8 * q + 8],
               "cmp_k2": lambda i, tb, g, q: rows(A["cmp_w2_2"][0]),
               "cmp_v2": lambda i, tb, g, q: rows(A["cmp_w2_2"][1]),
               "nsa_q": plain(b_in, B_Q), "nsa_zq": plain(b_in, B_ZQ), "nsa_qm": plain(b_in, B_QM),
               "nsa_zm": plain(b_in, B_ZM), "nsa_gl": lambda i, tb, g, q: b_in[:, :, B_GL:B_GL + P]}
        for n_, name in enumerate(("nsa_kc", "nsa_vc", "nsa_ks", "nsa_vs", "nsa_kw", "nsa_vw")):
            SRC[name] = plain(w_kv, n_ * NT)
        for hf in range(2):
            h0 = hf * HALF_H
            SRC[f"mla_qn{hf}"] = lambda i, tb, g, q, h0=h0: wuq[:, :, h0 + 4 * tb:h0 + 4 * tb + 4, 0:NOPE]
            SRC[f"mla_qr{hf}"] = lambda i, tb, g, q, h0=h0: wuq[:, :, h0:h0 + 8, NOPE:NOPE + ROPE]
            SRC[f"mla_k{hf}"] = lambda i, tb, g, q, h0=h0: wukv[:, :, h0 + 4 * tb:h0 + 4 * tb + 4, 0:P]
            SRC[f"mla_v{hf}"] = lambda i, tb, g, q, h0=h0: wukv[:, :, h0 + 4 * tb:h0 + 4 * tb + 4, P:2 * P]
            SRC[f"ffn_in{hf}"] = ffn_cols(hf)
            SRC[f"ffn_down{hf}"] = ffn_rows(hf)

        def turns(eng, g, peel_last=False, peel_first=False, flat=False):
            n = g.turns - 1 if peel_last else g.turns
            if g.turns == 1 or flat:
                for i in range(g.turns):
                    yield i, i == g.turns - 1
                return
            if peel_first:
                yield 0, False
            with eng.Fori(int(peel_first), n) as i:
                yield i, not peel_last
            if peel_last:
                yield g.turns - 1, True

        def do_next(steps):
            for do in steps:
                if do:
                    do()
                return

        def per(i, n):
            return 0 if isinstance(i, int) and i == 0 else i * n

        def all_taken(eng, g):
            for b in range(2):
                n = (g.t1 - b + 1) // 2
                if n:
                    eng.wait_ge(taken[b], n)

        def tile_is_done(eng, g, i, tb):
            eng.wait_ge(piece_done, g.p0 + (tb + 1) * g.kp + per(i, g.body * g.kp))

        def last_taken(eng, g, i, tb):
            t = g.t0 + tb - 1
            eng.wait_ge(taken[t % 2], t // 2 + 1 + per(i, g.body // 2))

        def ring(g, tb, q):
            return g.r0 + tb * g.slots + q + (q // g.rider if g.rider and g.mode != "A" else 0)

        def ada_buffer(g, a):
            return a % 2 if g.rider == 1 else 0

        def has_ada(g, q):
            return g.rider and (q + 1) % g.rider == 0

        def ada_place(g, tb, q):
            return (g.a0 + tb // g.rider, tb % g.rider * g.kp // g.rider + q // g.rider,
                    ring(g, tb, q) + (g.mode != "A"))

        def psum_tile(g, tb):
            return tile_ps[(g.t0 + tb) % 2], taken[(g.t0 + tb) % 2]

        def pair_unit(h, tt, nk, scores, v, apart=1, **rest):
            unit = dict(nk=nk, scale=HD ** -0.5, add=None, mul=None, gate=None, z=None, first=True, last=True,
                        q=slice(tt * P, tt * P + P), apart=apart,
                        scores=[scores(h + e * apart) for e in range(2)], v=[v(h + e * apart) for e in range(2)])
            unit.update(rest)
            return unit

        def mla_units(hf):
            def unit(h, tt):
                q, nk = slice(tt * P, tt * P + P), (tt + 1) * P

                def scores(h):
                    r = slice(64 * (h % 2), 64 * (h % 2) + 64)
                    return [(mla_q[:, h, q], mla_k[:, h, 0:nk]), (mla_qr[r, h // 2, q], k_rope[r, 0:nk])]
                return pair_unit(h, tt, nk, scores, lambda h: [mla_v[:, j, h * P:(h + 1) * P] for j in range(tt + 1)],
                                 scale=(NOPE + ROPE) ** -0.5, add=cst("causal")[:, 2 * P - nk:2 * P],
                                 apart=2, chunk=hf * HALF_H + h)
            return [unit(h, tt) for h in range(HALF_H) if h % 4 < 2 for tt in range(TT)]

        def mem_units():
            def unit(h, tt):
                q = slice(tt * P, tt * P + P)
                return pair_unit(h, tt, S, lambda h: [(mem_q[:, h, q], mem_k[:, h, :])],
                                 lambda h: [mem_v[:, j, h * P:(h + 1) * P] for j in range(TT)],
                                 chunk=12 + h, z=mem_z[:, h:h + 2, q])
            return [unit(h, tt) for h in range(0, MEM_H, 2) for tt in range(TT)]

        def nsa_units():
            units = []
            group = lambda h: h // (NSA_H // NSA_G)
            gv = lambda h: slice(group(h) * HD, (group(h) + 1) * HD)
            for h in range(0, NSA_H, 2):
                for tt in range(TT):
                    q, nk = slice(tt * P, tt * P + P), (tt + 1) * P
                    gate = lambda b: gates[:, tt, 3 * h + b:3 * h + b + 4:3]
                    rest = dict(chunk=h, z=silu_z[:, h:h + 2, q])
                    at_ = slice(tt * NCMP, (tt + 1) * NCMP)
                    units.append(pair_unit(
                        h, tt, NCMP, lambda h: [(nsa_q[:, h, q], k_cmp[:, group(h) * NCMP:(group(h) + 1) * NCMP])],
                        lambda h: [v_cmp[:, gv(h)]], add=cst("cmp_add")[:, at_], mul=cst("cmp_mul")[:, at_],
                        gate=gate(0), last=False, **rest))
                    for b, (k, v) in enumerate(((ks, vs), (kw, vw))):
                        units.append(pair_unit(
                            h, tt, nk, lambda h: [(nsa_q[:, h, q], k[:, group(h), 0:nk])],
                            lambda h: [v[:, j, gv(h)] for j in range(tt + 1)],
                            add=cst("causal")[:, 2 * P - nk:2 * P], gate=gate(1 + b), first=False, last=b == 1, **rest))
            return units

        UNITS = {"mla0": mla_units(0), "mla1": mla_units(1), "mem_a": mem_units(), "nsa": nsa_units(),
                 "mem_b": mem_units()}
        U0, FIN0 = {}, {}
        n_u = n_f = 0
        for name, us in UNITS.items():
            U0[name], FIN0[name] = n_u, n_f
            n_u += len(us)
            n_f += sum(u["last"] for u in us)
            UNITS[name] = us

        block = ctx.enter_context(nc.Block())

        @block.sync
        def _(sp):
            x_in, mem_in = A["x"][0], A["mem_2"][0]
            sp.dma_start(const[:], A["const"]).then_inc(ld_const, 16)
            n_vec = 0
            for name, (at0, w) in VECTORS.items():
                v = A[name]
                v = v.rearrange(" ".join(f"a{k}" for k in range(len(v.shape))) + " -> (" +
                                " ".join(f"a{k}" for k in range(len(v.shape))) + ")") if len(v.shape) > 1 else v
                v = v.rearrange("(r p) -> r p", p=P)
                done = 0
                while done < w:
                    r, t = (at0 + done) % P, (at0 + done) // P
                    n = min(P - r, w - done)
                    sp.dma_start(vec_rows[r:r + n, t, :], v[done:done + n]).then_inc(ld_vec, 16)
                    n_vec += 1
                    done += n
            assert n_vec == N_VEC_DMA
            sp.dma_start(mem_rows[:], mem_in.rearrange("(t p) d -> p t d", p=P)).then_inc(ld_mem, 16)
            sp.dma_start(x_rows[:], x_in.rearrange("(t p) d -> p t d", p=P)).then_inc(ld_x, 16)

            def free_slot(g, i, r):
                for kind, s_, n in (("split", cut_lo, g.body * g.kp * g.split),
                                    ("plain", piece_done, g.body * g.kp), ("ada", ada_done, 4 * g.ada_tiles(g.body))):
                    r1 = r + g.body * g.slots
                    now = r >= 4 and KIND[r - 4] == kind
                    later = g.turns > 1 and KIND[r1 - 4] == kind
                    if later:
                        sp.wait_ge(s_, max(BEFORE[kind][r - 3] * now, BEFORE[kind][r1 - 3] - n) + per(i, n))
                    elif now:
                        sp.wait_ge(s_, BEFORE[kind][r - 3])

            def load_ada(g, i, tb, q):
                a, e, r = ada_place(g, tb, q)
                col = bass.ds(per(i, g.ada_tiles(g.body) * NT) + a * NT, NT)
                sp.dma_start(w_raw[r % 4][:].rearrange("p (c n) -> p c n", c=4),
                             ada_w[:, 4 * e:4 * e + 4, col]).then_inc(landed[r % 4], 16)

            def load(name):
                g = G[name]
                for i, _ in turns(sp, g):
                    for tb in range(g.body):
                        for q in range(g.kp):
                            free_slot(g, i, ring(g, tb, q))
                            if g.mode == "A":
                                load_ada(g, i, tb, q)
                                continue
                            slot = ring(g, tb, q) % 4
                            src = SRC[name](i, tb, g, q)
                            dst = w_raw[slot][:, 0:g.kc * g.width].rearrange("p (c n) -> p c n", c=g.kc)
                            parts = [(dst, src)]
                            if len(src.shape) == 4:
                                dst = dst.rearrange("p c (h e) -> p c h e", h=src.shape[2])
                                parts = [(dst[:, c], src[:, c]) for c in range(g.kc)]
                            elif name == "mla_kr":
                                parts = [(dst[:, :, k * ROPE:(k + 1) * ROPE], src) for k in range(2)]
                            assert len(parts) == g.dmas
                            for d_, s_ in parts:
                                sp.dma_start(d_, s_).then_inc(landed[slot], 16)
                            if has_ada(g, q):
                                free_slot(g, i, ring(g, tb, q) + 1)
                                load_ada(g, i, tb, q)

            for name in ("ada0", "mem_k0", "mem_v0", "mem_k1", "mem_v1", "ada1"):
                load(name)
            sp.wait_ge(piece_done, G["mem_v1"].p1)
            sp.dma_start(gk_w[0:RANK, :], A["gla_gk_w"][0]).then_inc(ld_gk, 16)
            sp.dma_start(gk_w[RANK:RANK + 1, :], A["gla_gk_b"]).then_inc(ld_gk, 16)
            load("gla_q")
            load("gla_gk")
            load("gla_k")
            sp.dma_start(gla_const[:].rearrange("p a b c -> p (a b c)"), A["gla_const"]).then_inc(ld_gla, 16)
            load("gla_v")
            for name in ("gla_g", "gate_a", "gla_wo", "mla_cq", "mla_ckv", "mla_kr", "gate_b"):
                load(name)
            for hf in range(2):
                for name in ("mla_qn", "mla_qr", "mla_k", "mla_v"):
                    load(f"{name}{hf}")
            for name in ("mla_wo", "w_out", "ffn_in0", "ffn_down0", "ffn_in1", "ffn_down1",
                         "pool_u", "pool_zu", "pool_qm", "pool_zm"):
                load(name)
            load("pool_w")
            for name in ("pool_out", "nsa_kc", "nsa_vc", "nsa_ks", "nsa_vs", "nsa_kw", "nsa_vw",
                         "cmp_k1", "cmp_v1", "cmp_k2", "cmp_v2", "nsa_q", "nsa_gl", "nsa_zq", "nsa_qm", "nsa_zm"):
                load(name)
            load("nsa_out")
            for k in range(4):
                sp.wait_ge(turn_out[k % 2], TURNS_BEFORE_OUT + k // 2 + 1)
                cs = slice(k // 2 * (D // 2), (k // 2 + 1) * (D // 2))
                sp.dma_start(out[0, k % 2 * P:(k % 2 + 1) * P, cs], out_rows[:, k % 2, cs]).then_inc(st_out, 16)
            sp.wait_ge(st_out, 64)
            sp.wait_ge(st_mkv, 64)

        @block.gpsimd
        def _(pool):
            def mem_kv_load(i, after):
                pool.wait_ge(piece_done, G[after].p1)
                if i == 0:
                    pool.wait_ge(st_mkv, 64)
                pool.dma_start(mem_k[:].rearrange("p h n -> p (h n)"), mem_store[i][:, 0]).then_inc(ld_mkv, 16)
                pool.dma_start(mem_v[:].rearrange("p t n -> p (t n)"), mem_store[i][:, 1]).then_inc(ld_mkv, 16)

            def positions(name):
                pool.dma_start(angles[:, 2, :].bitcast(I32), A[name].broadcast_to([P, S])).then_inc(ld_pos, 16)

            positions("positions")
            all_taken(pool, G["mem_v1"])
            for i in range(2):
                pool.dma_start(mem_store[i][:, 0], mem_k_out[:, i].rearrange("p h n -> p (h n)")).then_inc(st_mkv, 16)
                pool.dma_start(mem_store[i][:, 1], mem_v_out[:, i].rearrange("p t n -> p (t n)")).then_inc(st_mkv, 16)
            mem_kv_load(0, "pool_zm")
            pool.wait_ge(at_o, U0["mem_a"] + len(UNITS["mem_a"]))
            positions("positions_2")
            mem_kv_load(1, "nsa_zm")

        @block.tensor
        def _(pe):
            def mm(o, l, r, start, stop):
                return nc.tensor.matmul(o, l, r, start=start, stop=stop, skip_group_check=True)

            def product(name, x_hi, x_lo=None, ready=(), chunk_ready=None, between=()):
                g, between = G[name], iter(between)
                for s_, v_ in ready:
                    pe.wait_ge(s_, v_)
                for i, _ in turns(pe, g):
                    for tb in range(g.body):
                        ps, tk = psum_tile(g, tb)
                        use = (g.t0 + tb) // 2
                        if use:
                            pe.wait_ge(tk, use + per(i, g.body // 2))
                        for q in range(g.kp):
                            p = g.p0 + tb * g.kp + q
                            if g.split:
                                s_ = g.s0 + tb * g.kp + q
                                pe.wait_ge(cut_lo, s_ + 1 + per(i, g.body * g.kp))
                                slots = [w_hi[s_ % 2], w_lo[s_ % 2]]
                                passes = [(0, x_hi), (1, x_hi), (0, x_lo)]
                            else:
                                r = ring(g, tb, q)
                                pe.wait_ge(landed[r % 4], LANDED[r] + per(i, 16 * g.body * g.slots // 4))
                                slots, passes = [w_raw[r % 4]], [(0, x_hi)] + ([(0, x_lo)] if x_lo else [])
                            w = [t[:, 0:g.kc * g.width].rearrange("p (c n) -> p c n", c=g.kc) for t in slots]
                            for c in range(g.kc):
                                k = q * g.kc + c
                                begin, end = k == 0, k == g.kp * g.kc - 1
                                if tb == 0 and chunk_ready:
                                    for s_, v_ in chunk_ready(k):
                                        pe.wait_ge(s_, v_)
                                for a, (wi, xx) in enumerate(passes):
                                    first, final = begin and a == 0, end and a == len(passes) - 1
                                    xk = xx(tb, k)
                                    if g.mode == "T":
                                        n = xk.shape[-1]
                                        pad = 1 if n == 1 else S
                                        for b in range((g.width + P - 1) // P):
                                            m = min(P, g.width - b * P)
                                            last = mm(ps[0:m, b * pad:b * pad + n], w[wi][:, c, b * P:b * P + m], xk,
                                                      first and (b * pad) % 512 == 0, final)
                                    elif g.mode == "N":
                                        for tt in range(TT):
                                            last = mm(ps[:, tt * 512:tt * 512 + g.width],
                                                      xk[:, tt * P:(tt + 1) * P], w[wi][:, c, 0:g.width], first, final)
                                    elif g.mode == "R":
                                        last = mm(ps[0:NSA_G * NCMP, 0:g.width], xk, w[wi][:, c, :], first, final)
                                    else:
                                        for gg in range(NSA_G):
                                            last = mm(ps[0:NCMP, gg * HD:(gg + 1) * HD],
                                                      xk[:, gg * NCMP:(gg + 1) * NCMP], w[wi][:, c, :],
                                                      first and gg == 0, final)
                            last.then_inc(piece_done, 1)
                            do_next(between)
                        if g.rider and (tb + 1) % g.rider == 0:
                            ada_total(g, i, tb)

            def ada_total(g, i, tb):
                a, n = g.a0 + tb // g.rider, g.ada_tiles(g.body)
                pe.wait_ge(ada_done, 4 * (a + 1) + per(i, 4 * n))
                for b in range(BLK):
                    last = mm(bank[3][:, bass.ds(per(i, BLK * n) + BLK * a + b, 1)],
                              ada_acc[ada_buffer(g, a)][:, b * P:(b + 1) * P], ones[:, 0:1], True, True)
                last.then_inc(ada_sum, 1)

            def of(t, c0=0):
                return lambda tb, k: t[:, c0 + k, :]

            def norm(name):
                n = N[name]
                if n.sums == "pairs":
                    for j in range(n.n // 2):
                        pe.wait_ge(nm_sq, n.a0 + j + 1)
                        if j == 0 and n.k:
                            pe.wait_ge(nm_var, n.k)
                        for e in range(2):
                            last = mm(bank[0][:, 0:S], ones, SCRATCH[name][0][:, j % 2, e * S:(e + 1) * S],
                                      j == 0 and e == 0, j == n.n // 2 - 1 and e == 1)
                        last.then_inc(nm_acc, 1)
                elif n.sums == "tiles":
                    sq, part = SQUARES[name]
                    pe.wait_ge(nm_var, n.k)
                    for t in range(3):
                        pe.wait_ge(nm_part, n.part0 + t + 1)
                        mm(bank[0][:, 0:S], ones, part[:, t, :], t == 0, False)
                    pe.wait_ge(nm_sq, n.a0 + 4)
                    for c in range(3 * BLK, DC):
                        last = mm(bank[0][:, 0:S], ones, sq[:, c, :], False, c == DC - 1)
                    last.then_inc(nm_acc, 1)

            def rotations(name, rot, chunks, after=None):
                def one(j, t):
                    k = ROPE0[name] + j
                    if j == 0 and after:
                        all_taken(pe, G[after])
                    if k >= 2:
                        pe.wait_ge(rp_done, k - 1)
                    mm(bank[1 + k % 2][:, 0:t.shape[-1]], rot, t, True, True).then_inc(rp_rot, 1)
                return [lambda j=j, t=t: one(j, t) for j, t in enumerate(chunks)]

            def rotate(name, rot, chunks):
                for do in rotations(name, rot, chunks):
                    do()

            def attention(name):
                us, u0, f0 = UNITS[name], U0[name], FIN0[name]
                n, fins = len(us), f0
                for s_ in range(n + 3):
                    if s_ < n:
                        u, nk = us[s_], us[s_]["nk"]
                        if u0 + s_ >= 2:
                            pe.wait_ge(at_masked, u0 + s_ - 1)
                        for hd, pairs in enumerate(u["scores"]):
                            for e, (l, r) in enumerate(pairs):
                                last = mm(bank[s_ % 2][:, hd * nk:(hd + 1) * nk], l, r, hd == 0 and e == 0,
                                          e == len(pairs) - 1)
                        last.then_inc(at_s, 1)
                    if 0 <= s_ - 2 < n:
                        e, u = s_ - 2, us[s_ - 2]
                        pe.wait_ge(at_p, u0 + e + 1)
                        if u0 + e:
                            pe.wait_ge(at_pt, u0 + e)
                        nk, nv = u["nk"], len(u["v"][0])
                        for hd in range(2):
                            for j in range(nv):
                                k = min(P, nk - j * P)
                                a = hd * nv + j
                                last = nc.tensor.transpose(bank[2][0:k, a * P:(a + 1) * P],
                                                           probs_of(name, u0 + e)[:, hd * nk + j * P:hd * nk + j * P + k], ident)
                        last.then_inc(at_t, 1)
                    if 0 <= s_ - 3 < n:
                        e, u = s_ - 3, us[s_ - 3]
                        pe.wait_ge(at_pt, u0 + e + 1)
                        if u["first"] and fins:
                            pe.wait_ge(at_fin, fins)
                        nv = len(u["v"][0])
                        for hd, vs_ in enumerate(u["v"]):
                            for j, v in enumerate(vs_):
                                k = min(P, u["nk"] - j * P)
                                a = hd * nv + j
                                last = mm(bank[3][:, hd * P:(hd + 1) * P], v, probs_t[0:k, (u0 + e) % 2, a * P:(a + 1) * P],
                                          u["first"] and a == 0, u["last"] and j == nv - 1)
                        fins += u["last"]
                        last.then_inc(at_o, 1)

            pe.wait_ge(ld_const, 16)
            pe.wait_ge(ld_vec, 16 * N_VEC_DMA)
            for t in range(3):
                n = min(P, VEC_W - t * P)
                last = nc.tensor.transpose(bank[0][:, t * P:t * P + n], vec_rows[0:n, t, :], ident[0:n, 0:n])
            last.then_inc(vec_turned, 1)
            def to_features(k):
                if k % 4 == 0:
                    pe.wait_ge(ld_x if k else ld_mem, 16)
                src = x_rows if k >= 4 else mem_rows
                if k >= 2:
                    pe.wait_ge(turn_out[k % 2], k // 2)
                for c in range(4):
                    for tt in range(TT):
                        last = nc.tensor.transpose(tile_ps[k % 2][:, c * S + tt * P:c * S + (tt + 1) * P],
                                                   src[:, tt, (k % 4 * 4 + c) * P:(k % 4 * 4 + c + 1) * P], ident)
                last.then_inc(turned, 1)

            for k in range(4):
                to_features(k)
            pe.wait_ge(vec_ready, 1)
            norm("mem0")
            for k in range(4, 8):
                to_features(k)
            for b in range(2):
                pe.wait_ge(turn_out[b], 4)
            ada_total(G["ada0"], 0, 0)
            ada_total(G["ada0"], 0, 1)
            h, h_mem = (of(h_hi), of(h_lo)), (of(mem_hi), of(mem_lo))
            o = (of(o_hi), of(o_lo))
            done = lambda n: [(nm_lo, N[n].c0 + N[n].n)]
            as_normed = lambda n: (lambda k: [(nm_lo, N[n].c0 + k + 1)])
            product("mem_k0", *h, chunk_ready=as_normed("mem0"), between=[lambda: ada_total(G["ada0"], 0, 2)])
            norm("mix")
            product("mem_v0", *h)
            product("mem_k1", *h_mem, chunk_ready=as_normed("mem1"))
            product("mem_v1", *h_mem)
            for tb in range(G["ada1"].tiles):
                ada_total(G["ada1"], 0, tb)
            product("gla_q", *h, chunk_ready=as_normed("mix"))
            product("gla_gk", *h)

            def gate_logits(j):
                tt, half = j // 2, slice(j % 2 * 512, (j % 2 + 1) * 512)
                if j == 0:
                    all_taken(pe, G["gla_gk"])
                    pe.wait_ge(ld_gk, 32)
                if j >= 2:
                    pe.wait_ge(la_ready, j - 1)
                mm(bank[1 + j % 2], gk_t[0:RANK + 1, tt * P:(tt + 1) * P], gk_w[:, half], True, True).then_inc(z_ready, 1)

            product("gla_k", *h, between=[lambda j=j: gate_logits(j) for j in range(4)])
            product("gla_v", *h)

            def decays(e):
                hd, tt, d = e // 4, e // 2 % 2, e % 2
                if e == 0:
                    pe.wait_ge(la_ready, 4)
                    pe.wait_ge(ld_gla, 16)
                if e == 1:
                    pe.wait_ge(mod_ready, 2)
                if e >= 2:
                    pe.wait_ge(gl_ex, e - 1)
                for c in range(2):
                    last = mm(misc_ps[e % 2][:, c * 512:(c + 1) * 512],
                              log_a[:, tt, (2 * hd + d) * P:(2 * hd + d + 1) * P],
                              gla_const[:, tt, 4 * c:4 * c + 4, :], True, True)
                last.then_inc(gl_e, 1)

            def gla_scores(k, d):
                hd, tt = k // 2, k % 2
                pe.wait_ge(gl_qk, 2 * k + d + 1)
                if k and d == 0:
                    pe.wait_ge(gl_red, k)
                for l in range(GLA_SLOTS):
                    if l < LEVELS:
                        kk, qq = k_lev[:, d, l, :], q_lev[:, d, l, :]
                    else:
                        kk, qq = (qk[:, hd, c + d, tt * P:(tt + 1) * P] for c in (2, 0))
                    last = mm(tile_ps[0][:, l * P:(l + 1) * P], kk, qq, l % 4 == 0 and d == 0, d == 1)
                if tt:
                    if hd and d == 0:
                        pe.wait_ge(gl_out, hd)
                    last = mm(tile_ps[1][:, 0:P], k_across[:, d, :], q_lev[:, d, LEVELS, :], d == 0, d == 1)
                last.then_inc(gl_att, 1)

            def gla_output(hd):
                pe.wait_ge(gl_red, 2 * hd + 2)
                for c in range(BLK):
                    v = slice(hd * GLA_DV + c * P, hd * GLA_DV + (c + 1) * P)
                    mm(tile_ps[1][:, c * S:(c + 1) * S], gla_v[:, 0, v], gla_att[:, 0:2, :], c % 2 == 0, False)
                    last = mm(tile_ps[1][:, c * S + P:(c + 1) * S], gla_v[:, 1, v], gla_att[:, 2, :], False, True)
                last.then_inc(gl_o, 1)

            decays(0)
            decays(1)
            for k in range(2 * GLA_H):
                for d in range(2):
                    if 2 * k + 2 + d < 4 * GLA_H:
                        decays(2 * k + 2 + d)
                    gla_scores(k, d)
                if k % 2:
                    gla_output(k // 2)
            for hd in range(GLA_H):
                pe.wait_ge(nm_sq, N["gla"].a0 + hd + 1)
                for c in range(BLK):
                    last = mm(misc_ps[0][:, hd * S:(hd + 1) * S], ones, gla_sq[:, hd, c * S:(c + 1) * S],
                              c == 0 and hd % 2 == 0, c == BLK - 1)
            last.then_inc(nm_acc, 1)
            pe.wait_ge(gl_out, GLA_H)
            product("gla_g", *h)
            product("gate_a", *h)
            for b in range(2):
                pe.wait_ge(taken[b], (G["gla_g"].t1 - b + 1) // 2)
            product("gla_wo", *o)
            product("mla_cq", *h)
            product("mla_ckv", *h)
            norm("cq")
            product("mla_kr", *h)
            norm("ckv")
            product("gate_b", *h)
            all_taken(pe, G["mla_kr"])
            rotate("mla_kr", cst("rot_mla"), [k_rope[:, :]])
            for hf in range(2):
                q_op, kv_op = (of(cq_hi), of(cq_lo)), (of(ckv_hi), of(ckv_lo))
                product(f"mla_qn{hf}", *q_op, ready=done("cq"))
                product(f"mla_qr{hf}", *q_op)
                turn = rotations(f"mla_q{hf}", cst("rot_mla"), [mla_qr[:, c, :] for c in range(BLK)], f"mla_qr{hf}")
                product(f"mla_k{hf}", *kv_op, ready=done("ckv"), between=turn[:2])
                product(f"mla_v{hf}", *kv_op, between=turn[2:])
                all_taken(pe, G[f"mla_v{hf}"])
                pe.wait_ge(rp_done, ROPE0[f"mla_q{hf}"] + BLK)
                attention(f"mla{hf}")
            fin = lambda a: [(at_fin, FIN0[a] + sum(u["last"] for u in UNITS[a]))]
            product("mla_wo", *o, ready=fin("mla1"))
            def as_taken(t0, step=1):
                return lambda k: [(taken[(t0 + k // BLK * step) % 2], (t0 + k // BLK * step) // 2 + 1)] if k % BLK == 0 else []

            product("w_out", *h, chunk_ready=as_taken(G["mla_wo"].t0))
            norm("ffn")
            product("ffn_in0", *h, chunk_ready=as_normed("ffn"))
            product("ffn_down0", of(sw_hi), of(sw_lo), chunk_ready=as_taken(G["ffn_in0"].t0 + 1, 2))
            product("ffn_in1", *h)
            product("ffn_down1", of(sw_hi), of(sw_lo), chunk_ready=as_taken(G["ffn_in1"].t0 + 1, 2))
            norm("final1")
            norm("pool")
            product("pool_u", *h, chunk_ready=as_normed("pool"))
            product("pool_zu", *h)
            product("pool_qm", *h)
            product("pool_zm", *h)
            pe.wait_ge(pl_lo, 1)
            product("pool_w", lambda tb, k: pool_hi[:, 3 * tb + k, :], lambda tb, k: pool_lo[:, 3 * tb + k, :])
            all_taken(pe, G["pool_zm"])
            pe.wait_ge(ld_mkv, 32)
            attention("mem_a")
            all_taken(pe, G["pool_w"])
            product("pool_out", *o, ready=fin("mem_a"))
            norm("kv")
            product("nsa_kc", *h, chunk_ready=as_normed("kv"))
            turn_ks = rotations("nsa_ks", cst("rot_nsa"), [ks[:, c, :] for c in range(NSA_G)], "nsa_ks")
            turn_kw = rotations("nsa_kw", cst("rot_nsa"), [kw[:, c, :] for c in range(NSA_G)], "nsa_kw")
            for name, turn in (("vc", ()), ("ks", ()), ("vs", ()), ("kw", turn_ks), ("vw", turn_kw)):
                product(f"nsa_{name}", *h, between=turn)
            for n_, kv in enumerate("kv"):
                product(f"cmp_{kv}1", of(z_hi[n_]), of(z_lo[n_]), ready=[(zp_ready, n_ + 1)])
            all_taken(pe, G["cmp_v1"])
            n60 = NSA_G * NCMP
            for n_ in range(2):
                for j in range(2):
                    last = nc.tensor.transpose(bank[0][:, (2 * n_ + j) * n60:(2 * n_ + j + 1) * n60],
                                               hid_rows[:, n_, j * P:(j + 1) * P], ident[0:n60, 0:n60])
            last.then_inc(hid_turned, 1)
            product("cmp_k2", of(hidden), ready=[(hid_ready, 1)])
            product("cmp_v2", of(hidden, 2))
            all_taken(pe, G["cmp_k2"])
            rotate("cmp_k", cst("rot_nsa"), [k_cmp[:, :]])
            product("nsa_q", *h, chunk_ready=as_normed("nsa"))
            product("nsa_gl", *h)
            product("nsa_zq", *h, between=rotations("nsa_q", cst("rot_nsa"), [nsa_q[:, c, :] for c in range(NSA_H)],
                                                    "nsa_gl"))
            for tt in range(TT):
                last = nc.tensor.transpose(bank[3][:, tt * 3 * NSA_H:(tt + 1) * 3 * NSA_H],
                                           gate_rows[:, tt * P:(tt + 1) * P], ident[0:3 * NSA_H, 0:3 * NSA_H])
            last.then_inc(gates_turned, 1)
            product("nsa_qm", *h)
            product("nsa_zm", *h)
            all_taken(pe, G["nsa_zm"])
            pe.wait_ge(rp_done, ROPE0["nsa_q"] + NSA_H)
            pe.wait_ge(gates_ready, 1)
            attention("nsa")
            pe.wait_ge(ld_mkv, 64)
            attention("mem_b")
            product("nsa_out", *o, ready=fin("mem_b"))
            norm("final2")
            for k in range(4):
                pe.wait_ge(nm_plain, N["final2"].plain0 + (k // 2 + 1) * DC // 2)
                pe.wait_ge(turn_out[k % 2], TURNS_BEFORE_OUT + k // 2)
                if k == 0:
                    all_taken(pe, G["nsa_out"])
                for c in range(8):
                    last = nc.tensor.transpose(tile_ps[k % 2][:, c * P:(c + 1) * P],
                                               x[:, k // 2 * 8 + c, k % 2 * P:(k % 2 + 1) * P], ident)
                last.then_inc(turned, 1)

        @block.scalar
        def _(act):
            own = Steps(act, act_step)
            f = nc.scalar.activation

            def cut(g, i, s_, p, r):
                act.wait_ge(landed[r % 4], LANDED[r] + per(i, 16 * g.body * g.slots // 4))
                if s_ >= 2:
                    act.wait_ge(piece_done, p - 1 + per(i, g.body * g.kp))
                f(w_hi[s_ % 2][:], w_raw[r % 4][:], ACT.Copy).then_inc(cut_hi, 1)

            def cut_first(g, e):
                cut(g, 0, g.s0 + e, g.p0 + e, ring(g, e // g.kp, e % g.kp))

            def cut_in_norm(name, chunk):
                for product_, (norm_, when) in CUT_IN_NORM.items():
                    for e, c in when.items():
                        if norm_ == name and c == chunk and not (e == 0 and G[product_].first_ahead):
                            cut_first(G[product_], e)

            def product(name, take=None, flat=False, between=()):
                g, between = G[name], iter(between)
                if g.split and not g.precut:
                    cut_first(g, 0)
                for i, last in turns(act, g, peel_last=g.split and not g.ahead, peel_first=g.precut > 1, flat=flat):
                    for tb in range(g.body):
                        if g.split:
                            for q in range(1, g.kp + 1):
                                e = tb * g.kp + q
                                done = isinstance(i, int) and i == 0 and e < g.precut
                                if not done and not (e == g.body * g.kp and last and not g.ahead):
                                    cut(g, i, g.s0 + e, g.p0 + e, ring(g, e // g.kp, e % g.kp))
                                do_next(between)
                        if take:
                            ps, tk = psum_tile(g, tb)
                            tile_is_done(act, g, i, tb)
                            take(i, tb, g, ps, tk)

            def copy_to(dst, func=ACT.Copy, scale=1.0, pre=()):
                def take(i, tb, g, ps, tk):
                    for s_, v_ in pre:
                        if tb == 0:
                            act.wait_ge(s_, v_)
                    d = dst(i, tb, g)
                    n = int(np.prod(d.shape[1:]))
                    src = ps[0:d.shape[0], 0:n]
                    if len(d.shape) == 3:
                        src = src.rearrange("p (a b) -> p a b", a=d.shape[1])
                    elif len(d.shape) == 4:
                        src = src.rearrange("p (a b c) -> p a b c", a=d.shape[1], b=d.shape[2])
                    f(d, src, func, scale=scale).then_inc(tk, 1)
                return take

            def chunks(t):
                return lambda i, tb, g: t[:, bass.ds(per(i, g.body * BLK) + tb * BLK, BLK), :]

            def columns(t):
                return lambda i, tb, g: t[:, :, bass.ds(per(i, g.body * NT) + tb * NT, NT)]

            def norm(name):
                sums(name)
                apply(name)

            def sums(name, meanwhile=()):
                n = N[name]
                src = SOURCE[name]
                if n.sums == "shared":
                    return
                if n.sums == "pairs":
                    sq = SCRATCH[name][0]
                    for j in range(n.n // 2):
                        if j >= 2 or n.m0:
                            act.wait_ge(nm_acc, n.m0 + max(j - 1, 0))
                        if name == "pool":
                            act.wait_ge(nm_plain, N["final1"].plain0 + 2 * j + 2)
                        f(sq[:, j % 2, :].rearrange("p (a b) -> p a b", a=2), src(slice(2 * j, 2 * j + 2)),
                          ACT.Square).then_inc(nm_sq, 1)
                for do in meanwhile:
                    do()
                act.wait_ge(nm_var, n.k + 1)
                f(RSTD.get(name, rstd)[:], var[:], ACT.Sqrt).then_inc(nm_std, 1)

            def apply(name):
                n = N[name]
                cut_in_norm(name, -1)
                if n.split:
                    tmp, hi = SCRATCH[name][1], DEST[name][0]
                    shift = SHIFT.get(name)
                    for c in range(n.n):
                        act.wait_ge(nm_t, n.c0 + c + 1)
                        f(hi[:, c, :], tmp[:, c % 2, :], ACT.Identity,
                          bias=shift[:, c:c + 1] if shift is not None else 0.0).then_inc(nm_hi, 1)
                        cut_in_norm(name, c)

            def squares(name):
                n = N[name]
                sq = SQUARES[name][0]

                def take(i, tb, g, ps, tk):
                    t = g.t0 + tb
                    act.wait_ge(taken[t % 2], t // 2 + 1 + per(i, g.body // 2))
                    cs = slice(i * g.body * BLK + tb * BLK, i * g.body * BLK + tb * BLK + BLK)
                    f(sq[:, cs, :], x[:, cs, :], ACT.Square).then_inc(nm_sq, 1)
                return take

            def attention(name):
                us, u0 = UNITS[name], U0[name]
                n = len(us)
                for s_ in range(n + 2):
                    if 0 <= s_ - 2 < n:
                        k, u = u0 + s_ - 2, us[s_ - 2]
                        act.wait_ge(at_t, k + 1)
                        if k >= 2:
                            act.wait_ge(at_o, k - 1)
                        w = 2 * len(u["v"][0]) * P
                        r = min(P, u["nk"])
                        f(probs_t[0:r, k % 2, 0:w], bank[2][0:r, 0:w], ACT.Copy).then_inc(at_pt, 1)
                    if s_ < n:
                        k, nk = u0 + s_, us[s_]["nk"]
                        act.wait_ge(at_max, k + 1)
                        for hd in range(2):
                            p = probs_of(name, k)[:, hd * nk:(hd + 1) * nk]
                            c = 2 * (k % 2) + hd
                            last = f(p, p, ACT.Exp, bias=stats[:, c:c + 1], accum_out=stats[:, 4 + c:5 + c])
                        last.then_inc(at_exp, 1)

            def tables(k):
                act.wait_ge(tab_arg, k + 1)
                f(rope_sin[:], angles[:, 1, :], ACT.Sin).then_inc(tab_ready, 1)
                f(rope_cos[:], angles[:, 0, :], ACT.Sin, scale=-1.0, bias=half_pi).then_inc(tab_ready, 1)

            def leave(k):
                act.wait_ge(turned, k + 1)
                dst = x if k >= 4 else mem_t
                f(dst[:, k % 4 * 4:k % 4 * 4 + 4, :], tile_ps[k % 2][:].rearrange("p (a b) -> p a b", a=4),
                  ACT.Copy).then_inc(turn_out[k % 2], 1)

            act.wait_ge(vec_ready, 1)
            f(c_act[:], vec("c", 0, DC), ACT.Silu).then_inc(c_ready, 1)
            tables(0)
            leave(0)
            leave(2)
            act.wait_ge(turn_out[0], 2)
            act.wait_ge(turn_out[1], 2)
            sums("mem0", [lambda: leave(4), lambda: leave(5), lambda: leave(6), lambda: leave(7)])
            apply("mem0")
            for li in range(2):
                if li:
                    norm("mem1")
                product(f"mem_k{li}", copy_to(lambda i, tb, g, li=li: mem_k_out[:, li]))
                if li == 0:
                    act.wait_ge(turn_out[0], 4)
                    act.wait_ge(turn_out[1], 4)
                    sums("mix")
                product(f"mem_v{li}", copy_to(lambda i, tb, g, li=li: mem_v_out[:, li]))
            apply("mix")
            stored = [(st_mkv, 64)]
            pair = lambda c0: (lambda i, tb, g: qk[:, bass.ds(per(i, 2 * g.body) + 2 * tb, 2), c0:c0 + 2, :])
            product("gla_q", copy_to(pair(0), scale=GLA_DK ** -0.5))
            product("gla_gk", copy_to(lambda i, tb, g: gk_t[0:RANK, :], pre=[(gk_ones, 1)]))

            def log_sigmoid(j):
                act.wait_ge(z_ready, j + 1)
                la = log_a[:, j // 2, j % 2 * 512:(j % 2 + 1) * 512]
                own.wait(f(la, bank[1 + j % 2], ACT.Abs))
                own.wait(f(la, la, ACT.Exp, scale=-1.0))
                f(la, la, ACT.Ln, bias=1.0).then_inc(z_abs, 1)

            product("gla_k", copy_to(pair(2)), between=[None] + [lambda j=j: log_sigmoid(j) for j in range(4)])
            product("gla_v", copy_to(columns(gla_v), pre=stored))
            for k in range(2 * GLA_H):
                for e in (2 * k, 2 * k + 1):
                    act.wait_ge(gl_e, e + 1)
                    if e >= 2:
                        act.wait_ge(gl_qk, e - 1)
                    if e < 2:
                        act.wait_ge(ld_gk, 32)
                    f(decay[e % 2][:], misc_ps[e % 2][:].rearrange("p (a b) -> p a b", a=GLA_SLOTS),
                      ACT.Exp).then_inc(gl_ex, 1)
                if k % 2 == 0 and k:
                    hd = k // 2 - 1
                    act.wait_ge(gl_o, hd + 1)
                    f(qk[:, hd], tile_ps[1][:].rearrange("p (a b) -> p a b", a=4), ACT.Copy).then_inc(gl_out, 1)
            act.wait_ge(gl_o, GLA_H)
            f(qk[:, GLA_H - 1], tile_ps[1][:].rearrange("p (a b) -> p a b", a=4), ACT.Copy).then_inc(gl_out, 1)
            act.wait_ge(gl_out, GLA_H)
            for hd in range(GLA_H):
                f(gla_sq[:, hd, :], qk[:, hd].rearrange("p a b -> p (a b)"), ACT.Square).then_inc(nm_sq, 1)
            cut_in_norm("gla", -1)
            act.wait_ge(nm_var, N["gla"].k + 1)
            f(gla_var[:], gla_var[:], ACT.Sqrt).then_inc(nm_std, 1)

            def silu_g(i, tb, g, ps, tk):
                if tb == 0:
                    act.wait_ge(gl_red, 2 * GLA_H)
                f(gla_tmp[:, tb % 2, :], ps[:], ACT.Silu).then_inc(silu_ready, 1)

            product("gla_g", silu_g, flat=True)
            product("gate_a", copy_to(chunks(merged), ACT.Sigmoid))
            product("gla_wo")
            product("mla_cq", copy_to(lambda i, tb, g: cq[:, :, :], pre=[(piece_done, G["gla_wo"].p1)]))
            product("mla_ckv", copy_to(lambda i, tb, g: ckv[:, :, :]))
            all_taken(act, G["mla_cq"])
            norm("cq")
            product("mla_kr", copy_to(lambda i, tb, g: k_rope[:, :]))
            all_taken(act, G["mla_ckv"])
            norm("ckv")
            product("gate_b", copy_to(chunks(gate_b), ACT.Sigmoid, pre=[(taken[b], (G["gla_g"].t1 - b + 1) // 2) for b in range(2)]), flat=True)
            for hf in range(2):
                free = [(piece_done, G["gate_b"].p1)] if hf == 0 else [(at_o, U0["mla0"] + len(UNITS["mla0"]))]
                product(f"mla_qn{hf}", copy_to(lambda i, tb, g: mla_q[:, 4 * tb:4 * tb + 4, :], pre=free))
                product(f"mla_qr{hf}", copy_to(lambda i, tb, g: mla_qr[:, :, :]))
                product(f"mla_k{hf}", copy_to(lambda i, tb, g: mla_k[:, 4 * tb:4 * tb + 4, :]))
                product(f"mla_v{hf}", copy_to(lambda i, tb, g: mla_v[:, :, tb * NT:(tb + 1) * NT]))
                attention(f"mla{hf}")
            product("mla_wo")
            product("w_out", squares("ffn"), flat=True)
            norm("ffn")

            def silu_gate(part):
                def take(i, tb, g, ps, tk):
                    if tb % 2:
                        return
                    act.wait_ge(taken[(g.t0 + 1) % 2], (g.t0 + 1 + tb) // 2 + per(i, g.body // 2))
                    f(o_tmp[:, 0, :], ps[:], ACT.Silu).then_inc(tk, 1)
                return take

            product("ffn_in0", silu_gate(0))
            product("ffn_down0")
            product("ffn_in1", silu_gate(1))
            product("ffn_down1", squares("final1"), flat=True)
            norm("final1")
            norm("pool")
            product("pool_u", copy_to(chunks(u_t), pre=[(piece_done, G["ffn_down1"].p1)]))
            product("pool_zu", copy_to(chunks(silu_z), ACT.Silu))

            def pool_high():
                act.wait_ge(pl_t, 1)
                f(pool_hi[:], run_b[:], ACT.Copy).then_inc(pl_hi, 1)

            product("pool_qm", copy_to(lambda i, tb, g: mem_q[:, :, :], pre=[(pl_lo, 1)]), between=[pool_high])
            product("pool_zm", copy_to(lambda i, tb, g: mem_z[:, :, :], ACT.Silu))
            product("pool_w")
            attention("mem_a")
            tables(1)
            product("pool_out", squares("kv"), flat=True)
            norm("kv")
            product("nsa_kc", copy_to(lambda i, tb, g: kc[:, :, :], pre=[(at_fin, FIN0["nsa"])]))
            product("nsa_vc", copy_to(lambda i, tb, g: vc[:, :, :]))
            def z_high(n_):
                act.wait_ge(zp_sum, n_ + 1)
                f(z_hi[n_][:], z_pe[:], ACT.Copy).then_inc(zp_hi, 1)

            product("nsa_ks", copy_to(lambda i, tb, g: ks[:, :, :]), between=[None, None, None, lambda: z_high(0)])
            product("nsa_vs", copy_to(lambda i, tb, g: vs[:, :, :]), between=[None, None, None, lambda: z_high(1)])
            product("nsa_kw", copy_to(lambda i, tb, g: kw[:, :, :]))
            product("nsa_vw", copy_to(lambda i, tb, g: vw[:, :, :]))
            n60 = NSA_G * NCMP
            for n_, kv in enumerate("kv"):
                product(f"cmp_{kv}1", copy_to(lambda i, tb, g: hid_rows[:, n_, :], ACT.Silu))
            act.wait_ge(hid_turned, 1)
            f(hidden[:], bank[0][:, 0:4 * n60].rearrange("p (a b) -> p a b", a=4), ACT.Copy).then_inc(hid_ready, 1)
            product("cmp_k2", copy_to(lambda i, tb, g: k_cmp[:, :]))
            product("cmp_v2", copy_to(lambda i, tb, g: v_cmp[:, :]))
            norm("nsa")
            product("nsa_q", copy_to(chunks(nsa_q)))
            product("nsa_gl", copy_to(lambda i, tb, g: gate_rows[:, :], ACT.Sigmoid))
            product("nsa_zq", copy_to(chunks(silu_z), ACT.Silu))
            product("nsa_qm", copy_to(lambda i, tb, g: mem_q[:, :, :], pre=[(zp_ready, 2)]))
            product("nsa_zm", copy_to(lambda i, tb, g: mem_z[:, :, :], ACT.Silu))
            attention("nsa")
            attention("mem_b")
            product("nsa_out", squares("final2"), flat=True)
            norm("final2")
            for k in range(3):
                act.wait_ge(turned, 8 + k + 1)
                f(out_rows[:, k % 2, k // 2 * (D // 2):(k // 2 + 1) * (D // 2)], tile_ps[k % 2][:],
                  ACT.Copy).then_inc(turn_out[k % 2], 1)

        @block.vector
        def _(dve):
            v = nc.vector
            own = Steps(dve, dve_step)

            def f32(t):
                return t.bitcast(F32)

            def cut(g, i, s_, p, r):
                dve.wait_ge(cut_hi, s_ + 1 + per(i, g.body * g.kp))
                v.tensor_tensor(w_lo[s_ % 2][:], w_raw[r % 4][:], f32(w_hi[s_ % 2][:]),
                                ALU.subtract).then_inc(cut_lo, 1)

            def cut_first(g, e):
                cut(g, 0, g.s0 + e, g.p0 + e, ring(g, e // g.kp, e % g.kp))

            def cut_in_norm(name, chunk):
                for product_, (norm_, when) in CUT_IN_NORM.items():
                    for e, c in when.items():
                        if norm_ == name and c == chunk and e >= 2 and G[product_].rider == 1:
                            ada_piece(G[product_], 0, 0, e - 2)
                        if norm_ == name and c == chunk and not (e == 0 and G[product_].first_ahead):
                            cut_first(G[product_], e)

            def product(name, take=None, flat=False, between=()):
                g, between = G[name], iter(between)
                if g.split and not g.precut:
                    cut_first(g, 0)
                for i, last in turns(dve, g, peel_last=g.split and not g.ahead, peel_first=g.precut > 1, flat=flat):
                    for tb in range(g.body):
                        if g.split:
                            for q in range(1, g.kp + 1):
                                done = g.rider == 1 and isinstance(i, int) and i == 0 and tb * g.kp + q < g.precut - 1
                                if has_ada(g, q - 1) and not done:
                                    ada_piece(g, i, tb, q - 1)
                                e = tb * g.kp + q
                                done = isinstance(i, int) and i == 0 and e < g.precut
                                if not done and not (e == g.body * g.kp and last and not g.ahead):
                                    cut(g, i, g.s0 + e, g.p0 + e, ring(g, e // g.kp, e % g.kp))
                                do_next(between)
                        if take:
                            ps, tk = psum_tile(g, tb)
                            take(i, tb, g, ps, tk)

            def ada_piece(g, i, tb, q):
                a, e, r = ada_place(g, tb, q)
                n = g.ada_tiles(g.body)
                w = w_raw[r % 4][:].rearrange("p (c n) -> p c n", c=4)
                acc = ada_acc[ada_buffer(g, a)]
                dve.wait_ge(landed[r % 4], LANDED[r] + per(i, 16 * g.body * g.slots // 4))
                if e == 0 and a >= 2:
                    dve.wait_ge(ada_sum, a - (g.rider == 1) + per(i, n))
                for c in range(4):
                    k = 4 * e + c
                    if k == 0:
                        ins = v.tensor_scalar(acc, w[:, c, :], c_act[:, 0:1], None, ALU.mult)
                    else:
                        if c == 0:
                            dve.wait_ge(ada_done, 4 * a + e + per(i, 4 * n))
                        else:
                            dve.wait_ge(ada_step, 12 * a + 3 * e + c + per(i, 12 * n))
                        ins = v.scalar_tensor_tensor(acc, w[:, c, :], c_act[:, k:k + 1], acc, ALU.mult, ALU.add)
                    if c < 3:
                        ins.then_inc(ada_step, 1)
                    else:
                        ins.then_inc(ada_done, 1)

            mod_takes = [0]

            def take_mod(a0, a1):
                dve.wait_ge(ada_sum, a1)
                m = slice(BLK * a0, BLK * a1)
                v.tensor_tensor(mod[:, m], bank[3][:, m], vec("ada_b", 0, 6 * DC)[:, m], ALU.add).then_inc(mod_ready, 1)
                mod_takes[0] += 1
                dve.wait_ge(mod_ready, mod_takes[0])

            def gain(name, k, part):
                own.wait(v.scalar_tensor_tensor(gain_eff[:, k, :], mod[:, part * DC:(part + 1) * DC], 1.0,
                                                vec(name, 0, DC), ALU.add, ALU.mult))

            def step(i, tb, g, j, ins):
                ins.then_inc(tile_step, 1)
                k = STEPS[g.name]
                dve.wait_ge(tile_step, STEP0[g.name] + k * tb + j + 1 + per(i, k * g.body))

            def in_chunks(t, n=BLK):
                return t.rearrange("p (a b) -> p a b", a=n)

            def some(t, i, tb, g, n=BLK):
                return t[:, bass.ds(per(i, g.body * n) + tb * n, n), :]

            def split_to(i, tb, g, j, src, hi, lo, tk):
                step(i, tb, g, j, v.tensor_copy(hi, src))
                v.tensor_tensor(lo, src, f32(hi), ALU.subtract).then_inc(tk, 1)

            def norm(name):
                sums(name)
                apply(name)

            def root_mean_square(n, rs, var_, src):
                dve.wait_ge(nm_acc, n.m0 + {"pairs": n.n // 2}.get(n.sums, 1))
                if n.k:
                    dve.wait_ge(nm_std, n.k)
                width = P * (n.n // GLA_H if n.sums == "heads" else n.n)
                v.tensor_scalar(var_, src, 1.0 / width, EPS, ALU.mult, ALU.add).then_inc(nm_var, 1)
                dve.wait_ge(nm_std, n.k + 1)
                own.wait(v.reciprocal(rs, rs))

            def sums(name):
                n = N[name]
                if n.sums != "shared":
                    rs = RSTD.get(name, rstd)[:]
                    root_mean_square(n, rs, var[:], bank[0][:, 0:S])

            def apply(name, between=()):
                n, between = N[name], iter(between)
                src, gain, rs = SOURCE[name], GAIN[name], RSTD.get(name, rstd)[:]
                cut_in_norm(name, -1)
                if not n.split:
                    for c in range(n.n):
                        v.scalar_tensor_tensor(DEST[name][0][:, c, :], src(c), gain[:, c:c + 1], rs,
                                               ALU.mult, ALU.mult).then_inc(nm_plain, 1)
                    return
                tmp, (hi, lo) = SCRATCH[name][1], DEST[name]
                shift = SHIFT.get(name)
                for c in range(n.n + 1):
                    if c < n.n:
                        if n.c0 + c:
                            dve.wait_ge(nm_lo, n.c0 + max(c - 1, 0))
                        v.scalar_tensor_tensor(tmp[:, c % 2, :], src(c), gain[:, c:c + 1], rs,
                                               ALU.mult, ALU.mult).then_inc(nm_t, 1)
                    if c:
                        e = c - 1
                        dve.wait_ge(nm_hi, n.c0 + e + 1)
                        if shift is None:
                            ins = v.tensor_tensor(lo[:, e, :], tmp[:, e % 2, :], f32(hi[:, e, :]), ALU.subtract)
                        else:
                            ins = v.scalar_tensor_tensor(lo[:, e, :], tmp[:, e % 2, :], shift[:, e:e + 1],
                                                         f32(hi[:, e, :]), ALU.add, ALU.subtract)
                        ins.then_inc(nm_lo, 1)
                        cut_in_norm(name, e)
                        if e % 2:
                            do_next(between)

            def rotations(name, chunks, cos=None, sin=None):
                def one(j, t):
                    k = ROPE0[name] + j
                    n = t.shape[-1] if len(t.shape) == 2 else t.shape[1] * t.shape[2]
                    dve.wait_ge(rp_rot, k + 1)
                    src = bank[1 + k % 2][:, 0:n]
                    tmp = var[:, 0:n]
                    if len(t.shape) == 3:
                        src, tmp = (a.rearrange("p (a b) -> p a b", a=t.shape[1]) for a in (src, tmp))
                    own.wait(v.tensor_tensor(tmp, src, sin if sin is not None else rope_sin[:], ALU.mult))
                    own.wait(v.tensor_tensor(t, t, cos if cos is not None else rope_cos[:], ALU.mult))
                    v.tensor_tensor(t, t, tmp, ALU.add).then_inc(rp_done, 1)
                    dve.wait_ge(rp_done, k + 1)
                return [lambda j=j, t=t: one(j, t) for j, t in enumerate(chunks)]

            def rotate(name, chunks, cos=None, sin=None):
                for do in rotations(name, chunks, cos, sin):
                    do()

            def both(t):
                return t.unsqueeze(1).broadcast_to([P, 2, t.shape[-1]])

            def attention(name):
                us, u0, fins = UNITS[name], U0[name], FIN0[name]
                n = len(us)
                for s_ in range(n + 4):
                    if 0 <= s_ - 4 < n and us[s_ - 4]["last"]:
                        u, k = us[s_ - 4], u0 + s_ - 4
                        dve.wait_ge(at_o, k + 1)
                        pair = slice(u["chunk"], u["chunk"] + u["apart"] + 1, u["apart"])
                        hi, lo = o_hi[:, pair, u["q"]], o_lo[:, pair, u["q"]]
                        src = in_chunks(bank[3][:, 0:2 * P], 2)
                        if fins:
                            dve.wait_ge(at_fin, fins)
                        fins += 1
                        if u["z"] is not None:
                            own.wait(v.tensor_tensor(in_chunks(var[:], 2), src, u["z"], ALU.mult))
                            src = in_chunks(var[:], 2)
                        own.wait(v.tensor_copy(hi, src))
                        v.tensor_tensor(lo, src, f32(hi), ALU.subtract).then_inc(at_fin, 1)
                    if s_ < n:
                        u, k = us[s_], u0 + s_
                        w = 2 * u["nk"]
                        p, sc = in_chunks(probs_of(name, k)[:, 0:w], 2), in_chunks(bank[s_ % 2][:, 0:w], 2)
                        dve.wait_ge(at_s, k + 1)
                        if k >= 3:
                            dve.wait_ge(at_t, k - 2)
                        if u["add"] is None:
                            ins = v.tensor_scalar(p, sc, u["scale"], None, ALU.mult)
                        else:
                            ins = v.scalar_tensor_tensor(p, sc, u["scale"], both(u["add"]), ALU.mult, ALU.add)
                        ins.then_inc(at_masked, 1)
                        dve.wait_ge(at_masked, k + 1)
                        c = 2 * (k % 2)
                        v.tensor_reduce(stats[:, c:c + 2], p, AX.X, ALU.max, negate=True).then_inc(at_max, 1)
                    if 0 <= s_ - 1 < n:
                        u, k = us[s_ - 1], u0 + s_ - 1
                        c = 2 * (k % 2)
                        p = in_chunks(probs_of(name, k)[:, 0:2 * u["nk"]], 2)
                        r = stats[:, 8 + c:10 + c]
                        dve.wait_ge(at_exp, k + 1)
                        own.wait(v.reciprocal(r, stats[:, 4 + c:6 + c]))
                        if u["gate"] is not None:
                            rg = stats[:, 12 + c:14 + c]
                            own.wait(v.tensor_tensor(rg, r, u["gate"], ALU.mult))
                            r = rg
                        rr = r.unsqueeze(2).broadcast_to([P, 2, u["nk"]])
                        ins = v.tensor_tensor(p, p, rr, ALU.mult)
                        if u["mul"] is not None:
                            own.wait(ins)
                            ins = v.tensor_tensor(p, p, both(u["mul"]), ALU.mult)
                        ins.then_inc(at_p, 1)

            def tables(k):
                dve.wait_ge(ld_pos, 16 * (k + 1))
                pos, a, t = angles[:, 2, :], angles[:, 1, :], angles[:, 0, :]
                own.wait(v.tensor_copy(a, pos.bitcast(I32)))
                own.wait(v.tensor_scalar(a, a, cst(("freq_mla", "freq_nsa")[k]), None, ALU.mult))
                big = 1.5 * 2.0 ** 23
                own.wait(v.tensor_scalar(t, a, 1.0 / (2 * math.pi), big, ALU.mult, ALU.add))
                own.wait(v.tensor_scalar(t, t, -big, None, ALU.add))
                hi = 6.28125
                mid = float(np.float32(round((2 * math.pi - hi) * 2 ** 20) / 2 ** 20))
                for c in (hi, mid, 2 * math.pi - hi - mid):
                    own.wait(v.scalar_tensor_tensor(a, t, -c, a, ALU.mult, ALU.add))
                pi = 3.1415925
                own.wait(v.tensor_scalar(a, a, pi, -pi, ALU.min, ALU.max))
                v.scalar_tensor_tensor(t, a, -1.0, a, ALU.mult, ALU.max).then_inc(tab_arg, 1)
                dve.wait_ge(tab_ready, 2 * k + 2)

            v.memset(half_pi, math.pi / 2).then_inc(dve_step, 1)
            own.n += 1
            dve.wait_ge(dve_step, 1)
            dve.wait_ge(vec_turned, 1)
            v.tensor_copy(cols[:], bank[0][:, 0:VEC_W]).then_inc(vec_ready, 1)
            def leave(k):
                dve.wait_ge(turned, k + 1)
                dst = x if k >= 4 else mem_t
                v.tensor_copy(dst[:, k % 4 * 4:k % 4 * 4 + 4, :], in_chunks(tile_ps[1][:])).then_inc(turn_out[1], 1)

            dve.wait_ge(ld_const, 16)
            tables(0)
            leave(1)
            leave(3)
            dve.wait_ge(turn_out[0], 2)
            dve.wait_ge(turn_out[1], 2)
            dve.wait_ge(c_ready, 1)
            early = [lambda tb=tb, q=q: ada_piece(G["ada0"], 0, tb, q) for tb in range(3) for q in range(4)]
            for do in early[:4]:
                do()
            sums("mem0")
            apply("mem0", early[4:])
            for li in range(2):
                if li:
                    norm("mem1")
                product(f"mem_k{li}")
                if li == 0:
                    sums("mix")
                product(f"mem_v{li}")
            for tb in range(G["ada1"].tiles):
                for q in range(4):
                    ada_piece(G["ada1"], 0, tb, q)
            take_mod(0, 2 * DC // BLK)
            gain("norm_mix_g", 0, 1)
            apply("mix")
            dve.wait_ge(nm_lo, N["mix"].c0 + DC)
            v.memset(gk_t[0:32, :], 1.0).then_inc(gk_ones, 1)
            product("gla_q")
            product("gla_gk")

            def log_a_out(j):
                dve.wait_ge(z_abs, j + 1)
                la = log_a[:, j // 2, j % 2 * 512:(j % 2 + 1) * 512]
                v.scalar_tensor_tensor(la, bank[1 + j % 2], 0.0, la, ALU.min, ALU.subtract).then_inc(la_ready, 1)

            product("gla_k", between=[None, None] + [lambda j=j: log_a_out(j) for j in range(4)])
            product("gla_v")
            take_mod(2 * DC // BLK, 3 * DC // BLK)

            all_taken(dve, G["gla_v"])
            def with_decays(k, d):
                hd, tt, e = k // 2, k % 2, 2 * k + d
                if k:
                    dve.wait_ge(gl_att, e - 1)
                dve.wait_ge(gl_ex, e + 1)
                ex = decay[e % 2]
                q, kk = (qk[:, hd, c + d, tt * P:(tt + 1) * P].unsqueeze(1) for c in (0, 2))
                v.tensor_tensor(q_lev[:, d], q.broadcast_to([P, GLA_SLOTS, P]), ex[:], ALU.mult)
                if tt == 0:
                    v.tensor_tensor(k_across[:, d, :], kk[:, 0, :], ex[:, LEVELS, :], ALU.mult)
                v.tensor_tensor(k_lev[:, d, 0:LEVELS, :], kk.broadcast_to([P, LEVELS, P]), ex[:, 0:LEVELS, :],
                                ALU.mult).then_inc(gl_qk, 1)

            with_decays(0, 0)
            with_decays(0, 1)
            for k in range(2 * GLA_H):
                hd, tt = k // 2, k % 2
                if k + 1 < 2 * GLA_H:
                    with_decays(k + 1, 0)
                dve.wait_ge(gl_att, 2 * k + 2)
                if tt == 0 and hd:
                    dve.wait_ge(gl_o, hd)
                sc = tile_ps[0][:].rearrange("p (l i) -> p l i", l=GLA_SLOTS)
                own.wait(v.tensor_tensor(sc, sc, gla_const[:, 2], ALU.mult))
                if tt:
                    v.tensor_copy(gla_att[:, 1, :], tile_ps[1][:, 0:P])
                v.tensor_reduce(gla_att[:, 2 * tt, :], tile_ps[0][:].rearrange("p (l i) -> p i l", l=GLA_SLOTS),
                                AX.X, ALU.add).then_inc(gl_red, 1)
                if k + 1 < 2 * GLA_H:
                    with_decays(k + 1, 1)
            dve.wait_ge(gl_out, GLA_H)
            n_gla = N["gla"]
            cut_in_norm("gla", -1)
            root_mean_square(n_gla, gla_var[:], gla_var[:], misc_ps[0][:].rearrange("p (a b) -> p a b", a=GLA_H))
            def gated(i, tb, g, ps, tk):
                hd = i * g.body + tb
                for c in range(BLK):
                    v.scalar_tensor_tensor(qk[:, hd, c, :], qk[:, hd, c, :], vec("gla_onorm_g", c), gla_var[:, hd, :],
                                           ALU.mult, ALU.mult).then_inc(nm_plain, 1)
                dve.wait_ge(nm_plain, n_gla.plain0 + (hd + 1) * BLK)
                dve.wait_ge(silu_ready, g.t0 - G["gla_g"].t0 + tb + 1 + per(i, g.body))
                o4 = qk[:, bass.ds(per(i, g.body) + tb, 1), :, :].rearrange("p a c n -> p (a c n)")
                step(i, tb, g, 0, v.tensor_tensor(o4, o4, gla_tmp[:, tb % 2, :], ALU.mult))
                split_to(i, tb, g, 1, in_chunks(o4), some(o_hi, i, tb, g), some(o_lo, i, tb, g), tk)

            product("gla_g", gated, flat=True)
            product("gate_a")

            def gla_merge(i, tb, g, ps, tk):
                tile_is_done(dve, g, i, tb)
                m = some(merged, i, tb, g)
                v.tensor_tensor(m, m, in_chunks(ps[:]), ALU.mult).then_inc(tk, 1)

            all_taken(dve, G["gate_a"])
            product("gla_wo", gla_merge)
            product("mla_cq")
            product("mla_ckv")
            norm("cq")
            product("mla_kr")
            norm("ckv")
            product("gate_b", flat=True)
            take_mod(3 * DC // BLK, 5 * DC // BLK)
            gain("norm_ffn_g", 1, 4)
            all_taken(dve, G["mla_kr"])
            rotate("mla_kr", [k_rope[:, :]])
            for hf in range(2):
                product(f"mla_qn{hf}")
                product(f"mla_qr{hf}")
                turn = rotations(f"mla_q{hf}", [mla_qr[:, c, :] for c in range(BLK)])
                product(f"mla_k{hf}", between=turn[:2])
                product(f"mla_v{hf}", between=turn[2:])
                attention(f"mla{hf}")

            def both_merge(i, tb, g, ps, tk):
                tile_is_done(dve, g, i, tb)
                last_taken(dve, g, i, tb)
                t = in_chunks(mla_tmp[:])
                step(i, tb, g, 0, v.tensor_tensor(t, in_chunks(ps[:]), some(gate_b, i, tb, g), ALU.mult))
                step(i, tb, g, 1, v.tensor_tensor(t, t, some(merged, i, tb, g), ALU.add))
                split_to(i, tb, g, 2, t, some(h_hi, i, tb, g), some(h_lo, i, tb, g), tk)

            all_taken(dve, G["gate_b"])
            product("mla_wo", both_merge)

            def residual(part=None, squared=None):
                def take(i, tb, g, ps, tk):
                    add(i, tb, g, ps, tk)
                    t = i * g.body + tb if squared else 0
                    if t:
                        dve.wait_ge(nm_sq, N[squared].a0 + t)
                        sq, sums_ = SQUARES[squared]
                        v.tensor_reduce(sums_[:, t - 1, :], sq[:, (t - 1) * BLK:t * BLK, :].rearrange("p c n -> p n c"),
                                        AX.X, ALU.add).then_inc(nm_part, 1)

                def add(i, tb, g, ps, tk):
                    tile_is_done(dve, g, i, tb)
                    xx = some(x, i, tb, g)
                    if part is None:
                        v.tensor_tensor(xx, xx, in_chunks(ps[:]), ALU.add).then_inc(tk, 1)
                        return
                    for c in range(BLK):
                        cc = (i * g.body + tb) * BLK + c
                        ins = v.scalar_tensor_tensor(x[:, cc, :], ps[:, c * S:(c + 1) * S], mod[:, part * DC + cc:part * DC + cc + 1],
                                                     x[:, cc, :], ALU.mult, ALU.add)
                    ins.then_inc(tk, 1)
                return take

            product("w_out", residual(2, "ffn"), flat=True)
            norm("ffn")
            take_mod(5 * DC // BLK, ADA_TILES)

            def up(i, tb, g, ps, tk):
                if tb % 2 == 0:
                    return
                if g.name == "ffn_in1":
                    dve.wait_ge(piece_done, G["ffn_down0"].p1)
                tile_is_done(dve, g, i, tb)
                dve.wait_ge(taken[g.t0 % 2], (g.t0 + tb - 1) // 2 + 1 + per(i, g.body // 2))
                t = o_tmp[:, 0, :]
                n = g.body // 2
                k = STEPS[g.name]
                s0 = STEP0[g.name] + k * (tb // 2)
                v.tensor_tensor(t, ps[:], t, ALU.mult).then_inc(tile_step, 1)
                dve.wait_ge(tile_step, s0 + 1 + per(i, k * n))
                at_ = bass.ds(per(i, n * BLK) + tb // 2 * BLK, BLK)
                hi, lo = sw_hi[:, at_, :], sw_lo[:, at_, :]
                v.tensor_copy(hi, in_chunks(t)).then_inc(tile_step, 1)
                dve.wait_ge(tile_step, s0 + 2 + per(i, k * n))
                v.tensor_tensor(lo, in_chunks(t), f32(hi), ALU.subtract).then_inc(tk, 1)

            for part in range(2):
                product(f"ffn_in{part}", up)
                product(f"ffn_down{part}", residual(5, "final1" if part else None), flat=True)
            norm("final1")
            norm("pool")

            product("pool_u")
            all_taken(dve, G["pool_u"])
            bufs = (run_a, run_b)

            def double(j):
                src, d, sh, c0 = (bufs[(j - 1) % 2] if j else u_t), bufs[j % 2], 2 ** j, 3 * j
                own.wait(v.tensor_copy(d[:, c0:, 0:sh], src[:, c0:, 0:sh]))
                own.wait(v.tensor_tensor(d[:, c0:, sh:], src[:, c0:, sh:], src[:, c0:, 0:S - sh], ALU.add))

            def centre(g_):
                cs = slice(3 * g_, 3 * g_ + 3)
                s_ = bufs[g_ % 2]
                a = CONST["pool_head"][0] + 16 * g_
                head = const[:, a:a + 16].unsqueeze(1).broadcast_to([P, 3, 16])
                own.wait(v.tensor_tensor(s_[:, cs, 0:16], s_[:, cs, 0:16], head, ALU.mult))
                ins = v.scalar_tensor_tensor(run_b[:, cs, :], s_[:, cs, :], 0.5 ** (g_ + 1), u_t[:, cs, :],
                                             ALU.mult, ALU.subtract)
                if g_ == POOL_G - 1:
                    ins.then_inc(pl_t, 1)
                else:
                    own.wait(ins)

            def pool_low():
                dve.wait_ge(pl_hi, 1)
                v.tensor_tensor(pool_lo[:], run_b[:], f32(pool_hi[:]), ALU.subtract).then_inc(pl_lo, 1)

            product("pool_zu", between=[lambda j=j: double(j) for j in range(POOL_G)] +
                    [lambda g_=g_: centre(g_) for g_ in range(POOL_G)])
            product("pool_qm", between=[None, pool_low])
            product("pool_zm")

            def pool_take(i, tb, g, ps, tk):
                tile_is_done(dve, g, i, tb)
                last_taken(dve, g, i, tb)
                t = in_chunks(pool_tmp[:], 3)
                a = VECTORS["a_pool_scale_2"][0] + 3 * tb
                scale = cols[:, a:a + 3].unsqueeze(2).broadcast_to([P, 3, S])
                step(i, tb, g, 0, v.tensor_tensor(t, in_chunks(ps[:, 0:3 * S], 3), scale, ALU.mult))
                step(i, tb, g, 1, v.tensor_tensor(t, t, silu_z[:, 3 * tb:3 * tb + 3, :], ALU.mult))
                split_to(i, tb, g, 2, t, o_hi[:, 3 * tb:3 * tb + 3, :], o_lo[:, 3 * tb:3 * tb + 3, :], tk)

            all_taken(dve, G["pool_zm"])
            dve.wait_ge(pl_lo, 1)
            product("pool_w", pool_take)
            attention("mem_a")
            tables(1)
            product("pool_out", residual(squared="kv"), flat=True)
            norm("kv")
            def z_sum(n_, a):
                if a == 0:
                    if n_:
                        dve.wait_ge(zp_ready, n_)
                    all_taken(dve, G[("nsa_kc", "nsa_vc")[n_]])
                z = (kc, vc)[n_][:].rearrange("p g (n b) -> p b g n", b=CMP_STRIDE)[:, :, :, a:a + NCMP]
                for gg in range(NSA_G):
                    pe_ = vec("cmp_pe_2", n_ * CMP_LEN + 16 * a, 16).unsqueeze(2).broadcast_to([P, 16, NCMP])
                    ins = v.tensor_tensor(z_pe[:, 16 * a:16 * a + 16, gg * NCMP:(gg + 1) * NCMP], z[:, :, gg, :],
                                          pe_, ALU.add)
                if a:
                    ins.then_inc(zp_sum, 1)

            def z_low(n_):
                dve.wait_ge(zp_hi, n_ + 1)
                v.tensor_tensor(z_lo[n_][:], z_pe[:], f32(z_hi[n_][:]), ALU.subtract).then_inc(zp_ready, 1)

            product("nsa_kc")
            product("nsa_vc")
            product("nsa_ks", between=[None, lambda: z_sum(0, 0), lambda: z_sum(0, 1)])
            product("nsa_vs", between=[lambda: z_low(0), lambda: z_sum(1, 0), lambda: z_sum(1, 1)])
            turn_ks = rotations("nsa_ks", [ks[:, c, :] for c in range(NSA_G)])
            turn_kw = rotations("nsa_kw", [kw[:, c, :] for c in range(NSA_G)])
            product("nsa_kw", between=[lambda: z_low(1)] + turn_ks[:3])
            product("nsa_vw", between=turn_ks[3:] + turn_kw[:3])
            product("cmp_k1", between=turn_kw[3:])
            product("cmp_v1")
            product("cmp_k2")
            product("cmp_v2")
            at_end = slice(CMP_LEN - 1, S, CMP_STRIDE)
            all_taken(dve, G["cmp_k2"])
            rotate("cmp_k", [k_cmp[:].rearrange("p (g n) -> p g n", g=NSA_G)],
                   rope_cos[:, at_end].unsqueeze(1).broadcast_to([P, NSA_G, NCMP]),
                   rope_sin[:, at_end].unsqueeze(1).broadcast_to([P, NSA_G, NCMP]))
            dve.wait_ge(piece_done, G["nsa_vw"].p1)
            norm("nsa")
            product("nsa_q")
            product("nsa_gl")
            turn = rotations("nsa_q", [nsa_q[:, c, :] for c in range(NSA_H)])
            product("nsa_zq", between=[None] + turn[:11])
            turn[11]()
            dve.wait_ge(gates_turned, 1)
            v.tensor_copy(gates[:], bank[3][:, 0:TT * 3 * NSA_H].rearrange("p (a b) -> p a b", a=TT)).then_inc(gates_ready, 1)
            product("nsa_qm")
            product("nsa_zm")
            all_taken(dve, G["nsa_zm"])
            attention("nsa")
            attention("mem_b")
            product("nsa_out", residual(squared="final2"), flat=True)
            norm("final2")
            dve.wait_ge(turned, 12)
            v.tensor_copy(out_rows[:, 1, D // 2:], tile_ps[1][:]).then_inc(turn_out[1], 1)


IN_NAMES = ("x", "c", "positions", "ada_w", "ada_b", "norm_mix_g", "w_in", "gla_gk_w", "gla_gk_b", "gla_onorm_g",
            "gla_wo", "mla_q_norm_g", "mla_wuq", "mla_kv_norm_g", "mla_wukv", "mla_wo", "w_out", "norm_ffn_g",
            "ffn_w_in", "ffn_w_down", "final_norm_g", "mem_2", "positions_2", "norm_g_2", "mem_norm_g_2",
            "w_mem_kv_2", "w_out_2", "a_w_in_2", "a_w_pool_2", "a_pool_scale_2", "b_w_in_2", "kv_norm_g_2",
            "w_kv_2", "cmp_pe_2", "cmp_w1_2", "cmp_w2_2", "final_g_2")


def kernel(**inputs):
    import concourse.bacc as bacc
    from concourse.bass_utils import run_bass_kernel_spmd

    nc = bacc.Bacc("TRN2", target_bir_lowering=False, num_devices=1)
    const, gla_const = constants()
    arrays = {"in_const": const, "in_gla_const": gla_const}
    for name in IN_NAMES:
        arrays[f"in_{name}"] = np.ascontiguousarray(inputs[name])
    A = {name[3:]: nc.dram_tensor(name, a.shape, mybir.dt.from_np(a.dtype), kind="ExternalInput").ap()
         for name, a in arrays.items()}
    out = nc.dram_tensor("out", (1, S, D), F32, kind="ExternalOutput").ap()
    program(nc, A, out)
    r = run_bass_kernel_spmd(nc, [arrays], core_ids=[0])
    return r.results[0]["out"]
```
